# Optimizing a Trainium2 kernel written in Bass

```python
import math
import jax, jax.numpy as jnp
from jax import lax
import numpy as np

'''Hybrid bidirectional encoder trunk: DEPTH layers of
  h = h + W_out[ norm_A(GQA-axial-rope) | norm_B(MLA) | norm_C(bidirectional S5 + GLU) ]  (parallel head groups)
  h = h + PEER(rmsnorm(h))                                   (product-key single-neuron experts)
  h = h + sigmoid(rmsnorm(h) @ W_gate) * (p[i] @ W_ple)        (per-layer input embeddings)
followed by a final RMSNorm.
Inputs: x (BATCH, SEQ, D_MODEL) f32, p (DEPTH, BATCH, SEQ, PLE_DIM) f32, stacked per-layer weights.
Output: (BATCH, SEQ, D_MODEL).
'''

D_MODEL = 1024
BATCH = 1
SEQ = 512
DEPTH = 2

PLE_DIM = 256
GRID_W = 64
Q_BLOCK = 128
ROPE_THETA = 10000.0
EPS = 1e-6

HEAD_DIM = 64
GQA_Q_HEADS = 4
GQA_KV_HEADS = 2
MLA_HEADS = 4
MLA_Q_RANK = 256
MLA_KV_RANK = 128
MLA_NOPE_DIM = 64
MLA_ROPE_DIM = 32
MLA_V_DIM = 64
S5_WIDTH = D_MODEL // 2
S5_GROUP_CH = 16
S5_GROUPS = S5_WIDTH // S5_GROUP_CH
S5_STATE = 64

GQA_WIDTH = GQA_Q_HEADS * HEAD_DIM
MLA_WIDTH = MLA_HEADS * MLA_V_DIM
MIX_WIDTH = GQA_WIDTH + MLA_WIDTH + S5_WIDTH

IN_WIDTHS = (GQA_Q_HEADS * HEAD_DIM, GQA_KV_HEADS * HEAD_DIM, GQA_KV_HEADS * HEAD_DIM,
             MLA_Q_RANK, MLA_KV_RANK, MLA_ROPE_DIM, S5_WIDTH)
IN_COLS = sum(IN_WIDTHS)
SPLIT_POINTS = tuple(sum(IN_WIDTHS[:k]) for k in range(1, len(IN_WIDTHS)))

N_KEYS = 128
N_EXPERTS = N_KEYS * N_KEYS
PEER_HEADS = 8
PEER_QUERY_DIM = 256
PEER_HALF = PEER_QUERY_DIM // 2
PEER_TOPK = 16
PEER_CHUNK = 128

kernel_name = 'hybrid_gqa_mla_s5_peer_encoder'

def rmsnorm(x, g):
    xf = x.astype(jnp.float32)
    y = xf * lax.rsqrt(jnp.mean(xf * xf, axis=-1, keepdims=True) + EPS)
    return (y * g.astype(jnp.float32)).astype(x.dtype)

def axial_rope_tables(n_tok, rot_dim):
    rows = n_tok // GRID_W
    r = jnp.broadcast_to(jnp.arange(rows, dtype=jnp.float32)[:, None], (rows, GRID_W)).reshape(-1)
    c = jnp.broadcast_to(jnp.arange(GRID_W, dtype=jnp.float32)[None, :], (rows, GRID_W)).reshape(-1)
    half = rot_dim // 2
    freqs = ROPE_THETA ** (-jnp.arange(0, half, 2, dtype=jnp.float32) / half)
    ang = jnp.concatenate([r[:, None] * freqs, c[:, None] * freqs], axis=-1)
    return jnp.cos(ang), jnp.sin(ang)

def apply_rope(x, cos, sin):
    half = x.shape[-1] // 2
    x1, x2 = x[..., :half], x[..., half:]
    c, s = cos[:, None, :], sin[:, None, :]
    return jnp.concatenate([x1 * c - x2 * s, x1 * s + x2 * c], axis=-1).astype(x.dtype)

def blocked_attention(q, k, v):
    b, n, hq, dk = q.shape
    hkv, dv = k.shape[2], v.shape[-1]
    rep = hq // hkv
    nb = n // Q_BLOCK
    scale = dk ** -0.5
    qb = q.reshape(b, nb, Q_BLOCK, hkv, rep, dk).transpose(1, 0, 3, 4, 2, 5)

    def attend(qi):
        s = jnp.einsum('bgrqd,bkgd->bgrqk', qi, k).astype(jnp.float32) * scale
        w = jax.nn.softmax(s, axis=-1).astype(v.dtype)
        return jnp.einsum('bgrqk,bkgd->bgrqd', w, v)

    o = lax.map(attend, qb)
    return o.transpose(1, 0, 4, 2, 3, 5).reshape(b, n, hq, dv)

def _ssm_combine(left, right):
    a1, b1 = left
    a2, b2 = right
    return a1 * a2, a2 * b1 + b2

def s5_bidirectional(u, a_re, a_im, log_dt, b_re, b_im, c_re, c_im, d_skip):
    bsz, n, _ = u.shape
    f32 = jnp.float32
    uf = u.astype(f32).reshape(bsz, n, S5_GROUPS, S5_GROUP_CH)
    uc = uf.astype(jnp.complex64)
    y = d_skip.astype(f32).reshape(S5_GROUPS, S5_GROUP_CH) * uf
    for direction in range(2):
        lam = lax.complex(a_re[direction].astype(f32), a_im[direction].astype(f32))
        dt = jnp.exp(log_dt[direction].astype(f32))[:, None]
        lam_bar = jnp.exp(lam * dt)
        b_mat = lax.complex(b_re[direction].astype(f32), b_im[direction].astype(f32))
        b_bar = ((lam_bar - 1.0) / lam)[..., None] * b_mat
        bu = jnp.einsum('blgc,gpc->blgp', uc, b_bar)
        a_elems = jnp.broadcast_to(lam_bar, (1, n) + lam_bar.shape)
        _, xs = lax.associative_scan(_ssm_combine, (a_elems, bu), reverse=(direction == 1), axis=1)
        c_mat = lax.complex(c_re[direction].astype(f32), c_im[direction].astype(f32))
        y = y + jnp.real(jnp.einsum('blgp,gcp->blgc', xs, c_mat))
    return y.reshape(bsz, n, S5_WIDTH).astype(u.dtype)

def peer_ffn(xn, w_query, sub_keys, u_tab, v_tab):
    b, n, d = xn.shape
    t = xn.reshape(b * n, d)
    q = (t @ w_query).reshape(-1, PEER_HEADS, 2, PEER_HALF)
    s = jnp.einsum('thcd,ckd->thck', q, sub_keys).astype(jnp.float32)
    s1, i1 = lax.top_k(s[:, :, 0], PEER_TOPK)
    s2, i2 = lax.top_k(s[:, :, 1], PEER_TOPK)
    cand = (s1[..., :, None] + s2[..., None, :]).reshape(-1, PEER_HEADS, PEER_TOPK * PEER_TOPK)
    cand_id = (i1[..., :, None] * N_KEYS + i2[..., None, :]).reshape(-1, PEER_HEADS, PEER_TOPK * PEER_TOPK)
    top_s, top_pos = lax.top_k(cand, PEER_TOPK)
    eid = jnp.take_along_axis(cand_id, top_pos, axis=-1)
    gates = jax.nn.softmax(top_s, axis=-1).astype(xn.dtype)
    nch = t.shape[0] // PEER_CHUNK

    def expert_chunk(args):
        xc, ec, gc = args
        a = jnp.einsum('cd,ckd->ck', xc, u_tab[ec])
        return jnp.einsum('ck,ckd->cd', gc * jax.nn.gelu(a), v_tab[ec])

    out = lax.map(expert_chunk, (t.reshape(nch, PEER_CHUNK, d),
                                 eid.reshape(nch, PEER_CHUNK, -1),
                                 gates.reshape(nch, PEER_CHUNK, -1)))
    return out.reshape(b, n, d)

def setup_inputs(seed: int = 0) -> dict:
    key = jax.random.key(seed)
    ks = iter(jax.random.split(key, 40))
    f32 = jnp.float32

    def nrm(shape, scale):
        return scale * jax.random.normal(next(ks), shape, f32)

    def gain(shape):
        return 1.0 + nrm(shape, 0.02)

    L = DEPTH
    n_idx = jnp.arange(S5_STATE, dtype=f32)
    return {
        'x': nrm((BATCH, SEQ, D_MODEL), 1.0),
        'p': nrm((DEPTH, BATCH, SEQ, PLE_DIM), 1.0),
        'mix_norm': gain((L, D_MODEL)),
        'w_in': nrm((L, D_MODEL, IN_COLS), D_MODEL ** -0.5),
        'gqa_q_norm': gain((L, HEAD_DIM)),
        'gqa_k_norm': gain((L, HEAD_DIM)),
        'mla_q_norm': gain((L, MLA_Q_RANK)),
        'w_mla_q_up': nrm((L, MLA_Q_RANK, MLA_HEADS * (MLA_NOPE_DIM + MLA_ROPE_DIM)), MLA_Q_RANK ** -0.5),
        'mla_kv_norm': gain((L, MLA_KV_RANK)),
        'w_mla_kv_up': nrm((L, MLA_KV_RANK, MLA_HEADS * (MLA_NOPE_DIM + MLA_V_DIM)), MLA_KV_RANK ** -0.5),
        's5_a_re': -0.5 + nrm((L, 2, S5_GROUPS, S5_STATE), 0.01),
        's5_a_im': math.pi * n_idx + nrm((L, 2, S5_GROUPS, S5_STATE), 0.01),
        's5_log_dt': jax.random.uniform(next(ks), (L, 2, S5_GROUPS), f32, math.log(1e-3), math.log(1e-1)),
        's5_b_re': nrm((L, 2, S5_GROUPS, S5_STATE, S5_GROUP_CH), S5_GROUP_CH ** -0.5),
        's5_b_im': nrm((L, 2, S5_GROUPS, S5_STATE, S5_GROUP_CH), S5_GROUP_CH ** -0.5),
        's5_c_re': nrm((L, 2, S5_GROUPS, S5_GROUP_CH, S5_STATE), S5_STATE ** -0.5),
        's5_c_im': nrm((L, 2, S5_GROUPS, S5_GROUP_CH, S5_STATE), S5_STATE ** -0.5),
        's5_d': nrm((L, S5_WIDTH), 0.5),
        'w_glu': nrm((L, S5_WIDTH, S5_WIDTH), S5_WIDTH ** -0.5),
        'b_glu': nrm((L, S5_WIDTH), 0.02),
        'group_out_norm': gain((L, MIX_WIDTH)),
        'w_out': nrm((L, MIX_WIDTH, D_MODEL), MIX_WIDTH ** -0.5),
        'ffn_norm': gain((L, D_MODEL)),
        'w_peer_query': nrm((L, D_MODEL, PEER_HEADS * PEER_QUERY_DIM), D_MODEL ** -0.5),
        'peer_sub_keys': nrm((L, 2, N_KEYS, PEER_HALF), PEER_HALF ** -0.5),
        'peer_down': nrm((L, N_EXPERTS, D_MODEL), D_MODEL ** -0.5),
        'peer_up': nrm((L, N_EXPERTS, D_MODEL), 0.35),
        'ple_norm': gain((L, D_MODEL)),
        'w_ple_gate': nrm((L, D_MODEL, D_MODEL), D_MODEL ** -0.5),
        'w_ple_proj': nrm((L, PLE_DIM, D_MODEL), PLE_DIM ** -0.5),
        'final_norm': gain((D_MODEL,)),
    }

def reference(x, p, mix_norm, w_in, gqa_q_norm, gqa_k_norm, mla_q_norm, w_mla_q_up,
              mla_kv_norm, w_mla_kv_up, s5_a_re, s5_a_im, s5_log_dt, s5_b_re, s5_b_im,
              s5_c_re, s5_c_im, s5_d, w_glu, b_glu, group_out_norm, w_out, ffn_norm,
              w_peer_query, peer_sub_keys, peer_down, peer_up, ple_norm, w_ple_gate,
              w_ple_proj, final_norm):
    b, n, _ = x.shape
    cos_a, sin_a = axial_rope_tables(n, HEAD_DIM)
    cos_b, sin_b = axial_rope_tables(n, MLA_ROPE_DIM)
    h = x
    for i in range(DEPTH):
        hn = rmsnorm(h, mix_norm[i])
        proj = hn @ w_in[i]
        qa, ka, va, q_lat, kv_lat, k_rope, u_ssm = jnp.split(proj, SPLIT_POINTS, axis=-1)

        qa = apply_rope(rmsnorm(qa.reshape(b, n, GQA_Q_HEADS, HEAD_DIM), gqa_q_norm[i]), cos_a, sin_a)
        ka = apply_rope(rmsnorm(ka.reshape(b, n, GQA_KV_HEADS, HEAD_DIM), gqa_k_norm[i]), cos_a, sin_a)
        va = va.reshape(b, n, GQA_KV_HEADS, HEAD_DIM)
        out_a = blocked_attention(qa, ka, va).reshape(b, n, GQA_WIDTH)

        qb = (rmsnorm(q_lat, mla_q_norm[i]) @ w_mla_q_up[i]).reshape(b, n, MLA_HEADS, MLA_NOPE_DIM + MLA_ROPE_DIM)
        q_nope, q_pe = qb[..., :MLA_NOPE_DIM], apply_rope(qb[..., MLA_NOPE_DIM:], cos_b, sin_b)
        kv = (rmsnorm(kv_lat, mla_kv_norm[i]) @ w_mla_kv_up[i]).reshape(b, n, MLA_HEADS, MLA_NOPE_DIM + MLA_V_DIM)
        k_nope, v_b = kv[..., :MLA_NOPE_DIM], kv[..., MLA_NOPE_DIM:]
        k_pe = apply_rope(k_rope.reshape(b, n, 1, MLA_ROPE_DIM), cos_b, sin_b)
        q_full = jnp.concatenate([q_nope, q_pe], axis=-1)
        k_full = jnp.concatenate([k_nope, jnp.broadcast_to(k_pe, (b, n, MLA_HEADS, MLA_ROPE_DIM))], axis=-1)
        out_b = blocked_attention(q_full, k_full, v_b).reshape(b, n, MLA_WIDTH)

        y = s5_bidirectional(u_ssm, s5_a_re[i], s5_a_im[i], s5_log_dt[i], s5_b_re[i], s5_b_im[i],
                             s5_c_re[i], s5_c_im[i], s5_d[i])
        z = jax.nn.gelu(y)
        out_c = z * jax.nn.sigmoid(z @ w_glu[i] + b_glu[i])

        g = group_out_norm[i]
        merged = jnp.concatenate([
            rmsnorm(out_a, g[:GQA_WIDTH]),
            rmsnorm(out_b, g[GQA_WIDTH:GQA_WIDTH + MLA_WIDTH]),
            rmsnorm(out_c, g[GQA_WIDTH + MLA_WIDTH:]),
        ], axis=-1)
        h = h + merged @ w_out[i]

        h = h + peer_ffn(rmsnorm(h, ffn_norm[i]), w_peer_query[i], peer_sub_keys[i], peer_down[i], peer_up[i])

        gate = jax.nn.sigmoid(rmsnorm(h, ple_norm[i]) @ w_ple_gate[i])
        h = h + gate * (p[i] @ w_ple_proj[i])
    return rmsnorm(h, final_norm)


_drawn_inputs = setup_inputs


def setup_inputs(seed=0):
    import zlib

    import numpy as np

    out = dict(_drawn_inputs(seed))
    spreads = {}
    factors = {'gqa_q_norm': 3.551,
     'gqa_k_norm': 3.44,
     'mla_q_norm': 3.419,
     's5_a_re': 5.905,
     'b_glu': 3.981,
     'ple_norm': 8.0,
     'final_norm': 2.73}
    for name, (base, spread) in spreads.items():
        noise = np.random.default_rng([zlib.crc32(name.encode()), seed]).standard_normal(out[name].shape)
        drawn = base * np.exp(spread * noise) if base else spread * noise
        out[name] = __import__('jax').numpy.asarray(drawn.astype(out[name].dtype))
    for name, factor in factors.items():
        out[name] = (out[name] * factor).astype(out[name].dtype)
    return out
```

```python
from contextlib import ExitStack

import numpy as np

import concourse.bass as bass
from concourse import mybir

F32 = mybir.dt.float32
BF16 = mybir.dt.bfloat16
U32 = mybir.dt.uint32
ALU = mybir.AluOpType
ACT = mybir.ActivationFunctionType
AX = mybir.AxisListType

P = 128
LAYERS = 2
T = 512
TT = T // P
D = 1024
DT = D // P
EPS = 1e-6
HD = 64
ROPE = 32
MD = HD + ROPE
G, CH, ST = 32, 16, 64
Q = 8
NK = T // Q
MT = G * CH // P
GM = G // MT
KEYS = 128
HEADS, TOPK = 8, 16
BLOCKS = 4
JB = KEYS // BLOCKS
BATCH = 8

MIX, GQ, GK, MQ, MKV, GROUP, FFN, PLE, FIN, BGLU, NVEC = 0, 8, 9, 10, 12, 13, 21, 29, 37, 45, 49
T_QA, T_KA, T_QL, T_KVL, T_U, T_VA = 0, 2, 3, 5, 6, 10
N_IN = 11

MAGIC = 12582912.0
TWO_PI = (6.28125, 0.0019350051879882812, 3.019916050561733e-07)
PI_SAFE = 3.1415925


class Phase:

    def __init__(self, nc, *names):
        self.nc, self.names = nc, names

    def __enter__(self):
        self.stack = ExitStack()
        self.sems = [self.stack.enter_context(self.nc.semaphore(n)) for n in self.names]
        return self

    def sb(self, name, shape, dt=F32):
        return self.stack.enter_context(self.nc.sbuf_tensor(name, shape, dt))

    def psum(self, name, shape):
        return self.stack.enter_context(self.nc.psum_tensor(name, shape, F32))

    def __exit__(self, *exc):
        if exc[0] is None:
            nc = self.nc
            nc.all_engine_barrier()
            for s in self.sems:
                nc.gpsimd.sem_clear(s)
            nc.all_engine_barrier()
        return self.stack.__exit__(*exc)


def linear(nc, name, tiles, k, width, weight, products, act_step=None, dve_step=None, banks=1):
    ring = 3
    with Phase(nc, *[f"{name}_weight{r}" for r in range(ring)], f"{name}_product", f"{name}_act",
               f"{name}_dve") as ph:
        *s_weight, s_product, s_act, s_dve = ph.sems
        w = ph.sb(f"{name}_w", [P, ring, k, width])
        ps = ph.psum(f"{name}_ps", [P, 2, banks, T])
        s_free = s_dve if dve_step else s_act
        with nc.Block() as block:

            @block.sync
            def _(sp):
                for i in range(tiles):
                    if i >= ring:
                        sp.wait_ge(s_product, i - ring + 1)
                    sp.dma_start(w[:, i % ring], weight(i)).then_inc(s_weight[i % ring], 16)

            @block.tensor
            def _(pe):
                for i in range(tiles):
                    pe.wait_ge(s_weight[i % ring], 16 * (i // ring + 1))
                    if i >= 2:
                        pe.wait_ge(s_free, i - 1)
                    products(i, ps[:, i % 2], w[:, i % ring]).then_inc(s_product, 1)

            @block.scalar
            def _(act):
                for i in range(tiles if act_step else 0):
                    act.wait_ge(s_product, i + 1)
                    if dve_step and i >= 2:
                        act.wait_ge(s_dve, i - 1)
                    act_step(act, i, ps[:, i % 2]).then_inc(s_act, 1)

            @block.vector
            def _(dve):
                for i in range(tiles if dve_step else 0):
                    if act_step:
                        dve.wait_ge(s_act, i + 1)
                    else:
                        dve.wait_ge(s_product, i + 1)
                    dve_step(dve, i, ps[:, i % 2]).then_inc(s_dve, 1)


def rmsnorm(nc, K, name, groups):
    n = max(len(g[0]) for g in groups)
    with Phase(nc, f"{name}_square", f"{name}_sum", f"{name}_root", f"{name}_out") as ph:
        s_square, s_sum, s_root, s_out = ph.sems
        sq = ph.sb(f"{name}_sq", [P, n, T])
        root = ph.sb(f"{name}_rt", [P, T])
        inv = ph.sb(f"{name}_inv", [P, T])
        ps = ph.psum(f"{name}_ps", [P, 2, T])
        first = [sum(len(g[0]) for g in groups[:i]) for i in range(len(groups))]
        with nc.Block() as block:

            @block.scalar
            def _(act):
                for i, (src, mean, _, _, _) in enumerate(groups):
                    if i:
                        act.wait_ge(s_sum, i)
                        act.wait_ge(s_out, i)
                    for j, tile in enumerate(src):
                        nc.scalar.activation(sq[:, j], tile, ACT.Square).then_inc(s_square, 1)
                    act.wait_ge(s_sum, i + 1)
                    nc.scalar.activation(root[:], ps[:, i % 2], ACT.Sqrt, bias=K.eps[:, 0:1],
                                         scale=1.0 / mean).then_inc(s_root, 1)

            @block.tensor
            def _(pe):
                for i, (src, _, ones, _, _) in enumerate(groups):
                    for j in range(len(src)):
                        pe.wait_ge(s_square, first[i] + j + 1)
                        last = nc.tensor.matmul(ps[:, i % 2], ones[:], sq[:, j], start=(j == 0),
                                                stop=(j == len(src) - 1))
                    last.then_inc(s_sum, 1)

            @block.vector
            def _(dve):
                for i, (src, _, _, gain, dst) in enumerate(groups):
                    dve.wait_ge(s_root, i + 1)
                    nc.vector.reciprocal(inv[:], root[:])
                    dve.drain()
                    for j, tile in enumerate(src):
                        last = nc.vector.scalar_tensor_tensor(
                            out=dst[j], in0=tile, scalar=K.vec[:, gain + j:gain + j + 1], in1=inv[:],
                            op0=ALU.mult, op1=ALU.mult)
                    last.then_inc(s_out, 1)
                    dve.drain()


def constants(nc, K, x_t, const):
    with Phase(nc, "start_load", "start_fill") as ph:
        s_load, s_fill = ph.sems
        with nc.Block() as block:

            @block.sync
            def _(sp):
                sp.dma_start(K.h[:], x_t).then_inc(s_load, 16)
                sp.dma_start(K.const[:], const).then_inc(s_load, 16)
                sp.wait_ge(s_load, 32)

            @block.gpsimd
            def _(pool):
                nc.gpsimd.memset(K.ones[:], 1.0).then_inc(s_fill, 1)
                nc.gpsimd.memset(K.eps[:], EPS).then_inc(s_fill, 1)


def in_projection(nc, K, A, l, w_in, w_rope):
    def products(i, ps, w):
        if i < T_VA:
            for k in range(DT):
                last = nc.tensor.matmul(ps[:, 0], w[:, k], K.xn[:, k], start=(k == 0), stop=(k == DT - 1))
            return last
        for tt in range(TT):
            for k in range(DT):
                last = nc.tensor.matmul(ps[:, 0, tt * P:(tt + 1) * P], K.xn[:, k, tt * P:(tt + 1) * P],
                                        w[:, k], start=(k == 0), stop=(k == DT - 1))
        return last

    def out(act, i, ps):
        if T_U <= i < T_VA:
            return nc.scalar.copy(A.up[:, i - T_U].rearrange("p (q k) -> p q k", q=Q),
                                  ps[:, 0].rearrange("p (k q) -> p q k", q=Q))
        dst = (A.va[:].rearrange("p a b -> p (a b)") if i == T_VA else A.kvl[:] if i == T_KVL
               else A.ql[:, i - T_QL] if i >= T_QL else A.qka[:, i])
        return nc.scalar.copy(dst, ps[:, 0])

    linear(nc, "inproj", N_IN, DT, P, lambda i: w_in[l, i], products, act_step=out)

    def rope_products(i, ps, w):
        for k in range(DT):
            last = nc.tensor.matmul(ps[HD:MD, 0], w[:, k], K.xn[:, k], start=(k == 0), stop=(k == DT - 1))
        return last

    linear(nc, "inrope", 1, DT, ROPE, lambda i: w_rope[l], rope_products,
           act_step=lambda act, i, ps: nc.scalar.copy(A.kpe[HD:MD, :], ps[HD:MD, 0]))


def regroup(nc, name, scratch, chans, places, back):
    by_chan = scratch.rearrange("(m p) q k -> p m (q k)", p=P)
    by_place = scratch.rearrange("(g c) q k -> q c g k", c=CH)
    with Phase(nc, f"{name}_stored", f"{name}_loaded") as ph:
        s_stored, s_loaded = ph.sems
        with nc.Block() as block:

            @block.sync
            def _(sp):
                if not back:
                    sp.dma_start(by_chan, chans[:]).then_inc(s_stored, 16)
                    sp.wait_ge(s_stored, 16)
                    for q in range(Q):
                        sp.dma_start(places[q * CH:(q + 1) * CH], by_place[q]).then_inc(s_loaded, 16)
                    sp.wait_ge(s_loaded, 16 * Q)
                else:
                    for q in range(Q):
                        sp.dma_start(by_place[q], places[q * CH:(q + 1) * CH]).then_inc(s_stored, 16)
                    sp.wait_ge(s_stored, 16 * Q)
                    sp.dma_start(chans[:], by_chan).then_inc(s_loaded, 16)
                    sp.wait_ge(s_loaded, 16)


def cmul(eng, out_r, out_i, a, b, tmp_r, tmp_i):
    eng.tensor_tensor(out_r, a[0], b[0], ALU.mult)
    eng.tensor_tensor(tmp_r, a[1], b[1], ALU.mult)
    eng.tensor_tensor(out_i, a[0], b[1], ALU.mult)
    eng.tensor_tensor(tmp_i, a[1], b[0], ALU.mult)
    eng.drain()
    eng.tensor_tensor(out_r, out_r, tmp_r, ALU.subtract)
    return eng.tensor_tensor(out_i, out_i, tmp_i, ALU.add)


def s5_tables(nc, S, l, s5_lam):
    H = ST
    with Phase(nc, "lam_load", "lam_act", "lam_dve") as ph:
        s_load, s_act, s_dve = ph.sems
        lam = ph.sb("lam", [P, 3, G])
        t = ph.sb("lam_t", [P, 8, G])
        big = ph.sb("lam_big", [P, 2, 4, G])
        power = ph.sb("lam_power", [P, 2, Q + 1, G])
        with nc.Block() as block:

            @block.sync
            def _(sp):
                sp.dma_start(lam[:], s5_lam[l]).then_inc(s_load, 16)

            @block.scalar
            def _(act):
                act.wait_ge(s_load, 16)
                nc.scalar.activation(t[:, 0], lam[:, 2], ACT.Exp).then_inc(s_act, 1)
                act.wait_ge(s_dve, 1)
                nc.scalar.activation(t[:, 3], t[:, 1], ACT.Exp).then_inc(s_act, 1)
                act.wait_ge(s_dve, 2)
                nc.scalar.activation(t[:, 6], t[:, 4], ACT.Sin).then_inc(s_act, 1)
                nc.scalar.activation(t[:, 7], t[:, 5], ACT.Sin).then_inc(s_act, 1)

            @block.vector
            def _(dve):
                v = nc.vector
                dve.wait_ge(s_act, 1)
                v.tensor_tensor(t[:, 1], lam[:, 0], t[:, 0], ALU.mult).then_inc(s_dve, 1)
                v.tensor_tensor(t[:, 2], lam[:, 1], t[:, 0], ALU.mult)
                dve.drain()
                v.tensor_scalar(t[:, 4], t[:, 2], 1.0 / (2.0 * float(np.pi)), MAGIC, ALU.mult, ALU.add)
                dve.drain()
                v.tensor_scalar(t[:, 4], t[:, 4], MAGIC, None, ALU.subtract)
                dve.drain()
                for part in TWO_PI:
                    v.scalar_tensor_tensor(out=t[:, 2], in0=t[:, 4], scalar=-part, in1=t[:, 2],
                                           op0=ALU.mult, op1=ALU.add)
                    dve.drain()
                v.tensor_scalar(t[:, 4], t[:, 2], PI_SAFE, -PI_SAFE, ALU.min, ALU.max)
                dve.drain()
                v.tensor_scalar(t[:, 5], t[:, 4], -1.0, None, ALU.mult)
                dve.drain()
                v.tensor_tensor(t[:, 5], t[:, 5], t[:, 4], ALU.max)
                dve.drain()
                v.tensor_scalar(t[:, 5], t[:, 5], -1.0, float(np.pi) / 2, ALU.mult, ALU.add).then_inc(s_dve, 1)
                dve.wait_ge(s_act, 4)
                v.memset(power[:, 0, 0], 1.0)
                v.memset(power[:, 1, 0], 0.0)
                v.tensor_tensor(power[:, 0, 1], t[:, 3], t[:, 7], ALU.mult)
                v.tensor_tensor(power[:, 1, 1], t[:, 3], t[:, 6], ALU.mult)
                dve.drain()
                for lo, n in ((1, 1), (2, 2), (4, 4)):
                    a = [power[:, r, 1:1 + n] for r in range(2)]
                    b = [power[:, r, lo:lo + 1].broadcast_to([P, n, G]) for r in range(2)]
                    cmul(v, power[:, 0, lo + 1:lo + 1 + n], power[:, 1, lo + 1:lo + 1 + n], a, b,
                         big[:, 0, 0:n], big[:, 1, 0:n])
                    dve.drain()
                v.tensor_scalar(t[:, 0], power[:, 0, 1], -1.0, None, ALU.add)
                v.tensor_tensor(t[:, 1], lam[:, 0], lam[:, 0], ALU.mult)
                v.tensor_tensor(t[:, 2], lam[:, 1], lam[:, 1], ALU.mult)
                v.tensor_scalar(t[:, 3], lam[:, 1], -1.0, None, ALU.mult)
                dve.drain()
                v.tensor_tensor(t[:, 1], t[:, 1], t[:, 2], ALU.add)
                cmul(v, t[:, 4], t[:, 5], (t[:, 0], power[:, 1, 1]), (lam[:, 0], t[:, 3]), t[:, 6], t[:, 7])
                dve.drain()
                v.reciprocal(t[:, 2], t[:, 1])
                dve.drain()
                v.tensor_tensor(S.factor[:, 0], t[:, 4], t[:, 2], ALU.mult)
                v.tensor_tensor(S.factor[:, 1], t[:, 5], t[:, 2], ALU.mult)
                v.memset(S.outpow[:], 0.0)
                dve.drain()
                for r in range(2):
                    v.tensor_copy(S.outpow[0:H, r, 0:Q + 1], power[0:H, r])
                    v.tensor_copy(S.outpow[H:P, r, 1:Q + 2], power[H:P, r, ::-1])
                    v.tensor_copy(S.inpow[0:H, r], power[0:H, r, 0:Q][:, ::-1])
                    v.tensor_copy(S.inpow[H:P, r], power[H:P, r, 0:Q])
                    v.tensor_copy(S.step[:, 0, r], power[:, 0, Q])
                v.tensor_copy(S.step[:, 1, 0], power[:, 1, Q])
                v.tensor_scalar(S.step[:, 1, 1], power[:, 1, Q], -1.0, None, ALU.mult)
                dve.drain()
                v.tensor_scalar(S.outpow[:, 2], S.outpow[:, 1], -1.0, None, ALU.mult)
                dve.drain()


def s5_maps(nc, K, S, l, m, s5_bc, s5_d):
    with Phase(nc, "map_load", "map_bbar", "map_p1", "map_turn", "map_turned", "map_q", "map_k", "map_full",
               "map_m0", "map_s", "map_out") as ph:
        (s_load, s_bbar, s_p1, s_turn, s_turned, s_q, s_k, s_full, s_m0, s_s, s_out) = ph.sems
        bc = ph.sb("bc", [P, 4, GM, CH])
        dd = ph.sb("dd", [CH, GM])
        bbar = ph.sb("bbar", [P, 2, GM, CH])
        btmp = ph.sb("btmp", [P, 2, GM, CH])
        ptmp, p1 = [K.xn[:, n * DT // 2:(n + 1) * DT // 2].rearrange("p a b -> p (a b)")
                    .rearrange("p (r g q c) -> p r g q c", r=2, g=GM, q=Q) for n in range(2)]
        p1t = ph.sb("p1t", [P, 2 * GM, P])
        qtmp = ph.sb("qtmp", [P, GM, Q + 2, CH])
        qmap = ph.sb("qmap_m", [P, 2, GM, Q + 2, CH])
        full = ph.sb("full", [CH, GM, 2 * Q - 1, CH])
        diag = ph.sb("diag", [CH, GM, CH])
        ps_t = ph.psum("ps_t", [P, 2, 4, P])
        ps_k = ph.psum("ps_k", [P, 2, GM, P])
        ps_s = ph.psum("ps_s", [P, 2, GM, NK])
        with nc.Block() as block:

            @block.sync
            def _(sp):
                sp.dma_start(bc[:], s5_bc[l, m]).then_inc(s_load, 16)
                sp.dma_start(dd[:], s5_d[l, m]).then_inc(s_load, 16)
                sp.wait_ge(s_full, 1)
                for q in range(Q):
                    sp.dma_start(S.m0[q * CH:(q + 1) * CH, bass.ds(m * GM, GM), :],
                                 full[:, :, Q - 1 - q:2 * Q - 1 - q].rearrange("c g t d -> c g (t d)")
                                 ).then_inc(s_m0, 16)
                sp.wait_ge(s_m0, 16 * Q)

            @block.vector
            def _(dve):
                v = nc.vector
                dve.wait_ge(s_load, 32)
                f = [S.factor[:, r, bass.ds(m * GM, GM)].unsqueeze(2).broadcast_to([P, GM, CH]) for r in range(2)]
                cmul(v, bbar[:, 0], bbar[:, 1], f, (bc[:, 0], bc[:, 1]), btmp[:, 0], btmp[:, 1])
                dve.drain()
                shape = [P, GM, Q, CH]
                pw = [S.inpow[:, r, :, bass.ds(m * GM, GM)].rearrange("p q g -> p g q").unsqueeze(3)
                      .broadcast_to(shape) for r in range(2)]
                bb = [bbar[:, r].unsqueeze(2).broadcast_to(shape) for r in range(2)]
                cmul(v, p1[:, 0], p1[:, 1], pw, bb, ptmp[:, 0], ptmp[:, 1]).then_inc(s_p1, 1)
                dve.wait_ge(s_k, 1)
                kf = ps_k[0:CH, 0].rearrange("c g (t d) -> c g t d", d=CH)
                kb = ps_k[0:CH, 1].rearrange("c g (t d) -> c g t d", d=CH)
                v.tensor_copy(full[:, :, 0:Q], kb)
                v.tensor_copy(full[:, :, Q:2 * Q - 1], kf[:, :, 1:Q])
                v.tensor_tensor(diag[:], K.ident[0:CH, 0:CH].unsqueeze(1).broadcast_to([CH, GM, CH]),
                                dd[:].unsqueeze(2).broadcast_to([CH, GM, CH]), ALU.mult)
                dve.drain()
                v.tensor_tensor(full[:, :, Q - 1], full[:, :, Q - 1], kf[:, :, 0], ALU.add)
                dve.drain()
                v.tensor_tensor(full[:, :, Q - 1], full[:, :, Q - 1], diag[:], ALU.add).then_inc(s_full, 1)

            @block.gpsimd
            def _(pool):
                g = nc.gpsimd
                pool.wait_ge(s_load, 32)
                shape = [P, GM, Q + 2, CH]
                c = [bc[:, 2 + r].unsqueeze(2).broadcast_to(shape) for r in range(2)]
                pw = [S.outpow[:, r, :, bass.ds(m * GM, GM)].rearrange("p q g -> p g q").unsqueeze(3)
                      .broadcast_to(shape) for r in range(3)]
                g.tensor_tensor(qmap[:, 0], c[0], pw[0], ALU.mult)
                g.tensor_tensor(qtmp[:], c[1], pw[2], ALU.mult)
                pool.drain()
                g.tensor_tensor(qmap[:, 0], qmap[:, 0], qtmp[:], ALU.add)
                pool.drain()
                g.tensor_tensor(qmap[:, 1], c[0], pw[2], ALU.mult)
                g.tensor_tensor(qtmp[:], c[1], pw[0], ALU.mult)
                pool.drain()
                g.tensor_tensor(qmap[:, 1], qmap[:, 1], qtmp[:], ALU.subtract).then_inc(s_q, 1)

            @block.tensor
            def _(pe):
                pe.wait_ge(s_p1, 1)
                for n in range(2 * GM // 4):
                    if n >= 2:
                        pe.wait_ge(s_turned, n - 1)
                    for u in range(4):
                        r, g = divmod(4 * n + u, GM)
                        last = nc.tensor.transpose(ps_t[:, n % 2, u], p1[:, r, g].rearrange("p q c -> p (q c)"),
                                                   K.ident[:])
                    last.then_inc(s_turn, 1)
                pe.wait_ge(s_q, 1)
                for back in range(2):
                    lo = back * ST
                    for g in range(GM):
                        for r in range(2):
                            rhs = qmap[lo:lo + ST, r, g, 2 * back:2 * back + Q]
                            last = nc.tensor.matmul(ps_k[0:CH, back, g], bbar[lo:lo + ST, r, g],
                                                    rhs.rearrange("p s c -> p (s c)"),
                                                    start=(r == 0), stop=(r == 1))
                last.then_inc(s_k, 1)
                pe.wait_ge(s_turned, 2 * GM // 4)
                for r in range(2):
                    for g in range(GM):
                        last = nc.tensor.matmul(ps_s[:, r, g], p1t[:, r * GM + g],
                                                S.ug[:, bass.ds(m * GM + g, 1), :].rearrange("p o k -> p (o k)"),
                                                start=True, stop=True)
                last.then_inc(s_s, 1)

            @block.scalar
            def _(act):
                for n in range(2 * GM // 4):
                    act.wait_ge(s_turn, n + 1)
                    nc.scalar.copy(p1t[:, 4 * n:4 * n + 4], ps_t[:, n % 2]).then_inc(s_turned, 1)
                act.wait_ge(s_q, 1)
                nc.scalar.copy(S.qmap[:, :, bass.ds(m * GM, GM)].rearrange("p r g s c -> p r (g s c)"),
                               qmap[:].rearrange("p r g s c -> p r (g s c)"))
                act.wait_ge(s_s, 1)
                for r in range(2):
                    for lo, order in ((0, 1), (ST, -1)):
                        nc.scalar.copy(
                            S.s[lo:lo + ST, :, r, bass.ds(m * GM, GM)].rearrange("p k g -> p g k"),
                            ps_s[lo:lo + ST, r][:, :, ::order]).then_inc(s_out, 1)


def s5_scan(nc, S):
    with Phase(nc, "scan_done", "scan_order") as ph:
        s_done, s_order = ph.sems
        t = ph.sb("scan_t", [P, 2, 2, G])
        with nc.Block() as block:

            @block.vector
            def _(dve):
                v = nc.vector
                v.memset(S.x[:, 0], 0.0)
                v.memset(S.x[:, 1], 0.0)
                dve.drain()
                with dve.Fori(0, NK - 1) as k:
                    x = S.x[:, bass.ds(k, 1)].rearrange("p o r g -> p (o r) g")
                    y = S.x[:, bass.ds(k + 1, 1)].rearrange("p o r g -> p (o r) g")
                    s = S.s[:, bass.ds(k, 1)].rearrange("p o r g -> p (o r) g")
                    v.tensor_tensor(t[:, 0], S.step[:, 0], x, ALU.mult)
                    v.tensor_tensor(t[:, 1, ::-1], S.step[:, 1], x, ALU.mult)
                    dve.drain()
                    v.tensor_tensor(t[:, 0], t[:, 0], s, ALU.add)
                    dve.drain()
                    v.tensor_tensor(y, t[:, 0], t[:, 1], ALU.add)
                    dve.drain()
                v.tensor_copy(S.xq[0:ST], S.x[0:ST].rearrange("p k r g -> p r g k")).then_inc(s_done, 1)

            @block.scalar
            def _(act):
                act.wait_ge(s_done, 1)
                for r in range(2):
                    nc.scalar.copy(S.xq[ST:P, r], S.x[ST:P, :, r].rearrange("p k g -> p g k")[:, :, ::-1])


def s5_output(nc, S, z):
    with Phase(nc, "y_product", "y_gelu") as ph:
        s_y, s_gelu = ph.sems
        ps = ph.psum("ps_y", [P, 2, GM, NK])
        with nc.Block() as block:

            @block.tensor
            def _(pe):
                for m in range(MT):
                    if m >= 2:
                        pe.wait_ge(s_gelu, m - 1)
                    for gg in range(GM):
                        g = m * GM + gg
                        nc.tensor.matmul(ps[:, m % 2, gg], S.m0[:, g], S.ug[:, g], start=True, stop=False)
                        for r in range(2):
                            last = nc.tensor.matmul(ps[:, m % 2, gg],
                                                    S.qmap[:, r, g, 1:Q + 1].rearrange("p s c -> p (s c)"),
                                                    S.xq[:, r, g], start=False, stop=(r == 1))
                    last.then_inc(s_y, 1)

            @block.scalar
            def _(act):
                for m in range(MT):
                    act.wait_ge(s_y, m + 1)
                    nc.scalar.activation(z[:, m * GM:(m + 1) * GM], ps[:, m % 2],
                                         ACT.Gelu_apprx_tanh).then_inc(s_gelu, 1)


def s5_glu(nc, K, A, l, w_glu):
    with nc.sbuf_tensor("sig", [P, 2, T], F32) as sig:
        def products(i, ps, w):
            for k in range(MT):
                last = nc.tensor.matmul(ps[:, 0], w[:, k], A.up[:, k], start=(k == 0), stop=(k == MT - 1))
            return last

        def gate(act, i, ps):
            return nc.scalar.activation(sig[:, i % 2], ps[:, 0], ACT.Sigmoid, bias=K.vec[:, BGLU + i:BGLU + i + 1])

        def out(dve, i, ps):
            return nc.vector.tensor_tensor(
                A.mixed[:, 4 + i].rearrange("p (k q) -> p q k", q=Q),
                A.up[:, i].rearrange("p (q k) -> p q k", q=Q),
                sig[:, i % 2].rearrange("p (q k) -> p q k", q=Q), ALU.mult)

        linear(nc, "glu", MT, MT, P, lambda i: w_glu[l, i], products, act_step=gate, dve_step=out)


def gqa_rope(nc, K, A, rope_a):
    with Phase(nc, "ropea_load", "ropea_turn", "ropea_out") as ph:
        s_load, s_turn, s_out = ph.sems
        table = ph.sb("rope_a", [P, 2, T])
        t = ph.sb("rope_at", [P, 2, T])
        ps = ph.psum("ps_ra", [P, 3, T])
        with nc.Block() as block:

            @block.sync
            def _(sp):
                sp.dma_start(table[:], rope_a).then_inc(s_load, 16)

            @block.tensor
            def _(pe):
                for i in range(3):
                    nc.tensor.matmul(ps[:, i], K.turn_a[:], A.qka[:, i], start=True, stop=True).then_inc(s_turn, 1)

            @block.vector
            def _(dve):
                v = nc.vector
                dve.wait_ge(s_load, 16)
                for i in range(3):
                    dve.wait_ge(s_turn, i + 1)
                    v.tensor_tensor(t[:, 0], ps[:, i], table[:, 1], ALU.mult)
                    v.tensor_tensor(t[:, 1], A.qka[:, i], table[:, 0], ALU.mult)
                    dve.drain()
                    v.tensor_tensor(A.qka[:, i], t[:, 0], t[:, 1], ALU.add).then_inc(s_out, 1)
                    dve.drain()


def mla_heads(nc, K, A, l, w_qup, w_kvup, rope_b):
    with Phase(nc, "up_load", "up_q", "up_k", "up_v", "up_qout", "up_kout", "up_vout", "up_turn", "up_out") as ph:
        s_load, s_q, s_k, s_v, s_qout, s_kout, s_vout, s_turn, s_out = ph.sems
        wq = ph.sb("w_qup", [P, 2, 4 * MD])
        wkv = ph.sb("w_kvup", [P, 4, 2, HD])
        table = ph.sb("rope_b", [P, 2, T])
        t = ph.sb("rope_bt", [P, 2, T])
        ps_a = ph.psum("ps_up", [P, 2, T])
        ps_v = ph.psum("ps_v", [P, 2, T])
        ps_r = ph.psum("ps_rb", [P, 2, T])
        rot = slice(HD, MD)
        with nc.Block() as block:

            @block.sync
            def _(sp):
                sp.dma_start(wq[:], w_qup[l]).then_inc(s_load, 16)
                sp.dma_start(wkv[:], w_kvup[l]).then_inc(s_load, 16)
                sp.dma_start(table[rot], rope_b).then_inc(s_load, 16)

            @block.tensor
            def _(pe):
                pe.wait_ge(s_load, 48)
                for h in range(4):
                    if h >= 2:
                        pe.wait_ge(s_qout, h - 1)
                    for k in range(2):
                        last = nc.tensor.matmul(ps_a[0:MD, h % 2], wq[:, k, h * MD:(h + 1) * MD], A.ql[:, k],
                                                start=(k == 0), stop=(k == 1))
                    last.then_inc(s_q, 1)
                for h in range(4):
                    pe.wait_ge(s_qout if h < 2 else s_kout, h + 3 if h < 2 else h - 1)
                    nc.tensor.matmul(ps_a[0:HD, h % 2], wkv[:, h, 0], A.kvl[:], start=True,
                                     stop=True).then_inc(s_k, 1)
                for tt in range(TT):
                    last = nc.tensor.matmul(ps_v[:, tt // 2, (tt % 2) * 256:(tt % 2 + 1) * 256],
                                            A.kvl[:, tt * P:(tt + 1) * P], wkv[:, :, 1], start=True, stop=True)
                last.then_inc(s_v, 1)
                for n in range(5):
                    if n >= 2:
                        pe.wait_ge(s_out, n - 1)
                    rhs = A.qb[rot, n] if n < 4 else A.kpe[rot, :]
                    nc.tensor.matmul(ps_r[rot, n % 2], K.turn_b[rot], rhs, start=True, stop=True).then_inc(s_turn, 1)

            @block.scalar
            def _(act):
                for h in range(4):
                    act.wait_ge(s_q, h + 1)
                    nc.scalar.copy(A.qb[0:MD, h], ps_a[0:MD, h % 2]).then_inc(s_qout, 1)
                for h in range(4):
                    act.wait_ge(s_k, h + 1)
                    nc.scalar.copy(A.kb[0:HD, h], ps_a[0:HD, h % 2]).then_inc(s_kout, 1)
                act.wait_ge(s_v, 1)
                nc.scalar.copy(A.vb[:].rearrange("p a b -> p (a b)"),
                               ps_v[:].rearrange("p a b -> p (a b)")).then_inc(s_vout, 1)

            @block.vector
            def _(dve):
                v = nc.vector
                for n in range(5):
                    dve.wait_ge(s_turn, n + 1)
                    x = A.qb[rot, n] if n < 4 else A.kpe[rot, :]
                    v.tensor_tensor(t[rot, 0], ps_r[rot, n % 2], table[rot, 1], ALU.mult)
                    v.tensor_tensor(t[rot, 1], x, table[rot, 0], ALU.mult)
                    dve.drain()
                    if n < 4:
                        v.tensor_tensor(x, t[rot, 0], t[rot, 1], ALU.add).then_inc(s_out, 1)
                        dve.drain()
                    else:
                        for h in range(4):
                            v.tensor_tensor(A.kb[rot, h], t[rot, 0], t[rot, 1], ALU.add)


def attention(nc, K, A):
    heads = []
    for h in range(4):
        g, r = h // 2, h % 2
        lo = g * HD
        heads.append((A.qka[lo:lo + HD, r], A.qka[lo:lo + HD, 2], [A.va[:, kt, lo:lo + HD] for kt in range(TT)],
                      float(HD) ** -0.5))
    for h in range(4):
        heads.append((A.qb[0:MD, h], A.kb[0:MD, h], [A.vb[:, kt, h * HD:(h + 1) * HD] for kt in range(TT)],
                      float(MD) ** -0.5))
    N = len(heads) * TT
    with Phase(nc, "att_score", "att_max", "att_exp", "att_norm", "att_turn", "att_turned", "att_value",
               "att_out") as ph:
        s_score, s_max, s_exp, s_norm, s_turn, s_turned, s_value, s_out = ph.sems
        w = ph.sb("att_w", [P, 2, T])
        wt = ph.sb("att_wt", [P, 2, TT, T])
        st = ph.sb("att_st", [P, 4, N])
        ps_s = ph.psum("ps_as", [P, 3, T])
        ps_t = ph.psum("ps_at", [P, 2, TT, P])
        ps_o = ph.psum("ps_ao", [P, 2, T])
        with nc.Block() as block:

            @block.tensor
            def _(pe):
                def turn(n):
                    pe.wait_ge(s_norm, n + 1)
                    if n >= 2:
                        pe.wait_ge(s_turned, n - 1)
                    for kt in range(TT):
                        last = nc.tensor.transpose(ps_t[:, n % 2, kt], w[:, n % 2, kt * P:(kt + 1) * P], K.ident[:])
                    last.then_inc(s_turn, 1)

                def values(h):
                    lo = (h % 2) * HD
                    pe.wait_ge(s_turned, TT * (h + 1))
                    if h >= 2:
                        pe.wait_ge(s_out, h - 1)
                    for kt in range(TT):
                        last = nc.tensor.matmul(ps_o[lo:lo + HD, h % 2], heads[h][2][kt], wt[:, h % 2, kt],
                                                start=(kt == 0), stop=(kt == TT - 1))
                    last.then_inc(s_value, 1)

                for n in range(N + 2):
                    if n < N:
                        h, qt = divmod(n, TT)
                        if n >= 3:
                            pe.wait_ge(s_exp, n - 2)
                        nc.tensor.matmul(ps_s[:, n % 3], heads[h][0][:, qt * P:(qt + 1) * P], heads[h][1],
                                         start=True, stop=True).then_inc(s_score, 1)
                    if n >= 2:
                        turn(n - 2)
                    if n >= 6 and (n - 6) % TT == 0:
                        values((n - 6) // TT)
                values(len(heads) - 1)

            @block.vector
            def _(dve):
                v = nc.vector
                for n in range(N + 1):
                    if n < N:
                        scale = heads[n // TT][3]
                        dve.wait_ge(s_score, n + 1)
                        v.tensor_reduce(st[:, 0, n:n + 1], ps_s[:, n % 3], AX.X, ALU.max)
                        dve.drain()
                        v.tensor_scalar(st[:, 1, n:n + 1], st[:, 0, n:n + 1], -scale, None,
                                        ALU.mult).then_inc(s_max, 1)
                    if n >= 1:
                        m = n - 1
                        dve.wait_ge(s_exp, n)
                        v.reciprocal(st[:, 3, m:n], st[:, 2, m:n])
                        dve.drain()
                        v.tensor_scalar(w[:, m % 2], w[:, m % 2], st[:, 3, m:n], None, ALU.mult).then_inc(s_norm, 1)

            @block.scalar
            def _(act):
                def turned(n):
                    h, qt = divmod(n, TT)
                    act.wait_ge(s_turn, n + 1)
                    if h >= 2:
                        act.wait_ge(s_value, h - 1)
                    nc.scalar.copy(wt[:, h % 2, :, qt * P:(qt + 1) * P], ps_t[:, n % 2]).then_inc(s_turned, 1)

                def out(h):
                    lo = (h % 2) * HD
                    act.wait_ge(s_value, h + 1)
                    nc.scalar.copy(A.mixed[lo:lo + HD, h // 2], ps_o[lo:lo + HD, h % 2]).then_inc(s_out, 1)

                for n in range(N + 2):
                    if n < N:
                        act.wait_ge(s_max, n + 1)
                        if n >= 2:
                            act.wait_ge(s_turn, n - 1)
                        nc.scalar.activation(w[:, n % 2], ps_s[:, n % 3], ACT.Exp, bias=st[:, 1, n:n + 1],
                                             scale=heads[n // TT][3], accum_out=st[:, 2, n:n + 1]
                                             ).then_inc(s_exp, 1)
                    if n >= 2:
                        turned(n - 2)
                    if n >= 7 and (n - 7) % TT == 0:
                        out((n - 7) // TT)
                for h in range((N + 1 - 7) // TT + 1, len(heads)):
                    out(h)


def mix_out(nc, K, A, l, w_out):
    def products(i, ps, w):
        for k in range(DT):
            last = nc.tensor.matmul(ps[:, 0], w[:, k], A.mixed[:, k], start=(k == 0), stop=(k == DT - 1))
        return last

    linear(nc, "mixout", DT, DT, P, lambda i: w_out[l, i], products,
           dve_step=lambda dve, i, ps: nc.vector.tensor_tensor(K.h[:, i], K.h[:, i], ps[:, 0], ALU.add))


def ple(nc, K, l, p_t, w_ple):
    with Phase(nc, "emb_load") as ph:
        s_load, = ph.sems
        emb = ph.sb("emb", [P, 2, T])
        gate = ph.sb("emb_gate", [P, 2, T])
        t = ph.sb("emb_t", [P, 2, T])
        with nc.Block() as block:

            @block.sync
            def _(sp):
                sp.dma_start(emb[:], p_t[l]).then_inc(s_load, 16)
                sp.wait_ge(s_load, 16)

        def products(i, ps, w):
            for k in range(DT):
                nc.tensor.matmul(ps[:, 0], w[:, k], K.xn[:, k], start=(k == 0), stop=(k == DT - 1))
            for k in range(2):
                last = nc.tensor.matmul(ps[:, 1], w[:, DT + k], emb[:, k], start=(k == 0), stop=(k == 1))
            return last

        def out(dve, i, ps):
            nc.vector.tensor_tensor(t[:, i % 2], gate[:, i % 2], ps[:, 1], ALU.mult)
            dve.drain()
            return nc.vector.tensor_tensor(K.h[:, i], K.h[:, i], t[:, i % 2], ALU.add)

        linear(nc, "ple", DT, DT + 2, P, lambda i: w_ple[l, i], products,
               act_step=lambda act, i, ps: nc.scalar.activation(gate[:, i % 2], ps[:, 0], ACT.Sigmoid),
               dve_step=out, banks=2)


def peer(nc, K, l, w_query, sub_keys, down_t, up):
    GB = 2 * BATCH
    STEPS = 4
    TURNS = JB // STEPS
    VB = DT // 2
    names = (["w_query0", "w_query1", "sub_keys"] + [f"down{r}" for r in range(2)] + [f"up{r}" for r in range(STEPS)]
             + ["hidden", "gelu", "query", "query_out", "scores", "scores_out", "ranked", "shifted", "exped",
                "picked", "pick_turn", "pick_turned", "onehot", "gate", "gated", "value", "added"])
    with Phase(nc, *["peer_" + n for n in names]) as ph:
        S = dict(zip(names, ph.sems))
        s_wq = [S["w_query0"], S["w_query1"]]
        s_down = [S[f"down{r}"] for r in range(2)]
        s_up = [S[f"up{r}"] for r in range(STEPS)]
        act_w = ph.sb("act_w", [P, JB, T])
        down_w = ph.sb("down_w", [P, 2, DT, P])
        up_w = ph.sb("up_w", [P, STEPS, VB * P])
        hot_i = ph.sb("hot_i", [P, 4, BATCH, KEYS], BF16)
        is_j = ph.sb("is_j", [P, 4, BATCH, JB], BF16)
        hot_j = ph.sb("hot_j", [P, 4, 3, BATCH, JB], BF16)
        key_t = ph.sb("key_t", [P, 2, T], BF16)
        gate_t = ph.sb("gate_t", [P, 3, T], BF16)
        rest = ph.sb("gate_rest", [P, T])
        ps_v = ph.psum("ps_val", [P, VB, T])
        ps_a = ph.psum("ps_hid", [P, 2, T])
        ps_g = ph.psum("ps_gate", [P, 2, GB, JB])
        other = ph.sb("act_o", [P, JB, T])
        room = [other[:].rearrange("p j t -> p (j t)"), 0]

        def carve(shape, dt=F32):
            n = int(np.prod(shape)) // (2 if dt == BF16 else 1)
            v = room[0][:, room[1]:room[1] + n]
            room[1] += n
            v = v if dt == F32 else v.bitcast(dt)
            names = "abcd"[:len(shape)]
            sizes = {c: s for c, s in zip(names[1:], shape[1:])}
            return v.rearrange(f"p ({' '.join(names)}) -> p {' '.join(names)}", **sizes) if len(shape) > 1 else v

        wq = carve([2, DT, 256])
        keys = carve([2, KEYS])
        qh = carve([2, 2, T])
        sc = [carve([TT * 2, KEYS]) for _ in range(2)]
        top = carve([TT * 2, TOPK])
        topi = carve([TT * 2, TOPK], U32)
        cand = carve([TT, TOPK * TOPK])
        best = carve([TT, TOPK])
        besti = carve([TT, TOPK], U32)
        rank = carve([2, TT, TOPK], U32)
        rankb = carve([2, TT, TOPK], BF16)
        keyb = carve([TT * 2, TOPK], BF16)
        eq = carve([TT, TOPK, TOPK], BF16)
        picks = carve([3, TT, P])
        sums = carve([TT, HEADS])
        assert room[1] <= JB * T
        wbuf = [act_w, other]

        with nc.Block() as block:

            @block.sync
            def _(sp):
                def down(q, j, n):
                    sp.dma_start(down_w[:, j % 2], down_t[l, bass.ds(q * JB + n, 1)].rearrange("o p k i -> p (o k) i")
                                 ).then_inc(s_down[j % 2], 16)

                def load_up(q, half, j, u):
                    sp.dma_start(up_w[:, u], up[l, bass.ds(q * JB + j, 1), half].rearrange("o p d -> p (o d)")
                                 ).then_inc(s_up[u], 16)

                def down_turn(q, it):
                    for u in range(STEPS):
                        n = it * STEPS + u
                        if not (isinstance(n, int) and q == 0 and n < 2):
                            sp.wait_ge(S["hidden"], q * JB + n - 1)
                        down(q, u, n)

                def up_turn(q, half, it):
                    base = (2 * q + half) * JB
                    for u in range(STEPS):
                        n = it * STEPS + u
                        if not (isinstance(n, int) and base == 0 and n < STEPS):
                            sp.wait_ge(S["value"], base + n - STEPS + 1)
                        load_up(q, half, n, u)

                def down_block(q):
                    down_turn(q, 0)
                    with sp.Fori(1, TURNS) as it:
                        down_turn(q, it)

                def up_block(q):
                    for half in range(2):
                        up_turn(q, half, 0)
                        with sp.Fori(1, TURNS) as it:
                            up_turn(q, half, it)

                down_block(0)
                for q in range(BLOCKS):
                    if q + 1 < BLOCKS:
                        down_block(q + 1)
                    up_block(q)

            @block.tensor
            def _(pe):
                def hidden(q, n, u):
                    pe.wait_ge(s_down[u % 2], 16 * ((q * JB + n - (u % 2)) // 2 + 1) if isinstance(n, int)
                               else 8 * q * JB + 8 * (n - (u % 2)) + 16)
                    if not (isinstance(n, int) and q * JB + n < 2):
                        pe.wait_ge(S["gelu"], q * JB + n - 1)
                    for k in range(DT):
                        last = nc.tensor.matmul(ps_a[:, u % 2], down_w[:, u % 2, k], K.xn[:, k], start=(k == 0),
                                                stop=(k == DT - 1))
                    last.then_inc(S["hidden"], 1)

                def value(q, half, n, u, first):
                    base = (2 * q + half) * JB
                    pe.wait_ge(s_up[u], (16 * ((base + n) // STEPS + 1)) if isinstance(n, int)
                               else 16 * (base // STEPS + 1) + 4 * (n - u))
                    for c in range(VB):
                        if first and 2 * q + half:
                            pe.wait_ge(S["added"], VB * (2 * q + half - 1) + c + 1)
                        rhs = wbuf[q % 2][:, bass.ds(n, 1)].rearrange("p o t -> p (o t)")
                        last = nc.tensor.matmul(ps_v[:, c], up_w[:, u, c * P:(c + 1) * P], rhs,
                                                start=first, stop=False, skip_group_check=True)
                    last.then_inc(S["value"], 1)

                def head(it, u):
                    h = it * 2 + u
                    first = isinstance(h, int) and h == 0
                    pe.wait_ge(s_wq[u], 16 * (it + 1))
                    for c in range(2):
                        if not first:
                            pe.wait_ge(S["query_out"], 2 * h - 1 + c)
                        for k in range(DT):
                            last = nc.tensor.matmul(ps_v[:, c], wq[:, u, k, c * P:(c + 1) * P], K.xn[:, k],
                                                    start=(k == 0), stop=(k == DT - 1))
                        last.then_inc(S["query"], 1)
                    pe.wait_ge(S["query_out"], 2 * h + 2)
                    if not first:
                        pe.wait_ge(S["scores_out"], h)
                    for tt in range(TT):
                        for c in range(2):
                            lo = (tt % 2) * 256 + c * P
                            last = nc.tensor.matmul(ps_v[:, 2 + tt // 2, lo:lo + P], qh[:, u, c, tt * P:(tt + 1) * P],
                                                    keys[:, c], start=True, stop=True)
                    last.then_inc(S["scores"], 1)

                def gates(q, quad, u):
                    if u % 2 == 0 and not (isinstance(quad, int) and q == 0 and quad == 0):
                        pe.wait_ge(S["gated"], q * (T // GB) + quad * 2 + u // 2 - 1)
                    pe.wait_ge(S["onehot"], q * (T // BATCH) + quad * 4 + u + 1)
                    for i in range(BATCH):
                        for part in range(3):
                            last = nc.tensor.matmul(ps_g[:, u // 2, (u % 2) * BATCH + i], hot_i[:, u, i],
                                                    hot_j[:, u, part, i], start=(part == 0), stop=(part == 2))
                    last.then_inc(S["gate"], 1)

                def head_turn(it):
                    for u in range(2):
                        head(it, u)
                        for s in range(4):
                            hidden(0, it * 8 + u * 4 + s, s)

                pe.wait_ge(S["sub_keys"], 16)
                head_turn(0)
                with pe.Fori(1, HEADS // 2) as it:
                    head_turn(it)
                pe.wait_ge(S["picked"], 1)
                for n in range(3):
                    for tt in range(TT):
                        last = nc.tensor.transpose(ps_v[:, n, tt * P:(tt + 1) * P], picks[:, n, tt], K.ident[:])
                    last.then_inc(S["pick_turn"], 1)

                def loop(turn):
                    turn(0)
                    with pe.Fori(1, TURNS) as it:
                        turn(it)

                def second_block(it):
                    for u in range(STEPS):
                        hidden(1, it * STEPS + u, u)
                        for s in range(2):
                            gates(0, it * 2 + u // 2, (u % 2) * 2 + s)

                def value_turn(q, half, it):
                    for u in range(STEPS):
                        value(q, half, it * STEPS + u, u, isinstance(it, int) and u == 0)
                        if q + 1 < BLOCKS:
                            gates(q + 1, half * TURNS + it, u)

                def hidden_turn(q, it):
                    for u in range(STEPS):
                        hidden(q, it * STEPS + u, u)

                loop(second_block)
                pe.wait_ge(S["pick_turned"], 3)
                for q in range(BLOCKS):
                    pe.wait_ge(S["gated"], (q + 1) * (T // GB))
                    for half in range(2):
                        loop(lambda it: value_turn(q, half, it))
                    if q + 2 < BLOCKS:
                        loop(lambda it: hidden_turn(q + 2, it))

            @block.scalar
            def _(act):
                def gelu(q, n, u):
                    act.wait_ge(S["hidden"], q * JB + n + 1)
                    dst = wbuf[q % 2][:, bass.ds(n, 1)].rearrange("p o t -> p (o t)")
                    nc.scalar.activation(dst, ps_a[:, u % 2], ACT.Gelu_apprx_tanh).then_inc(S["gelu"], 1)

                def load_query(h, u):
                    act.dma_start(wq[:, u], w_query[l, bass.ds(h, 1)].rearrange("o p k c -> p (o k) c")
                                  ).then_inc(s_wq[u], 16)

                def first(it):
                    return isinstance(it, int) and it == 0

                def head(it, u, load):
                    h = it * 2 + u
                    for c in range(2):
                        act.wait_ge(S["query"], 2 * h + c + 1)
                        if not first(it):
                            act.wait_ge(S["scores"], h - 1)
                        nc.scalar.copy(qh[:, u, c], ps_v[:, c]).then_inc(S["query_out"], 1)
                    act.wait_ge(S["scores"], h + 1)
                    if load:
                        load_query(h + 2, u)
                    if not first(it):
                        act.wait_ge(S["ranked"], h - 1)
                    nc.scalar.copy(sc[u].rearrange("p a b -> p (a b)"),
                                   ps_v[:, 2:4].rearrange("p a b -> p (a b)")).then_inc(S["scores_out"], 1)

                def head_turn(it, load=True):
                    for u in range(2):
                        head(it, u, load)
                        for s in range(4):
                            gelu(0, it * 8 + u * 4 + s, s)

                act.dma_start(keys, sub_keys[l]).then_inc(S["sub_keys"], 16)
                for u in range(2):
                    load_query(u, u)
                head_turn(0)
                with act.Fori(1, HEADS // 2 - 1) as it:
                    head_turn(it)
                head_turn(HEADS // 2 - 1, load=False)
                act.wait_ge(S["shifted"], 1)
                nc.scalar.activation(picks[:, 2], picks[:, 2], ACT.Exp).then_inc(S["exped"], 1)
                for n in range(2):
                    act.wait_ge(S["pick_turn"], n + 1)
                    nc.scalar.copy(key_t[:, n], ps_v[:, n]).then_inc(S["pick_turned"], 1)
                for q in range(1, BLOCKS):
                    with act.Fori(0, TURNS) as it:
                        for u in range(STEPS):
                            gelu(q, it * STEPS + u, u)

            @block.vector
            def _(dve):
                v = nc.vector
                NEG = -3.0e38

                def top16(values, out, index, rows):
                    for i in range(rows):
                        v.max(out[:, i, 0:8], values[:, i])
                    dve.drain()
                    for i in range(rows):
                        v.max_index(index[:, i, 0:8], out[:, i, 0:8], values[:, i])
                    for i in range(rows):
                        v.match_replace(values[:, i], out[:, i, 0:8], values[:, i], NEG)
                    dve.drain()
                    for i in range(rows):
                        v.max(out[:, i, 8:16], values[:, i])
                    dve.drain()
                    for i in range(rows):
                        v.max_index(index[:, i, 8:16], out[:, i, 8:16], values[:, i])
                    dve.drain()

                def head(it, u):
                    h = it * 2 + u
                    cols = bass.ds(h * TOPK, TOPK)
                    dve.wait_ge(S["scores_out"], h + 1)
                    v.tensor_copy(sums[:, 0, 0:1], sc[u][:, 0, 0:1])
                    top16(sc[u], top, topi, TT * 2)
                    v.tensor_copy(keyb, topi)
                    pair = top.rearrange("p (t c) k -> p t c k", c=2)
                    shape = [P, TT, TOPK, TOPK]
                    v.tensor_tensor(cand.rearrange("p t (a b) -> p t a b", b=TOPK),
                                    pair[:, :, 0].unsqueeze(3).broadcast_to(shape),
                                    pair[:, :, 1].unsqueeze(2).broadcast_to(shape), ALU.add)
                    dve.drain()
                    top16(cand, best, besti, TT)
                    v.tensor_scalar(rank[:, 0], besti, 4, None, ALU.logical_shift_right)
                    v.tensor_scalar(rank[:, 1], besti, 15, None, ALU.bitwise_and)
                    v.tensor_tensor(picks[:, 2, :, cols], best,
                                    best[:, :, 0:1].broadcast_to([P, TT, TOPK]), ALU.subtract)
                    dve.drain()
                    v.tensor_copy(rankb, rank)
                    dve.drain()
                    keypair = keyb.rearrange("p (t c) k -> p t c k", c=2)
                    iota16 = K.iotab[:, 0:TOPK].unsqueeze(1).unsqueeze(1).broadcast_to(shape)
                    for c in range(2):
                        v.tensor_tensor(eq, rankb[:, c].unsqueeze(3).broadcast_to(shape), iota16, ALU.is_equal)
                        dve.drain()
                        v.tensor_tensor(eq, eq, keypair[:, :, c].unsqueeze(2).broadcast_to(shape), ALU.mult)
                        dve.drain()
                        last = v.tensor_reduce(picks[:, c, :, cols], eq, AX.X, ALU.add)
                        dve.drain()
                    dve.sem_inc(S["ranked"], 1)

                v.tensor_copy(K.iotab[:], K.iota[:])
                dve.drain()
                for u in range(2):
                    head(0, u)
                with dve.Fori(1, HEADS // 2) as it:
                    for u in range(2):
                        head(it, u)
                dve.drain().then_inc(S["shifted"], 1)
                dve.wait_ge(S["exped"], 1)
                weights = picks[:, 2].rearrange("p t (h k) -> p t h k", k=TOPK)
                v.tensor_reduce(sums, weights, AX.X, ALU.add)
                dve.drain()
                v.reciprocal(sums, sums)
                dve.drain()
                v.tensor_tensor(weights, weights, sums.unsqueeze(3).broadcast_to([P, TT, HEADS, TOPK]),
                                ALU.mult).then_inc(S["picked"], 1)
                dve.wait_ge(S["pick_turn"], 3)
                v.tensor_copy(rest[:], ps_v[:, 2])
                dve.drain()
                for part in range(3):
                    v.tensor_copy(gate_t[:, part], rest[:])
                    dve.drain()
                    if part < 2:
                        v.tensor_tensor(rest[:], rest[:], gate_t[:, part], ALU.subtract)
                        dve.drain()
                dve.sem_inc(S["pick_turned"], 1)
                dve.wait_ge(S["pick_turned"], 3)

                def gate_quad(q, quad):
                    i_shape, j_shape = [P, BATCH, KEYS], [P, BATCH, JB]
                    for u in range(4):
                        at = bass.ds(quad * 4 * BATCH + u * BATCH, BATCH)
                        if not (isinstance(quad, int) and q == 0 and quad == 0):
                            dve.wait_ge(S["gate"], q * (T // BATCH) + quad * 4 + u - 3)
                        v.tensor_tensor(hot_i[:, u], K.iotab[:].unsqueeze(1).broadcast_to(i_shape),
                                        key_t[:, 0, at].unsqueeze(2).broadcast_to(i_shape), ALU.is_equal)
                        v.tensor_tensor(is_j[:, u], K.iotab[:, q * JB:(q + 1) * JB].unsqueeze(1).broadcast_to(j_shape),
                                        key_t[:, 1, at].unsqueeze(2).broadcast_to(j_shape), ALU.is_equal)
                        dve.drain()
                        v.tensor_tensor(hot_j[:, u], is_j[:, u].unsqueeze(1).broadcast_to([P, 3, BATCH, JB]),
                                        gate_t[:, :, at].unsqueeze(3).broadcast_to([P, 3, BATCH, JB]),
                                        ALU.mult).then_inc(S["onehot"], 1)
                        if u == 0 and not (isinstance(quad, int) and quad == 0):
                            apply(q, quad - 1, 1)
                        if u == 2:
                            apply(q, quad, 0)

                def apply(q, quad, bank):
                    dve.wait_ge(S["gate"], q * (T // BATCH) + quad * 4 + bank * 2 + 2)
                    w = wbuf[q % 2][:, :, bass.ds(quad * 2 * GB + bank * GB, GB)]
                    v.tensor_tensor(w, w, ps_g[:, bank].rearrange("p t j -> p j t"),
                                    ALU.mult).then_inc(S["gated"], 1)

                def gate_quads(q, a, b):
                    if a == 0:
                        dve.wait_ge(S["gelu"], JB * (q + 1))
                        gate_quad(q, 0)
                    with dve.Fori(max(a, 1), b) as quad:
                        gate_quad(q, quad)
                    if b == 2 * TURNS:
                        apply(q, b - 1, 1)

                def add(q, half):
                    dve.wait_ge(S["value"], (2 * q + half + 1) * JB)
                    for c in range(VB):
                        n = half * VB + c
                        v.tensor_tensor(K.h[:, n], K.h[:, n], ps_v[:, c], ALU.add).then_inc(S["added"], 1)

                gate_quads(0, 0, 2 * TURNS)
                for q in range(BLOCKS):
                    for half in range(2):
                        if q + 1 < BLOCKS:
                            gate_quads(q + 1, half * TURNS, (half + 1) * TURNS)
                        add(q, half)


class Views:
    pass


def encoder(nc, x_t, const, vec, w_in, w_rope, rope_a, rope_b, w_qup, w_kvup, s5_lam, s5_bc, s5_d, w_glu, w_out,
            w_query, sub_keys, down_t, up, p_t, w_ple, scratch, out):
    with ExitStack() as ctx:
        def sb(name, shape, dt=F32):
            return ctx.enter_context(nc.sbuf_tensor(name, shape, dt))

        K = Views()
        K.h = sb("h", [P, DT, T])
        K.xn = sb("xn", [P, DT, T])
        K.const = sb("const", [P, 5, P])
        K.ident, K.pairs, K.turn_a, K.iota = (K.const[:, n] for n in range(4))
        K.turn_b = K.const[:, 4, 0:ROPE]
        K.iotab = sb("iotab", [P, P], BF16)
        K.ones = sb("ones", [P, P])
        K.eps = sb("eps", [P, 1])
        K.vec = sb("vec", [P, NVEC])
        constants(nc, K, x_t, const)

        with nc.Fori(0, LAYERS) as l:
            with Phase(nc, "vec_load") as ph:
                s_load, = ph.sems
                with nc.Block() as block:

                    @block.sync
                    def _(sp):
                        sp.dma_start(K.vec[:], vec[l]).then_inc(s_load, 16)
                        sp.wait_ge(s_load, 16)

            def tiles(t, a, b):
                return [t[:, n] for n in range(a, b)]

            rmsnorm(nc, K, "mixn", [(tiles(K.h, 0, DT), D, K.ones, MIX, tiles(K.xn, 0, DT))])
            with ExitStack() as layer:
                def lb(name, shape):
                    return layer.enter_context(nc.sbuf_tensor(name, shape, F32))

                A = Views()
                A.mixed = lb("mixed", [P, DT, T])
                A.qka = lb("qka", [P, 3, T])
                A.va = lb("va", [P, TT, P])
                A.ql = lb("ql", [P, 2, T])
                A.kvl = lb("kvl", [P, T])
                A.kpe = lb("kpe", [P, T])
                A.up = lb("up_cols", [P, MT, T])
                in_projection(nc, K, A, l, w_in, w_rope)
                with ExitStack() as ssm:
                    def mb(name, shape):
                        return ssm.enter_context(nc.sbuf_tensor(name, shape, F32))

                    S = Views()
                    S.ug = mb("ug", [P, G, NK])
                    S.qmap = mb("qmap", [P, 2, G, Q + 2, CH])
                    S.m0 = mb("m0", [P, G, Q * CH])
                    S.s = mb("s5_s", [P, NK, 2, G])
                    S.factor = mb("factor", [P, 2, G])
                    S.outpow = mb("outpow", [P, 3, Q + 2, G])
                    S.inpow = mb("inpow", [P, 2, Q, G])
                    S.step = mb("step", [P, 2, 2, G])
                    regroup(nc, "uin", scratch, A.up, S.ug, False)
                    s5_tables(nc, S, l, s5_lam)
                    with nc.Fori(0, MT) as m:
                        s5_maps(nc, K, S, l, m, s5_bc, s5_d)
                    with nc.sbuf_tensor("s5_xq", [P, 2, G, NK], F32) as xq:
                        S.xq = xq
                        with nc.sbuf_tensor("s5_x", [P, NK, 2, G], F32) as x:
                            S.x = x
                            s5_scan(nc, S)
                        with nc.sbuf_tensor("s5_z", [P, G, NK], F32) as z:
                            s5_output(nc, S, z)
                            regroup(nc, "zout", scratch, A.up, z, True)
                s5_glu(nc, K, A, l, w_glu)
                rmsnorm(nc, K, "latn", [
                    (tiles(A.qka, 0, 1), HD, K.pairs, GQ, tiles(A.qka, 0, 1)),
                    (tiles(A.qka, 1, 2), HD, K.pairs, GQ, tiles(A.qka, 1, 2)),
                    (tiles(A.qka, 2, 3), HD, K.pairs, GK, tiles(A.qka, 2, 3)),
                    (tiles(A.ql, 0, 2), 2 * P, K.ones, MQ, tiles(A.ql, 0, 2)),
                    ([A.kvl[:]], P, K.ones, MKV, [A.kvl[:]])])
                gqa_rope(nc, K, A, rope_a)
                with nc.sbuf_tensor("qb", [P, 4, T], F32) as qb, nc.sbuf_tensor("kb", [P, 4, T], F32) as kb, \
                        nc.sbuf_tensor("vb", [P, TT, 4 * HD], F32) as vb:
                    A.qb, A.kb, A.vb = qb, kb, vb
                    mla_heads(nc, K, A, l, w_qup, w_kvup, rope_b)
                    attention(nc, K, A)
                rmsnorm(nc, K, "groupn", [(tiles(A.mixed, a, b), (b - a) * P, K.ones, GROUP + a, tiles(A.mixed, a, b))
                                          for a, b in ((0, 2), (2, 4), (4, 8))])
                mix_out(nc, K, A, l, w_out)
            rmsnorm(nc, K, "ffnn", [(tiles(K.h, 0, DT), D, K.ones, FFN, tiles(K.xn, 0, DT))])
            peer(nc, K, l, w_query, sub_keys, down_t, up)
            rmsnorm(nc, K, "plen", [(tiles(K.h, 0, DT), D, K.ones, PLE, tiles(K.xn, 0, DT))])
            ple(nc, K, l, p_t, w_ple)

        rmsnorm(nc, K, "finn", [([K.h[:, n] for n in range(DT)], D, K.ones, FIN, [K.xn[:, n] for n in range(DT)])])
        with Phase(nc, "out_store") as ph:
            s_store, = ph.sems
            with nc.Block() as block:

                @block.sync
                def _(sp):
                    sp.dma_start(out, K.xn[:]).then_inc(s_store, 16)
                    sp.wait_ge(s_store, 16)


def rope_table(n, dim):
    half = dim // 2
    t = np.arange(n)
    freqs = (np.float32(10000.0) ** (-np.arange(0, half, 2, dtype=np.float32) / np.float32(half))).astype(np.float32)
    r, c = (t // 64).astype(np.float32), (t % 64).astype(np.float32)
    ang = np.concatenate([r[:, None] * freqs, c[:, None] * freqs], axis=-1).astype(np.float32)
    return np.cos(ang).T, np.sin(ang).T


def shape_constants():
    const = np.zeros((P, 5, P), np.float32)
    const[:, 0] = np.eye(P)
    const[:, 1] = np.kron(np.eye(2), np.ones((HD, HD)))
    const[:, 3] = np.arange(P)

    def turn(dim):
        m = np.zeros((dim, dim), np.float32)
        h = dim // 2
        m[np.arange(h) + h, np.arange(h)] = -1.0
        m[np.arange(h), np.arange(h) + h] = 1.0
        return m

    const[:, 2] = np.kron(np.eye(2), turn(HD))
    const[HD:MD, 4, 0:ROPE] = turn(ROPE)
    ca, sa = rope_table(T, HD)
    cb, sb = rope_table(T, ROPE)
    rope_a = np.stack([np.tile(ca, (4, 1)), np.tile(sa, (4, 1))], 1).astype(np.float32)
    rope_b = np.stack([np.tile(cb, (2, 1)), np.tile(sb, (2, 1))], 1).astype(np.float32)
    return const, np.ascontiguousarray(rope_a), np.ascontiguousarray(rope_b)


def lay_out(i):
    L = LAYERS
    c = np.ascontiguousarray
    const, rope_a, rope_b = shape_constants()

    def cols(a, n):
        return np.asarray(a).reshape(L, n, P).transpose(0, 2, 1)

    def tiled(a, rows, width=P):
        return a.reshape(L, rows, P, -1, width).transpose(0, 3, 2, 1, 4)

    vec = np.concatenate([
        cols(i["mix_norm"], DT), cols(np.tile(i["gqa_q_norm"], (1, 2)), 1), cols(np.tile(i["gqa_k_norm"], (1, 2)), 1),
        cols(i["mla_q_norm"], 2), cols(i["mla_kv_norm"], 1), cols(i["group_out_norm"], DT), cols(i["ffn_norm"], DT),
        cols(i["ple_norm"], DT), cols(np.tile(i["final_norm"], (L, 1)), DT), cols(i["b_glu"], MT)], axis=2)
    w = i["w_in"]
    qa, ka, va, ql, kvl, kr, u = np.split(w, np.cumsum([256, 128, 128, 256, 128, 32]), axis=2)
    qa = qa.reshape(L, D, 2, 2, HD).transpose(0, 1, 3, 2, 4).reshape(L, D, 256)
    w_in = tiled(np.concatenate([qa, ka, ql, kvl, u, va], axis=2), DT)
    w_rope = tiled(kr, DT, ROPE)[:, 0]
    w_qup = i["w_mla_q_up"].reshape(L, 2, P, 4 * MD).transpose(0, 2, 1, 3)
    w_kvup = i["w_mla_kv_up"].reshape(L, P, 4, 2, HD)

    def states(a):
        return a.transpose(0, 1, 3, 2).reshape(L, P, G)

    ldt = np.broadcast_to(i["s5_log_dt"][:, :, :, None], (L, 2, G, ST))
    s5_lam = np.stack([states(i["s5_a_re"]), states(i["s5_a_im"]), states(ldt)], axis=2)
    b = [i[n].transpose(0, 1, 3, 2, 4).reshape(L, P, MT, GM, CH) for n in ("s5_b_re", "s5_b_im")]
    cc = [i[n].transpose(0, 1, 4, 2, 3).reshape(L, P, MT, GM, CH) for n in ("s5_c_re", "s5_c_im")]
    s5_bc = np.stack(b + cc, axis=2).transpose(0, 3, 1, 2, 4, 5)
    s5_d = i["s5_d"].reshape(L, MT, GM, CH).transpose(0, 1, 3, 2)
    w_query = tiled(i["w_peer_query"], DT, 256)
    sub_keys = i["peer_sub_keys"].transpose(0, 3, 1, 2)
    down_t = i["peer_down"].reshape(L, KEYS, KEYS, DT, P).transpose(0, 2, 4, 3, 1)
    up = i["peer_up"].reshape(L, KEYS, KEYS, 2, D // 2).transpose(0, 2, 3, 1, 4)
    w_ple = np.concatenate([tiled(i["w_ple_gate"], DT), tiled(i["w_ple_proj"], 2)], axis=3)
    return [c(a) for a in (
        i["x"][0].reshape(T, DT, P).transpose(2, 1, 0), const, vec, w_in, w_rope, rope_a, rope_b, w_qup, w_kvup,
        s5_lam, s5_bc, s5_d, tiled(i["w_glu"], MT), tiled(i["w_out"], DT), w_query, sub_keys, down_t, up,
        i["p"][:, 0].reshape(L, T, 2, P).transpose(0, 3, 2, 1), w_ple)]


_NAMES = ["x_t", "const", "vec", "w_in", "w_rope", "rope_a", "rope_b", "w_qup", "w_kvup", "s5_lam", "s5_bc", "s5_d",
          "w_glu", "w_out", "w_query", "sub_keys", "down_t", "up", "p_t", "w_ple"]


def kernel(**inputs):
    import concourse.bacc as _bacc
    from concourse import mybir as _mybir
    from concourse.bass_utils import run_bass_kernel_spmd as _run

    nc = _bacc.Bacc("TRN2", target_bir_lowering=False, num_devices=1)
    arrays, args = {}, []
    for name, a in zip(_NAMES, lay_out({k: np.asarray(v) for k, v in inputs.items()})):
        arrays[f"in_{name}"] = a
        args.append(nc.dram_tensor(f"in_{name}", a.shape, _mybir.dt.from_np(a.dtype), kind="ExternalInput").ap())
    scratch = nc.dram_tensor("s5_scratch", (G * CH, Q, NK), F32, kind="Internal").ap()
    out = nc.dram_tensor("out_0_dram", (P, DT, T), F32, kind="ExternalOutput").ap()
    encoder(nc, *args, scratch, out)
    r = _run(nc, [arrays], core_ids=[0])
    got = r.results[0]["out_0_dram"]
    return np.ascontiguousarray(got.transpose(2, 1, 0).reshape(1, T, D))
```

```python
from contextlib import ExitStack

import numpy as np

import concourse.bass as bass
from concourse import mybir

F32 = mybir.dt.float32
F32R = mybir.dt.float32r
BF16 = mybir.dt.bfloat16
U32 = mybir.dt.uint32
ALU = mybir.AluOpType
ACT = mybir.ActivationFunctionType
AX = mybir.AxisListType

P = 128
LAYERS = 2
T = 512
TT = T // P
D = 1024
DT = D // P
EPS = 1e-6
HD = 64
ROPE = 32
MD = HD + ROPE
G, CH, ST = 32, 16, 64
Q = 8
NK = T // Q
MT = G * CH // P
GM = G // MT
SPAN = 8
SPANS = NK // SPAN
KEYS = 128
HEADS, TOPK = 8, 16
BLOCKS = 4
JB = KEYS // BLOCKS
BATCH = 8

MIX, GQ, GK, MQ, MKV, GROUP, FFN, PLE, FIN, BGLU, NVEC = 0, 8, 9, 10, 12, 13, 21, 29, 37, 45, 49
T_QA, T_KA, T_QL, T_KVL, T_U, T_VA, T_KR = 0, 2, 3, 5, 6, 10, 11
N_IN = 12

MAGIC = 12582912.0
TWO_PI = (6.28125, 0.0019350051879882812, 3.019916050561733e-07)
PI_SAFE = 3.1415925


class Phase:

    def __init__(self, nc, *names):
        self.nc, self.names = nc, names

    def __enter__(self):
        self.stack = ExitStack()
        self.sems = [self.stack.enter_context(self.nc.semaphore(n)) for n in self.names]
        return self

    def sb(self, name, shape, dt=F32):
        return self.stack.enter_context(self.nc.sbuf_tensor(name, shape, dt))

    def psum(self, name, shape):
        return self.stack.enter_context(self.nc.psum_tensor(name, shape, F32))

    def __exit__(self, *exc):
        if exc[0] is None:
            nc = self.nc
            nc.all_engine_barrier()
            for s in self.sems:
                nc.gpsimd.sem_clear(s)
            nc.all_engine_barrier()
        return self.stack.__exit__(*exc)


def linear(nc, name, tiles, k, width, weight, products, act_step=None, dve_step=None, banks=1):
    ring = 3
    with Phase(nc, *[f"{name}_weight{r}" for r in range(ring)], f"{name}_product", f"{name}_act",
               f"{name}_dve") as ph:
        *s_weight, s_product, s_act, s_dve = ph.sems
        w = ph.sb(f"{name}_w", [P, ring, k, width])
        ps = ph.psum(f"{name}_ps", [P, 2, banks, T])
        s_free = s_dve if dve_step else s_act
        with nc.Block() as block:

            @block.sync
            def _(sp):
                for i in range(tiles):
                    if i >= ring:
                        sp.wait_ge(s_product, i - ring + 1)
                    sp.dma_start(w[:, i % ring], weight(i)).then_inc(s_weight[i % ring], 16)

            @block.tensor
            def _(pe):
                for i in range(tiles):
                    pe.wait_ge(s_weight[i % ring], 16 * (i // ring + 1))
                    if i >= 2:
                        pe.wait_ge(s_free, i - 1)
                    products(i, ps[:, i % 2], w[:, i % ring]).then_inc(s_product, 1)

            @block.scalar
            def _(act):
                for i in range(tiles if act_step else 0):
                    act.wait_ge(s_product, i + 1)
                    if dve_step and i >= 2:
                        act.wait_ge(s_dve, i - 1)
                    act_step(act, i, ps[:, i % 2]).then_inc(s_act, 1)

            @block.vector
            def _(dve):
                for i in range(tiles if dve_step else 0):
                    if act_step:
                        dve.wait_ge(s_act, i + 1)
                    else:
                        dve.wait_ge(s_product, i + 1)
                    dve_step(dve, i, ps[:, i % 2]).then_inc(s_dve, 1)


def split_products(out, weights, acts, first, last, **kw):
    def go(nc):
        nc.tensor.matmul(out, weights[0], acts[0], start=first, stop=False, **kw)
        nc.tensor.matmul(out, weights[0], acts[1], start=False, stop=False, **kw)
        return nc.tensor.matmul(out, weights[1], acts[0], start=False, stop=last, **kw)
    return go


def split_linear(nc, name, tiles, k, weight, products, act_step=None, dve_step=None, banks=1):
    ring = 3
    with Phase(nc, *[f"{name}_weight{r}" for r in range(ring)], f"{name}_high", f"{name}_low",
               f"{name}_product", f"{name}_act", f"{name}_dve") as ph:
        *s_weight, s_high, s_low, s_product, s_act, s_dve = ph.sems
        w = ph.sb(f"{name}_w", [P, ring, k, P])
        high = ph.sb(f"{name}_wh", [P, 2, k, P], F32R)
        low = ph.sb(f"{name}_wl", [P, 2, k, P], F32R)
        ps = ph.psum(f"{name}_ps", [P, 2, banks, T])
        s_free = s_dve if dve_step else s_act

        def flat(t):
            return t.rearrange("p k c -> p (k c)")

        with nc.Block() as block:

            @block.sync
            def _(sp):
                for i in range(tiles):
                    if i >= ring:
                        sp.wait_ge(s_low, i - ring + 1)
                    sp.dma_start(w[:, i % ring], weight(i)).then_inc(s_weight[i % ring], 16)

            @block.gpsimd
            def _(pool):
                for i in range(tiles):
                    pool.wait_ge(s_high, i + 1)
                    nc.gpsimd.tensor_tensor(flat(low[:, i % 2]), flat(w[:, i % ring]),
                                            flat(high[:, i % 2].bitcast(F32)), ALU.subtract).then_inc(s_low, 1)

            @block.tensor
            def _(pe):
                for i in range(tiles):
                    pe.wait_ge(s_low, i + 1)
                    if i >= 2:
                        pe.wait_ge(s_free, i - 1)
                    products(i, ps[:, i % 2], (high[:, i % 2], low[:, i % 2])).then_inc(s_product, 1)

            @block.scalar
            def _(act):
                for i in range(tiles + 1):
                    if i < tiles:
                        act.wait_ge(s_weight[i % ring], 16 * (i // ring + 1))
                        if i >= 2:
                            act.wait_ge(s_product, i - 1)
                        nc.scalar.copy(flat(high[:, i % 2]), flat(w[:, i % ring])).then_inc(s_high, 1)
                    if i >= 1 and act_step:
                        act.wait_ge(s_product, i)
                        if dve_step and i >= 3:
                            act.wait_ge(s_dve, i - 2)
                        act_step(act, i - 1, ps[:, (i - 1) % 2]).then_inc(s_act, 1)

            @block.vector
            def _(dve):
                for i in range(tiles if dve_step else 0):
                    if act_step:
                        dve.wait_ge(s_act, i + 1)
                    else:
                        dve.wait_ge(s_product, i + 1)
                    dve_step(dve, i, ps[:, i % 2]).then_inc(s_dve, 1)


def rmsnorm(nc, K, name, groups):
    n = max(len(g[0]) for g in groups)
    with Phase(nc, f"{name}_square", f"{name}_sum", f"{name}_root", f"{name}_out",
               f"{name}_tile", f"{name}_high", f"{name}_low") as ph:
        s_square, s_sum, s_root, s_out, s_tile, s_high, s_low = ph.sems
        split = isinstance(groups[0][4][0], tuple)
        sq = ph.sb(f"{name}_sq", [P, n, T])
        root = ph.sb(f"{name}_rt", [P, T])
        inv = ph.sb(f"{name}_inv", [P, T])
        ps = ph.psum(f"{name}_ps", [P, 2, T])
        first = [sum(len(g[0]) for g in groups[:i]) for i in range(len(groups))]
        with nc.Block() as block:

            @block.scalar
            def _(act):
                for i, (src, mean, _, _, _) in enumerate(groups):
                    if i:
                        act.wait_ge(s_sum, i)
                        act.wait_ge(s_out, i)
                        if split:
                            act.wait_ge(s_low, first[i])
                    for j, tile in enumerate(src):
                        nc.scalar.activation(sq[:, j], tile, ACT.Square).then_inc(s_square, 1)
                    act.wait_ge(s_sum, i + 1)
                    nc.scalar.activation(root[:], ps[:, i % 2], ACT.Sqrt, bias=K.eps[:, 0:1],
                                         scale=1.0 / mean).then_inc(s_root, 1)
                    for j in range(len(src) if split else 0):
                        act.wait_ge(s_tile, first[i] + j + 1)
                        nc.scalar.copy(groups[i][4][j][0], sq[:, j]).then_inc(s_high, 1)

            @block.gpsimd
            def _(pool):
                for i, (src, _, _, _, dst) in enumerate(groups if split else ()):
                    for j in range(len(src)):
                        pool.wait_ge(s_high, first[i] + j + 1)
                        nc.gpsimd.tensor_tensor(dst[j][1], sq[:, j], dst[j][0].bitcast(F32),
                                                ALU.subtract).then_inc(s_low, 1)

            @block.tensor
            def _(pe):
                for i, (src, _, ones, _, _) in enumerate(groups):
                    for j in range(len(src)):
                        pe.wait_ge(s_square, first[i] + j + 1)
                        last = nc.tensor.matmul(ps[:, i % 2], ones[:], sq[:, j], start=(j == 0),
                                                stop=(j == len(src) - 1))
                    last.then_inc(s_sum, 1)

            @block.vector
            def _(dve):
                for i, (src, _, _, gain, dst) in enumerate(groups):
                    dve.wait_ge(s_root, i + 1)
                    nc.vector.reciprocal(inv[:], root[:])
                    dve.drain()
                    for j, tile in enumerate(src):
                        last = nc.vector.scalar_tensor_tensor(
                            out=sq[:, j] if split else dst[j], in0=tile, scalar=K.vec[:, gain + j:gain + j + 1],
                            in1=inv[:], op0=ALU.mult, op1=ALU.mult)
                        if split and j < len(src) - 1:
                            last.then_inc(s_tile, 1)
                    if split:
                        last.then_inc(s_tile, 1)
                        dve.drain().then_inc(s_out, 1)
                    else:
                        last.then_inc(s_out, 1)
                        dve.drain()


def constants(nc, K, x_t, const):
    with Phase(nc, "start_load", "start_fill") as ph:
        s_load, s_fill = ph.sems
        with nc.Block() as block:

            @block.sync
            def _(sp):
                sp.dma_start(K.h[:], x_t).then_inc(s_load, 16)
                sp.dma_start(K.const[:], const).then_inc(s_load, 16)
                sp.wait_ge(s_load, 32)

            @block.gpsimd
            def _(pool):
                nc.gpsimd.memset(K.ones[:], 1.0).then_inc(s_fill, 1)
                nc.gpsimd.memset(K.eps[:], EPS).then_inc(s_fill, 1)


def in_projection(nc, K, A, l, w_in):
    def products(i, ps, w):
        for tt in range(TT if i == T_VA else 1):
            for k in range(DT):
                tile = tuple(x[:, k] for x in w)
                if i != T_VA:
                    last = split_products(ps[:, 0], tile, (K.xh[:, k], K.xl[:, k]), k == 0, k == DT - 1)(nc)
                else:
                    cols = slice(tt * P, (tt + 1) * P)
                    last = split_products(ps[:, 0, cols], (K.xh[:, k, cols], K.xl[:, k, cols]), tile, k == 0,
                                          k == DT - 1)(nc)
        return last

    def out(act, i, ps):
        if T_U <= i < T_VA:
            return nc.scalar.copy(A.up[:, i - T_U].rearrange("p (q k) -> p q k", q=Q),
                                  ps[:, 0].rearrange("p (k q) -> p q k", q=Q))
        if i == T_KR:
            return nc.scalar.copy(A.kpe[HD:MD, :], ps[HD:MD, 0])
        dst = (A.va[:].rearrange("p a b -> p (a b)") if i == T_VA else A.kvl[:] if i == T_KVL
               else A.ql[:, i - T_QL] if i >= T_QL else A.qka[:, i])
        return nc.scalar.copy(dst, ps[:, 0])

    split_linear(nc, "inproj", N_IN, DT, lambda i: w_in[l, i], products, act_step=out)


def regroup(nc, name, scratch, chans, places):
    by_chan = scratch.rearrange("(m p) q k -> p m (q k)", p=P)
    by_place = scratch.rearrange("(g c) q k -> q c g k", c=CH)
    with Phase(nc, f"{name}_stored", f"{name}_loaded") as ph:
        s_stored, s_loaded = ph.sems
        with nc.Block() as block:

            @block.sync
            def _(sp):
                for q in range(Q):
                    sp.dma_start(by_place[q], places[q * CH:(q + 1) * CH]).then_inc(s_stored, 16)
                sp.wait_ge(s_stored, 16 * Q)
                sp.dma_start(chans[:], by_chan).then_inc(s_loaded, 16)
                sp.wait_ge(s_loaded, 16)


def cmul(eng, out_r, out_i, a, b, tmp_r, tmp_i):
    eng.tensor_tensor(out_r, a[0], b[0], ALU.mult)
    eng.tensor_tensor(tmp_r, a[1], b[1], ALU.mult)
    eng.tensor_tensor(out_i, a[0], b[1], ALU.mult)
    eng.tensor_tensor(tmp_i, a[1], b[0], ALU.mult)
    eng.drain()
    eng.tensor_tensor(out_r, out_r, tmp_r, ALU.subtract)
    return eng.tensor_tensor(out_i, out_i, tmp_i, ALU.add)


def s5_states(nc, K, A, S, l, s5_lam, s5_bc, s5_d, scratch):
    H = ST
    by_chan = scratch.rearrange("(m p) q k -> p m (q k)", p=P)
    by_place = scratch.rearrange("(g c) q k -> q c g k", c=CH)
    with Phase(nc, "s5_stored", "s5_u_loaded", "s5_lam_loaded", "s5_bc_loaded", "s5_d_loaded", "s5_act", "s5_dve",
               "s5_tables", "s5_p1", "s5_turn", "s5_turned", "s5_s", "s5_s_out", "s5_q", "s5_k", "s5_k_out",
               "s5_full", "s5_m0_even", "s5_m0_odd") as ph:
        (s_stored, s_u, s_lam, s_bc, s_d, s_act, s_dve, s_tables, s_p1, s_turn, s_turned, s_s, s_s_out, s_q, s_k,
         s_k_out, s_full, *s_m0) = ph.sems
        lam = ph.sb("lam", [P, 3, G])
        t = ph.sb("lam_t", [P, 8, G])
        power = ph.sb("lam_power", [P, 2, Q + 1, G])
        factor = ph.sb("factor", [P, 2, G])
        outpow = ph.sb("outpow", [P, 3, Q + 2, G])
        inpow = ph.sb("inpow", [P, 2, Q, G])
        leap = ph.sb("leap", [P, 2, SPAN + 1, 2, G])
        bc = ph.sb("bc", [P, 4, G, CH])
        dd = ph.sb("dd", [CH, G])
        bbar = ph.sb("bbar", [P, 2, G, CH])
        p1 = ph.sb("p1", [P, 2, GM, Q, CH])
        qtmp = ph.sb("qtmp", [P, GM, Q + 2, CH])
        work = ph.sb("s5_work", [P, 2 * GM * Q * CH])
        full = ph.sb("full", [CH, 2, GM, 2 * Q - 1, CH])
        near = ph.sb("near", [CH, 2, GM, CH])
        diag = ph.sb("diag", [CH, GM, CH])
        s = ph.sb("s5_s", [P, NK, 2, G])
        x = ph.sb("s5_x", [P, NK, 2, G])
        ps_t = ph.psum("ps_t", [P, 2, 4, P])
        ps_k = ph.psum("ps_k", [P, 2, GM, P])
        ps_s = ph.psum("ps_s", [P, 2, GM, NK])
        p1t = A.up[:].rearrange("p m t -> p (m t)").rearrange("p (n s) -> p n s", s=P)
        big = work[:, 0:8 * G].rearrange("p (r n g) -> p r n g", r=2, g=G)
        btmp = work[:, 0:2 * GM * CH].rearrange("p (r g c) -> p r g c", r=2, c=CH)
        ptmp = work[:].rearrange("p (r g q c) -> p r g q c", r=2, g=GM, c=CH)
        scan = work[:].rearrange("p (n b r g) -> p n b r g", n=4, b=SPANS, r=2)
        turns = 2 * GM // 4
        tile_of = [slice(m * GM, (m + 1) * GM) for m in range(MT)]
        with nc.Block() as block:

            @block.sync
            def _(sp):
                sp.dma_start(lam[:], s5_lam[l]).then_inc(s_lam, 16)
                sp.dma_start(by_chan, A.up[:]).then_inc(s_stored, 16)
                sp.dma_start(bc[:], s5_bc[l]).then_inc(s_bc, 16)
                sp.dma_start(dd[:], s5_d[l]).then_inc(s_d, 16)
                sp.wait_ge(s_stored, 16)
                for q in range(Q):
                    sp.dma_start(S.ug[q * CH:(q + 1) * CH], by_place[q]).then_inc(s_u, 16)
                for m in range(MT):
                    sp.wait_ge(s_full, m + 1)
                    for q in range(Q):
                        sp.dma_start(S.m0[q * CH:(q + 1) * CH, tile_of[m], :],
                                     full[:, m % 2, :, Q - 1 - q:2 * Q - 1 - q].rearrange("c g t d -> c g (t d)")
                                     ).then_inc(s_m0[m % 2], 16)
                for slot in range(2):
                    sp.wait_ge(s_m0[slot], 16 * Q * MT // 2)

            @block.vector
            def _(dve):
                v = nc.vector
                dve.wait_ge(s_act, 1)
                v.tensor_tensor(t[:, 1], lam[:, 0], t[:, 0], ALU.mult).then_inc(s_dve, 1)
                v.tensor_tensor(t[:, 2], lam[:, 1], t[:, 0], ALU.mult)
                dve.drain()
                v.tensor_scalar(t[:, 4], t[:, 2], 1.0 / (2.0 * float(np.pi)), MAGIC, ALU.mult, ALU.add)
                dve.drain()
                v.tensor_scalar(t[:, 4], t[:, 4], MAGIC, None, ALU.subtract)
                dve.drain()
                for part in TWO_PI:
                    v.scalar_tensor_tensor(out=t[:, 2], in0=t[:, 4], scalar=-part, in1=t[:, 2],
                                           op0=ALU.mult, op1=ALU.add)
                    dve.drain()
                v.tensor_scalar(t[:, 4], t[:, 2], PI_SAFE, -PI_SAFE, ALU.min, ALU.max)
                dve.drain()
                v.tensor_scalar(t[:, 5], t[:, 4], -1.0, None, ALU.mult)
                dve.drain()
                v.tensor_tensor(t[:, 5], t[:, 5], t[:, 4], ALU.max)
                dve.drain()
                v.tensor_scalar(t[:, 5], t[:, 5], -1.0, float(np.pi) / 2, ALU.mult, ALU.add).then_inc(s_dve, 1)
                dve.wait_ge(s_act, 4)
                v.memset(power[:, 0, 0], 1.0)
                v.memset(power[:, 1, 0], 0.0)
                v.tensor_tensor(power[:, 0, 1], t[:, 3], t[:, 7], ALU.mult)
                v.tensor_tensor(power[:, 1, 1], t[:, 3], t[:, 6], ALU.mult)
                dve.drain()
                for lo, n in ((1, 1), (2, 2), (4, 4)):
                    a = [power[:, r, 1:1 + n] for r in range(2)]
                    b = [power[:, r, lo:lo + 1].broadcast_to([P, n, G]) for r in range(2)]
                    cmul(v, power[:, 0, lo + 1:lo + 1 + n], power[:, 1, lo + 1:lo + 1 + n], a, b,
                         big[:, 0, 0:n], big[:, 1, 0:n])
                    dve.drain()
                v.tensor_scalar(t[:, 0], power[:, 0, 1], -1.0, None, ALU.add)
                v.tensor_tensor(t[:, 1], lam[:, 0], lam[:, 0], ALU.mult)
                v.tensor_tensor(t[:, 2], lam[:, 1], lam[:, 1], ALU.mult)
                v.tensor_scalar(t[:, 3], lam[:, 1], -1.0, None, ALU.mult)
                dve.drain()
                v.tensor_tensor(t[:, 1], t[:, 1], t[:, 2], ALU.add)
                cmul(v, t[:, 4], t[:, 5], (t[:, 0], power[:, 1, 1]), (lam[:, 0], t[:, 3]), t[:, 6], t[:, 7])
                dve.drain()
                v.reciprocal(t[:, 2], t[:, 1])
                dve.drain()
                v.tensor_tensor(factor[:, 0], t[:, 4], t[:, 2], ALU.mult)
                v.tensor_tensor(factor[:, 1], t[:, 5], t[:, 2], ALU.mult)
                v.memset(outpow[:], 0.0)
                dve.drain()
                for r in range(2):
                    v.tensor_copy(outpow[0:H, r, 0:Q + 1], power[0:H, r])
                    v.tensor_copy(outpow[H:P, r, 1:Q + 2], power[H:P, r, ::-1])
                    v.tensor_copy(inpow[0:H, r], power[0:H, r, 0:Q][:, ::-1])
                    v.tensor_copy(inpow[H:P, r], power[H:P, r, 0:Q])
                dve.drain()
                v.tensor_scalar(outpow[:, 2], outpow[:, 1], -1.0, None, ALU.mult)
                dve.drain().then_inc(s_tables, 1)
                dve.wait_ge(s_bc, 16)
                f = [factor[:, r].unsqueeze(2).broadcast_to([P, G, CH]) for r in range(2)]
                cmul(v, bbar[:, 0], bbar[:, 1], f, (bc[:, 0], bc[:, 1]), p1[:, 0, 0:4].rearrange(
                    "p g q c -> p (g q) c"), p1[:, 1, 0:4].rearrange("p g q c -> p (g q) c"))
                dve.drain()
                shape = [P, GM, Q, CH]
                for m in range(MT):
                    pw = [inpow[:, r, :, tile_of[m]].rearrange("p q g -> p g q").unsqueeze(3).broadcast_to(shape)
                          for r in range(2)]
                    bb = [bbar[:, r, tile_of[m]].unsqueeze(2).broadcast_to(shape) for r in range(2)]
                    if m:
                        dve.wait_ge(s_turn, turns * m)
                    cmul(v, p1[:, 0], p1[:, 1], pw, bb, ptmp[:, 0], ptmp[:, 1]).then_inc(s_p1, 1)
                    dve.drain()
                for r in range(2):
                    v.tensor_copy(leap[:, 0, 1, r], power[:, 0, Q])
                    v.tensor_copy(leap[:, 1, 1, r], power[:, 1, Q])
                    v.memset(leap[:, 0, 0, r], 1.0)
                    v.memset(leap[:, 1, 0, r], 0.0)
                dve.drain()
                for lo, n in ((1, 1), (2, 2), (4, 4)):
                    a = [leap[:, r, 1:1 + n, 0] for r in range(2)]
                    b = [leap[:, r, lo:lo + 1, 0].broadcast_to([P, n, G]) for r in range(2)]
                    cmul(v, leap[:, 0, lo + 1:lo + 1 + n, 0], leap[:, 1, lo + 1:lo + 1 + n, 0], a, b,
                         big[:, 0, 0:n], big[:, 1, 0:n])
                    dve.drain()
                for r in range(2):
                    v.tensor_copy(leap[:, r, 2:, 1], leap[:, r, 2:, 0])
                dve.drain()
                v.tensor_scalar(leap[:, 1, :, 0], leap[:, 1, :, 0], -1.0, None, ALU.mult)
                dve.drain()

                def step(out, state, power_n, add):
                    shape = [P, state.shape[1], 2, G]
                    tmp = scan[:, 0:2, 0:shape[1]]
                    v.tensor_tensor(tmp[:, 0], leap[:, 0, power_n].unsqueeze(1).broadcast_to(shape), state, ALU.mult)
                    v.tensor_tensor(tmp[:, 1], leap[:, 1, power_n].unsqueeze(1).broadcast_to(shape),
                                    state[:, :, ::-1], ALU.mult)
                    dve.drain()
                    v.tensor_tensor(tmp[:, 0], tmp[:, 0], add, ALU.add)
                    dve.drain()
                    v.tensor_tensor(out, tmp[:, 0], tmp[:, 1], ALU.add)
                    dve.drain()

                dve.wait_ge(s_s_out, 4 * MT)
                xs = x[:].rearrange("p (b i) r g -> p b i r g", i=SPAN)
                ss = s[:].rearrange("p (b i) r g -> p b i r g", i=SPAN)
                end, enter = scan[:, 2], scan[:, 3]
                v.memset(xs[:, :, 0], 0.0)
                v.tensor_copy(xs[:, :, 1], ss[:, :, 0])
                v.memset(enter[:, 0:1], 0.0)
                dve.drain()
                for i in range(1, SPAN):
                    step(xs[:, :, i + 1] if i < SPAN - 1 else end, xs[:, :, i], 1, ss[:, :, i])
                v.tensor_copy(enter[:, 1:2], end[:, 0:1])
                dve.drain()
                for b in range(1, SPANS - 1):
                    step(enter[:, b + 1:b + 2], enter[:, b:b + 1], SPAN, end[:, b:b + 1])
                swapped = scan[:, 0]
                v.tensor_copy(swapped, enter[:, :, ::-1])
                dve.drain()
                sf = s[:].rearrange("p k r g -> p k (r g)")
                mf = S.xq[:].rearrange("p r g k -> p (r g k)").rearrange("p (k n) -> p k n", k=NK)
                for out, plane, state in ((sf, 0, enter), (mf, 1, swapped)):
                    v.tensor_tensor(
                        out.rearrange("p (b i) n -> p b i n", i=SPAN),
                        leap[:, plane, 0:SPAN].rearrange("p i r g -> p i (r g)").unsqueeze(1)
                        .broadcast_to([P, SPANS, SPAN, 2 * G]),
                        state.rearrange("p b r g -> p b (r g)").unsqueeze(2)
                        .broadcast_to([P, SPANS, SPAN, 2 * G]), ALU.mult)
                dve.drain()
                v.tensor_tensor(sf, sf, mf, ALU.add)
                dve.drain()
                for lo, order in ((0, 1), (H, -1)):
                    v.tensor_tensor(S.xq[lo:lo + H].rearrange("p r g k -> p k (r g)")[:, ::order],
                                    s[lo:lo + H].rearrange("p k r g -> p k (r g)"),
                                    x[lo:lo + H].rearrange("p k r g -> p k (r g)"), ALU.add)

            @block.gpsimd
            def _(pool):
                g = nc.gpsimd
                pool.wait_ge(s_bc, 16)
                pool.wait_ge(s_tables, 1)
                shape = [P, GM, Q + 2, CH]
                for m in range(MT):
                    c = [bc[:, 2 + r, tile_of[m]].unsqueeze(2).broadcast_to(shape) for r in range(2)]
                    pw = [outpow[:, r, :, tile_of[m]].rearrange("p q g -> p g q").unsqueeze(3).broadcast_to(shape)
                          for r in range(3)]
                    q_re, q_im = (S.qmap[:, r, tile_of[m]] for r in range(2))
                    g.tensor_tensor(q_re, c[0], pw[0], ALU.mult)
                    g.tensor_tensor(qtmp[:], c[1], pw[2], ALU.mult)
                    g.tensor_tensor(q_im, c[0], pw[2], ALU.mult)
                    pool.drain()
                    g.tensor_tensor(q_re, q_re, qtmp[:], ALU.add)
                    pool.drain()
                    g.tensor_tensor(qtmp[:], c[1], pw[0], ALU.mult)
                    pool.drain()
                    g.tensor_tensor(q_im, q_im, qtmp[:], ALU.subtract).then_inc(s_q, 1)
                    pool.drain()
                pool.wait_ge(s_d, 16)
                for m in range(MT):
                    g.tensor_tensor(diag[:], K.ident[0:CH, 0:CH].unsqueeze(1).broadcast_to([CH, GM, CH]),
                                    dd[:, tile_of[m]].unsqueeze(2).broadcast_to([CH, GM, CH]), ALU.mult)
                    pool.wait_ge(s_k_out, 2 * (m + 1))
                    mid = full[:, m % 2, :, Q - 1]
                    g.tensor_tensor(mid, mid, near[:, m % 2], ALU.add)
                    pool.drain()
                    g.tensor_tensor(mid, mid, diag[:], ALU.add).then_inc(s_full, 1)
                    pool.drain()

            @block.tensor
            def _(pe):
                for m in range(MT):
                    pe.wait_ge(s_p1, m + 1)
                    for n in range(turns):
                        if m or n >= 2:
                            pe.wait_ge(s_turned, turns * m + n - 1)
                        for u in range(4):
                            r, g = divmod(4 * n + u, GM)
                            last = nc.tensor.transpose(ps_t[:, n % 2, u], p1[:, r, g].rearrange("p q c -> p (q c)"),
                                                       K.ident[:])
                        last.then_inc(s_turn, 1)
                    if m == 0:
                        pe.wait_ge(s_u, 16 * Q)
                    pe.wait_ge(s_turned, turns * (m + 1))
                    if m:
                        pe.wait_ge(s_s_out, 4 * m)
                    for r in range(2):
                        for g in range(GM):
                            last = nc.tensor.matmul(ps_s[:, r, g], p1t[:, r * GM + g], S.ug[:, m * GM + g],
                                                    start=True, stop=True)
                    last.then_inc(s_s, 1)
                for m in range(MT):
                    pe.wait_ge(s_q, m + 1)
                    for back in range(2):
                        if m:
                            pe.wait_ge(s_k_out, 2 * m - 1 + back)
                        lo = back * ST
                        for g in range(GM):
                            for r in range(2):
                                rhs = S.qmap[lo:lo + ST, r, m * GM + g, 2 * back:2 * back + Q]
                                last = nc.tensor.matmul(ps_k[0:CH, back, g], bbar[lo:lo + ST, r, m * GM + g],
                                                        rhs.rearrange("p s c -> p (s c)"),
                                                        start=(r == 0), stop=(r == 1))
                        last.then_inc(s_k, 1)

            @block.scalar
            def _(act):
                act.wait_ge(s_lam, 16)
                nc.scalar.activation(t[:, 0], lam[:, 2], ACT.Exp).then_inc(s_act, 1)
                act.wait_ge(s_dve, 1)
                nc.scalar.activation(t[:, 3], t[:, 1], ACT.Exp).then_inc(s_act, 1)
                act.wait_ge(s_dve, 2)
                nc.scalar.activation(t[:, 6], t[:, 4], ACT.Sin).then_inc(s_act, 1)
                nc.scalar.activation(t[:, 7], t[:, 5], ACT.Sin).then_inc(s_act, 1)
                act.wait_ge(s_stored, 16)
                for m in range(MT):
                    for n in range(turns):
                        act.wait_ge(s_turn, turns * m + n + 1)
                        if m and n == 0:
                            act.wait_ge(s_s, m)
                        nc.scalar.copy(p1t[:, 4 * n:4 * n + 4], ps_t[:, n % 2]).then_inc(s_turned, 1)
                    act.wait_ge(s_s, m + 1)
                    for r in range(2):
                        for lo, order in ((0, 1), (H, -1)):
                            nc.scalar.copy(s[lo:lo + H, :, r, tile_of[m]].rearrange("p k g -> p g k"),
                                           ps_s[lo:lo + H, r][:, :, ::order]).then_inc(s_s_out, 1)
                kf, kb = (ps_k[0:CH, back].rearrange("c g (t d) -> c g t d", d=CH) for back in range(2))
                for m in range(MT):
                    if m >= 2:
                        act.wait_ge(s_m0[m % 2], 16 * Q * (m // 2))
                    act.wait_ge(s_k, 2 * m + 1)
                    nc.scalar.copy(near[:, m % 2], kf[:, :, 0])
                    nc.scalar.copy(full[:, m % 2, :, Q:2 * Q - 1], kf[:, :, 1:Q]).then_inc(s_k_out, 1)
                    act.wait_ge(s_k, 2 * m + 2)
                    nc.scalar.copy(full[:, m % 2, :, 0:Q], kb).then_inc(s_k_out, 1)


def s5_output(nc, S, z):
    with Phase(nc, "y_product", "y_gelu") as ph:
        s_y, s_gelu = ph.sems
        ps = ph.psum("ps_y", [P, 2, GM, NK])
        with nc.Block() as block:

            @block.tensor
            def _(pe):
                for m in range(MT):
                    if m >= 2:
                        pe.wait_ge(s_gelu, m - 1)
                    for gg in range(GM):
                        g = m * GM + gg
                        nc.tensor.matmul(ps[:, m % 2, gg], S.m0[:, g], S.ug[:, g], start=True, stop=False)
                        for r in range(2):
                            last = nc.tensor.matmul(ps[:, m % 2, gg],
                                                    S.qmap[:, r, g, 1:Q + 1].rearrange("p s c -> p (s c)"),
                                                    S.xq[:, r, g], start=False, stop=(r == 1))
                    last.then_inc(s_y, 1)

            @block.scalar
            def _(act):
                for m in range(MT):
                    act.wait_ge(s_y, m + 1)
                    nc.scalar.activation(z[:, m * GM:(m + 1) * GM], ps[:, m % 2],
                                         ACT.Gelu_apprx_tanh).then_inc(s_gelu, 1)


def s5_glu(nc, K, A, l, w_glu):
    with nc.sbuf_tensor("sig", [P, 2, T], F32) as sig:
        def products(i, ps, w):
            for k in range(MT):
                last = nc.tensor.matmul(ps[:, 0], w[:, k], A.up[:, k], start=(k == 0), stop=(k == MT - 1))
            return last

        def gate(act, i, ps):
            return nc.scalar.activation(sig[:, i % 2], ps[:, 0], ACT.Sigmoid, bias=K.vec[:, BGLU + i:BGLU + i + 1])

        def out(dve, i, ps):
            return nc.vector.tensor_tensor(
                A.mixed[:, 4 + i].rearrange("p (k q) -> p q k", q=Q),
                A.up[:, i].rearrange("p (q k) -> p q k", q=Q),
                sig[:, i % 2].rearrange("p (q k) -> p q k", q=Q), ALU.mult)

        linear(nc, "glu", MT, MT, P, lambda i: w_glu[l, i], products, act_step=gate, dve_step=out)


def gqa_rope(nc, K, A, rope_a):
    with Phase(nc, "ropea_load", "ropea_turn", "ropea_out") as ph:
        s_load, s_turn, s_out = ph.sems
        table = ph.sb("rope_a", [P, 2, T])
        t = ph.sb("rope_at", [P, 2, T])
        ps = ph.psum("ps_ra", [P, 3, T])
        with nc.Block() as block:

            @block.sync
            def _(sp):
                sp.dma_start(table[:], rope_a).then_inc(s_load, 16)

            @block.tensor
            def _(pe):
                for i in range(3):
                    nc.tensor.matmul(ps[:, i], K.turn_a[:], A.qka[:, i], start=True, stop=True).then_inc(s_turn, 1)

            @block.vector
            def _(dve):
                v = nc.vector
                dve.wait_ge(s_load, 16)
                for i in range(3):
                    dve.wait_ge(s_turn, i + 1)
                    v.tensor_tensor(t[:, 0], ps[:, i], table[:, 1], ALU.mult)
                    v.tensor_tensor(t[:, 1], A.qka[:, i], table[:, 0], ALU.mult)
                    dve.drain()
                    v.tensor_tensor(A.qka[:, i], t[:, 0], t[:, 1], ALU.add).then_inc(s_out, 1)
                    dve.drain()


def mla_heads(nc, K, A, l, w_qup, w_kvup, rope_b):
    with Phase(nc, "up_load", "up_q", "up_k", "up_v", "up_qout", "up_kout", "up_vout", "up_turn", "up_out") as ph:
        s_load, s_q, s_k, s_v, s_qout, s_kout, s_vout, s_turn, s_out = ph.sems
        wq = ph.sb("w_qup", [P, 2, 4 * MD])
        wkv = ph.sb("w_kvup", [P, 4, 2, HD])
        table = ph.sb("rope_b", [P, 2, T])
        t = ph.sb("rope_bt", [P, 2, T])
        ps_a = ph.psum("ps_up", [P, 2, T])
        ps_v = ph.psum("ps_v", [P, 2, T])
        ps_r = ph.psum("ps_rb", [P, 2, T])
        rot = slice(HD, MD)
        with nc.Block() as block:

            @block.sync
            def _(sp):
                sp.dma_start(wq[:], w_qup[l]).then_inc(s_load, 16)
                sp.dma_start(wkv[:], w_kvup[l]).then_inc(s_load, 16)
                sp.dma_start(table[rot], rope_b).then_inc(s_load, 16)

            @block.tensor
            def _(pe):
                pe.wait_ge(s_load, 48)
                for h in range(4):
                    if h >= 2:
                        pe.wait_ge(s_qout, h - 1)
                    for k in range(2):
                        last = nc.tensor.matmul(ps_a[0:MD, h % 2], wq[:, k, h * MD:(h + 1) * MD], A.ql[:, k],
                                                start=(k == 0), stop=(k == 1))
                    last.then_inc(s_q, 1)
                for h in range(4):
                    pe.wait_ge(s_qout if h < 2 else s_kout, h + 3 if h < 2 else h - 1)
                    nc.tensor.matmul(ps_a[0:HD, h % 2], wkv[:, h, 0], A.kvl[:], start=True,
                                     stop=True).then_inc(s_k, 1)
                for tt in range(TT):
                    last = nc.tensor.matmul(ps_v[:, tt // 2, (tt % 2) * 256:(tt % 2 + 1) * 256],
                                            A.kvl[:, tt * P:(tt + 1) * P], wkv[:, :, 1], start=True, stop=True)
                last.then_inc(s_v, 1)
                for n in range(5):
                    if n >= 2:
                        pe.wait_ge(s_out, n - 1)
                    rhs = A.qb[rot, n] if n < 4 else A.kpe[rot, :]
                    nc.tensor.matmul(ps_r[rot, n % 2], K.turn_b[rot], rhs, start=True, stop=True).then_inc(s_turn, 1)

            @block.scalar
            def _(act):
                for h in range(4):
                    act.wait_ge(s_q, h + 1)
                    nc.scalar.copy(A.qb[0:MD, h], ps_a[0:MD, h % 2]).then_inc(s_qout, 1)
                for h in range(4):
                    act.wait_ge(s_k, h + 1)
                    nc.scalar.copy(A.kb[0:HD, h], ps_a[0:HD, h % 2]).then_inc(s_kout, 1)
                act.wait_ge(s_v, 1)
                nc.scalar.copy(A.vb[:].rearrange("p a b -> p (a b)"),
                               ps_v[:].rearrange("p a b -> p (a b)")).then_inc(s_vout, 1)

            @block.vector
            def _(dve):
                v = nc.vector
                for n in range(5):
                    dve.wait_ge(s_turn, n + 1)
                    x = A.qb[rot, n] if n < 4 else A.kpe[rot, :]
                    v.tensor_tensor(t[rot, 0], ps_r[rot, n % 2], table[rot, 1], ALU.mult)
                    v.tensor_tensor(t[rot, 1], x, table[rot, 0], ALU.mult)
                    dve.drain()
                    if n < 4:
                        v.tensor_tensor(x, t[rot, 0], t[rot, 1], ALU.add).then_inc(s_out, 1)
                        dve.drain()
                    else:
                        for h in range(4):
                            v.tensor_tensor(A.kb[rot, h], t[rot, 0], t[rot, 1], ALU.add)


def attention(nc, K, A):
    heads = []
    for h in range(4):
        g, r = h // 2, h % 2
        lo = g * HD
        heads.append((A.qka[lo:lo + HD, r], A.qka[lo:lo + HD, 2], [A.va[:, kt, lo:lo + HD] for kt in range(TT)],
                      float(HD) ** -0.5))
    for h in range(4):
        heads.append((A.qb[0:MD, h], A.kb[0:MD, h], [A.vb[:, kt, h * HD:(h + 1) * HD] for kt in range(TT)],
                      float(MD) ** -0.5))
    N = len(heads) * TT
    with Phase(nc, "att_score", "att_max", "att_exp", "att_norm", "att_turn", "att_turned", "att_value",
               "att_out") as ph:
        s_score, s_max, s_exp, s_norm, s_turn, s_turned, s_value, s_out = ph.sems
        w = ph.sb("att_w", [P, 2, T])
        wt = ph.sb("att_wt", [P, 2, TT, T])
        st = ph.sb("att_st", [P, 4, N])
        ps_s = ph.psum("ps_as", [P, 3, T])
        ps_t = ph.psum("ps_at", [P, 2, TT, P])
        ps_o = ph.psum("ps_ao", [P, 2, T])
        with nc.Block() as block:

            @block.tensor
            def _(pe):
                def turn(n):
                    pe.wait_ge(s_norm, n + 1)
                    if n >= 2:
                        pe.wait_ge(s_turned, n - 1)
                    for kt in range(TT):
                        last = nc.tensor.transpose(ps_t[:, n % 2, kt], w[:, n % 2, kt * P:(kt + 1) * P], K.ident[:])
                    last.then_inc(s_turn, 1)

                def values(h):
                    lo = (h % 2) * HD
                    pe.wait_ge(s_turned, TT * (h + 1))
                    if h >= 2:
                        pe.wait_ge(s_out, h - 1)
                    for kt in range(TT):
                        last = nc.tensor.matmul(ps_o[lo:lo + HD, h % 2], heads[h][2][kt], wt[:, h % 2, kt],
                                                start=(kt == 0), stop=(kt == TT - 1))
                    last.then_inc(s_value, 1)

                for n in range(N + 2):
                    if n < N:
                        h, qt = divmod(n, TT)
                        if n >= 3:
                            pe.wait_ge(s_exp, n - 2)
                        nc.tensor.matmul(ps_s[:, n % 3], heads[h][0][:, qt * P:(qt + 1) * P], heads[h][1],
                                         start=True, stop=True).then_inc(s_score, 1)
                    if n >= 2:
                        turn(n - 2)
                    if n >= 6 and (n - 6) % TT == 0:
                        values((n - 6) // TT)
                values(len(heads) - 1)

            @block.vector
            def _(dve):
                v = nc.vector
                for n in range(N + 1):
                    if n < N:
                        scale = heads[n // TT][3]
                        dve.wait_ge(s_score, n + 1)
                        v.tensor_reduce(st[:, 0, n:n + 1], ps_s[:, n % 3], AX.X, ALU.max)
                        dve.drain()
                        v.tensor_scalar(st[:, 1, n:n + 1], st[:, 0, n:n + 1], -scale, None,
                                        ALU.mult).then_inc(s_max, 1)
                    if n >= 1:
                        m = n - 1
                        dve.wait_ge(s_exp, n)
                        v.reciprocal(st[:, 3, m:n], st[:, 2, m:n])
                        dve.drain()
                        v.tensor_scalar(w[:, m % 2], w[:, m % 2], st[:, 3, m:n], None, ALU.mult).then_inc(s_norm, 1)

            @block.scalar
            def _(act):
                def turned(n):
                    h, qt = divmod(n, TT)
                    act.wait_ge(s_turn, n + 1)
                    if h >= 2:
                        act.wait_ge(s_value, h - 1)
                    nc.scalar.copy(wt[:, h % 2, :, qt * P:(qt + 1) * P], ps_t[:, n % 2]).then_inc(s_turned, 1)

                def out(h):
                    lo = (h % 2) * HD
                    act.wait_ge(s_value, h + 1)
                    nc.scalar.copy(A.mixed[lo:lo + HD, h // 2], ps_o[lo:lo + HD, h % 2]).then_inc(s_out, 1)

                for n in range(N + 2):
                    if n < N:
                        act.wait_ge(s_max, n + 1)
                        if n >= 2:
                            act.wait_ge(s_turn, n - 1)
                        nc.scalar.activation(w[:, n % 2], ps_s[:, n % 3], ACT.Exp, bias=st[:, 1, n:n + 1],
                                             scale=heads[n // TT][3], accum_out=st[:, 2, n:n + 1]
                                             ).then_inc(s_exp, 1)
                    if n >= 2:
                        turned(n - 2)
                    if n >= 7 and (n - 7) % TT == 0:
                        out((n - 7) // TT)
                for h in range((N + 1 - 7) // TT + 1, len(heads)):
                    out(h)


def mix_out(nc, K, l, w_out):
    def products(i, ps, w):
        for k in range(DT):
            last = split_products(ps[:, 0], tuple(x[:, k] for x in w), (K.xh[:, k], K.xl[:, k]), k == 0,
                                  k == DT - 1)(nc)
        return last

    split_linear(nc, "mixout", DT, DT, lambda i: w_out[l, i], products,
                 dve_step=lambda dve, i, ps: nc.vector.tensor_tensor(K.h[:, i], K.h[:, i], ps[:, 0], ALU.add))


def ple(nc, K, l, p_t, w_ple):
    with Phase(nc, "emb_load", "emb_high") as ph:
        s_load, s_high = ph.sems
        emb_h = ph.sb("emb_h", [P, 2, T], F32R)
        emb_l = ph.sb("emb_l", [P, 2, T], F32R)
        emb = ph.sb("emb", [P, 2, T])
        gate = ph.sb("emb_gate", [P, 2, T])
        t = ph.sb("emb_t", [P, 2, T])
        with nc.Block() as block:

            @block.sync
            def _(sp):
                sp.dma_start(emb[:], p_t[l]).then_inc(s_load, 16)

            @block.scalar
            def _(act):
                act.wait_ge(s_load, 16)
                nc.scalar.copy(emb_h[:], emb[:]).then_inc(s_high, 1)

            @block.vector
            def _(dve):
                dve.wait_ge(s_high, 1)
                nc.vector.tensor_tensor(emb_l[:], emb[:], emb_h[:].bitcast(F32), ALU.subtract)

        def products(i, ps, w):
            for k in range(DT):
                split_products(ps[:, 0], tuple(x[:, k] for x in w), (K.xh[:, k], K.xl[:, k]), k == 0,
                               k == DT - 1)(nc)
            for k in range(2):
                last = split_products(ps[:, 1], tuple(x[:, DT + k] for x in w), (emb_h[:, k], emb_l[:, k]), k == 0,
                                      k == 1)(nc)
            return last

        def out(dve, i, ps):
            nc.vector.tensor_tensor(t[:, i % 2], gate[:, i % 2], ps[:, 1], ALU.mult)
            dve.drain()
            return nc.vector.tensor_tensor(K.h[:, i], K.h[:, i], t[:, i % 2], ALU.add)

        split_linear(nc, "ple", DT, DT + 2, lambda i: w_ple[l, i], products,
               act_step=lambda act, i, ps: nc.scalar.activation(gate[:, i % 2], ps[:, 0], ACT.Sigmoid),
               dve_step=out, banks=2)


def peer(nc, K, l, w_query, sub_keys, down_t, up):
    GB = 2 * BATCH
    STEPS = 4
    TURNS = JB // STEPS
    RAW = 4
    UNIT = 4 * P
    VB = DT // 2
    HU = 12
    down_at, up_at, at = {0: 0}, {}, HEADS * HU
    for q in range(BLOCKS):
        if q + 1 < BLOCKS:
            down_at[q + 1] = at
            at += 2 * JB
        up_at[q] = at
        at += 2 * JB
    names = ([f"raw{r}" for r in range(RAW)]
             + ["sub_keys", "high", "low", "act_high", "act_low", "used", "gelu", "query_out",
                "scores", "scores_out", "ranked", "shifted", "exped", "picked", "pick_turn", "pick_turned", "onehot",
                "gate", "gated", "added"])
    with Phase(nc, *["peer_" + n for n in names]) as ph:
        S = dict(zip(names, ph.sems))
        s_raw = [S[f"raw{r}"] for r in range(RAW)]
        act_w = ph.sb("act_w", [P, JB, T])
        raw = ph.sb("raw", [P, RAW, UNIT])
        high = ph.sb("high", [P, 2, UNIT], F32R)
        low = ph.sb("low", [P, 2, UNIT], F32R)
        act_h = ph.sb("act_h", [P, 2, T], F32R)
        act_l = ph.sb("act_l", [P, 2, T], F32R)
        hot_i = ph.sb("hot_i", [P, 2, BATCH, KEYS], BF16)
        is_j = ph.sb("is_j", [P, 2, BATCH, JB], BF16)
        hot_j = ph.sb("hot_j", [P, 2, 3, BATCH, JB], BF16)
        key_t = ph.sb("key_t", [P, 2, T], BF16)
        gate_t = ph.sb("gate_t", [P, 3, T], BF16)
        ps_v = ph.psum("ps_val", [P, VB, T])
        ps_a = ph.psum("ps_hid", [P, 2, T])
        ps_g = ph.psum("ps_gate", [P, 2, GB, JB])
        other = ph.sb("act_o", [P, JB, T])
        room = [other[:].rearrange("p j t -> p (j t)"), 0]

        def carve(shape, dt=F32):
            n = int(np.prod(shape)) // (2 if dt == BF16 else 1)
            v = room[0][:, room[1]:room[1] + n]
            room[1] += n
            v = v if dt == F32 else v.bitcast(dt)
            names = "abcd"[:len(shape)]
            sizes = {c: s for c, s in zip(names[1:], shape[1:])}
            return v.rearrange(f"p ({' '.join(names)}) -> p {' '.join(names)}", **sizes) if len(shape) > 1 else v

        keys = carve([2, KEYS])
        qh = carve([2, 2, T])
        sc = [carve([TT * 2, KEYS]) for _ in range(2)]
        top = carve([TT * 2, TOPK])
        topi = carve([TT * 2, TOPK], U32)
        cand = carve([TT, TOPK * TOPK])
        best = carve([TT, TOPK])
        besti = carve([TT, TOPK], U32)
        rank = carve([2, TT, TOPK], U32)
        rankb = carve([2, TT, TOPK], BF16)
        keyb = carve([TT * 2, TOPK], BF16)
        eq = carve([TT, TOPK, TOPK], BF16)
        picks = carve([3, TT, P])
        sums = carve([TT, HEADS])
        rest = carve([T])
        assert room[1] <= JB * T
        wbuf = [act_w, other]

        with nc.Block() as block:

            def loop(eng, turns, turn):
                turn(0)
                with eng.Fori(1, turns) as it:
                    turn(it)

            def first(it):
                return isinstance(it, int) and it == 0

            @block.sync
            def _(sp):
                def load(n, pos, src, early=False):
                    if not early:
                        sp.wait_ge(S["low"], n - RAW + 1)
                    sp.dma_start(raw[:, pos], src).then_inc(s_raw[pos], 16)

                def down_unit(q, j, half):
                    return down_t[l, bass.ds(q * JB + j, 1), :, half * 4:half * 4 + 4].rearrange(
                        "o p k i -> p (o k i)")

                def head_turn(it):
                    for g in range(4):
                        load(it * HU + g, g, w_query[l, bass.ds(it, 1), g].rearrange("o p c -> p (o c)"), first(it))
                    for u in range(8):
                        load(it * HU + 4 + u, u % RAW, down_unit(0, it * 4 + u // 2, u % 2))

                def down_turn(q, it):
                    for u in range(2 * STEPS):
                        load(down_at[q] + it * 2 * STEPS + u, u % RAW, down_unit(q, it * STEPS + u // 2, u % 2))

                def up_turn(q, half, it):
                    for u in range(STEPS):
                        load(up_at[q] + half * JB + it * STEPS + u, u,
                             up[l, bass.ds(q * JB + it * STEPS + u, 1), half].rearrange("o p d -> p (o d)"))

                loop(sp, HEADS, head_turn)
                for q in range(BLOCKS):
                    if q + 1 < BLOCKS:
                        loop(sp, TURNS, lambda it: down_turn(q + 1, it))
                    for half in range(2):
                        loop(sp, TURNS, lambda it: up_turn(q, half, it))

            @block.gpsimd
            def _(pool):
                def low_part(n, pos):
                    pool.wait_ge(S["high"], n + 1)
                    nc.gpsimd.tensor_tensor(low[:, pos % 2], raw[:, pos], high[:, pos % 2].bitcast(F32),
                                            ALU.subtract).then_inc(S["low"], 1)

                def head_turn(it):
                    for u in range(HU):
                        low_part(it * HU + u, u % RAW)

                def down_turn(q, it):
                    for u in range(2 * STEPS):
                        low_part(down_at[q] + it * 2 * STEPS + u, u % RAW)

                def up_turn(q, half, it):
                    for u in range(STEPS):
                        n = half * JB + it * STEPS + u
                        low_part(up_at[q] + n, u)
                        pool.wait_ge(S["act_high"], q * 2 * JB + n + 1)
                        w = wbuf[q % 2][:, bass.ds(it * STEPS + u, 1)].rearrange("p o t -> p (o t)")
                        nc.gpsimd.tensor_tensor(act_l[:, u % 2], w, act_h[:, u % 2].bitcast(F32),
                                                ALU.subtract).then_inc(S["act_low"], 1)

                loop(pool, HEADS, head_turn)
                for q in range(BLOCKS):
                    if q + 1 < BLOCKS:
                        loop(pool, TURNS, lambda it: down_turn(q + 1, it))
                    for half in range(2):
                        loop(pool, TURNS, lambda it: up_turn(q, half, it))

            @block.tensor
            def _(pe):
                def unit(n, pos, outs, acts, starts, stops, **kw):
                    pe.wait_ge(S["high"], n + 1)
                    w = [t[:, pos % 2].rearrange("p (c i) -> p c i", c=4) for t in (high, low)]
                    for c in range(4):
                        for part in range(2):
                            nc.tensor.matmul(outs[c], w[0][:, c], acts[c][part], start=starts[c] and part == 0,
                                             stop=False, **kw)
                    pe.wait_ge(S["low"], n + 1)
                    for c in range(4):
                        last = nc.tensor.matmul(outs[c], w[1][:, c], acts[c][0], start=False, stop=stops[c], **kw)
                    last.then_inc(S["used"], 1)

                def x(k):
                    return K.xh[:, k], K.xl[:, k]

                def hidden(q, it, per, u, base):
                    n = it * per + u
                    if not (isinstance(it, int) and q * JB + n < 2):
                        pe.wait_ge(S["gelu"], q * JB + n - 1)
                    for half in range(2):
                        unit(base + 2 * u + half, 2 * u + half, [ps_a[:, u % 2]] * 4, [x(4 * half + c) for c in range(4)],
                             [half == 0 and c == 0 for c in range(4)], [half == 1 and c == 3 for c in range(4)])

                def head(h):
                    if not first(h):
                        pe.wait_ge(S["query_out"], 2 * h)
                    for g in range(4):
                        unit(h * HU + g, g, [ps_v[:, c % 2] for c in range(4)], [x(2 * g + c // 2) for c in range(4)],
                             [g == 0 and c < 2 for c in range(4)], [g == 3 and c >= 2 for c in range(4)])

                def scores(h):
                    pe.wait_ge(S["query_out"], 2 * h + 2)
                    if not first(h):
                        pe.wait_ge(S["scores_out"], h)
                    for tt in range(TT):
                        for c in range(2):
                            lo = (tt % 2) * 256 + c * P
                            last = nc.tensor.matmul(ps_v[:, 2 + tt // 2, lo:lo + P], qh[:, 0, c, tt * P:(tt + 1) * P],
                                                    keys[:, c], start=True, stop=True)
                    last.then_inc(S["scores"], 1)

                def value(q, half, it, u):
                    n = half * JB + it * STEPS + u
                    start = first(it) and u == 0
                    if start and 2 * q + half:
                        pe.wait_ge(S["added"], VB * (2 * q + half))
                    w = [t[:, u % 2] for t in (act_h, act_l)]
                    pe.wait_ge(S["act_low"], q * 2 * JB + n + 1)
                    unit(up_at[q] + n, u, [ps_v[:, c] for c in range(4)], [tuple(w)] * 4, [start] * 4, [False] * 4,
                         skip_group_check=True)

                def gates(q, quad, u):
                    if u % 2 == 0 and not (isinstance(quad, int) and q == 0 and quad == 0):
                        pe.wait_ge(S["gated"], q * (T // GB) + quad * 2 + u // 2 - 1)
                    pe.wait_ge(S["onehot"], q * (T // BATCH) + quad * 4 + u + 1)
                    for i in range(BATCH):
                        for part in range(3):
                            last = nc.tensor.matmul(ps_g[:, u // 2, (u % 2) * BATCH + i], hot_i[:, u % 2, i],
                                                    hot_j[:, u % 2, part, i], start=(part == 0), stop=(part == 2))
                    last.then_inc(S["gate"], 1)

                def head_turn(h):
                    head(h)
                    for u in range(4):
                        hidden(0, h, 4, u, h * HU + 4)
                        if u == 0:
                            scores(h)

                pe.wait_ge(S["sub_keys"], 16)
                loop(pe, HEADS, head_turn)
                pe.wait_ge(S["picked"], 1)
                for n in range(3):
                    for tt in range(TT):
                        last = nc.tensor.transpose(ps_v[:, n, tt * P:(tt + 1) * P], picks[:, n, tt], K.ident[:])
                    last.then_inc(S["pick_turn"], 1)

                def second_block(it):
                    for u in range(STEPS):
                        hidden(1, it, STEPS, u, down_at[1] + it * 2 * STEPS)
                        for s in range(2):
                            gates(0, it * 2 + u // 2, (u % 2) * 2 + s)

                def value_turn(q, half, it):
                    for u in range(STEPS):
                        value(q, half, it, u)
                        if q + 1 < BLOCKS:
                            gates(q + 1, half * TURNS + it, u)

                def hidden_turn(q, it):
                    for u in range(STEPS):
                        hidden(q, it, STEPS, u, down_at[q] + it * 2 * STEPS)

                loop(pe, TURNS, second_block)
                pe.wait_ge(S["pick_turned"], 3)
                for q in range(BLOCKS):
                    for half in range(2):
                        loop(pe, TURNS, lambda it: value_turn(q, half, it))
                    if q + 2 < BLOCKS:
                        loop(pe, TURNS, lambda it: hidden_turn(q + 2, it))

            @block.scalar
            def _(act):
                def gelu(q, it, per, u, done):
                    act.wait_ge(S["used"], done)
                    dst = wbuf[q % 2][:, bass.ds(it * per + u, 1)].rearrange("p o t -> p (o t)")
                    nc.scalar.activation(dst, ps_a[:, u % 2], ACT.Gelu_apprx_tanh).then_inc(S["gelu"], 1)

                def high_part(n, pos, count):
                    act.wait_ge(s_raw[pos], 16 * count)
                    if not (isinstance(n, int) and n < 2):
                        act.wait_ge(S["used"], n - 1)
                    nc.scalar.copy(high[:, pos % 2], raw[:, pos]).then_inc(S["high"], 1)

                def head_turn(h):
                    def high_parts(lo, hi):
                        for u in range(lo, hi):
                            high_part(h * HU + u, u % RAW, h * (HU // RAW) + u // RAW + 1)

                    high_parts(0, 6)
                    for c in range(2):
                        act.wait_ge(S["used"], h * HU + 4)
                        if not first(h):
                            act.wait_ge(S["scores"], h)
                        nc.scalar.copy(qh[:, 0, c], ps_v[:, c]).then_inc(S["query_out"], 1)
                    high_parts(6, 8)
                    gelu(0, h, 4, 0, h * HU + 6)
                    act.wait_ge(S["scores"], h + 1)
                    if not first(h):
                        act.wait_ge(S["ranked"], h)
                    nc.scalar.copy(sc[0].rearrange("p a b -> p (a b)"),
                                   ps_v[:, 2:4].rearrange("p a b -> p (a b)")).then_inc(S["scores_out"], 1)
                    high_parts(8, 10)
                    gelu(0, h, 4, 1, h * HU + 8)
                    high_parts(10, 12)
                    gelu(0, h, 4, 2, h * HU + 10)
                    gelu(0, h, 4, 3, h * HU + 12)

                def block_turn(q, it):
                    for u in range(STEPS):
                        for half in range(2):
                            n = 2 * u + half
                            high_part(down_at[q] + it * 2 * STEPS + n, n % RAW,
                                      down_at[q] // RAW + it * 2 + n // RAW + 1)
                        if u:
                            gelu(q, it, STEPS, u - 1, down_at[q] + it * 2 * STEPS + 2 * u)
                        elif not first(it):
                            gelu(q, it - 1, STEPS, STEPS - 1, down_at[q] + it * 2 * STEPS)

                def block(q):
                    loop(act, TURNS, lambda it: block_turn(q, it))
                    gelu(q, TURNS - 1, STEPS, STEPS - 1, down_at[q] + 2 * JB)

                def value_turn(q, half, it):
                    for u in range(STEPS):
                        n = half * JB + it * STEPS + u
                        high_part(up_at[q] + n, u, (up_at[q] + half * JB) // RAW + it + 1)
                        w = wbuf[q % 2][:, bass.ds(it * STEPS + u, 1)].rearrange("p o t -> p (o t)")
                        nc.scalar.copy(act_h[:, u % 2], w).then_inc(S["act_high"], 1)

                act.dma_start(keys, sub_keys[l]).then_inc(S["sub_keys"], 16)
                loop(act, HEADS, head_turn)
                act.wait_ge(S["shifted"], 1)
                nc.scalar.activation(picks[:, 2], picks[:, 2], ACT.Exp).then_inc(S["exped"], 1)
                for n in range(2):
                    act.wait_ge(S["pick_turn"], n + 1)
                    nc.scalar.copy(key_t[:, n], ps_v[:, n]).then_inc(S["pick_turned"], 1)
                block(1)
                for q in range(BLOCKS):
                    act.wait_ge(S["gated"], (q + 1) * (T // GB))
                    for half in range(2):
                        loop(act, TURNS, lambda it: value_turn(q, half, it))
                    if q + 2 < BLOCKS:
                        block(q + 2)

            @block.vector
            def _(dve):
                v = nc.vector
                NEG = -3.0e38

                def top16(values, out, index, rows):
                    for i in range(rows):
                        v.max(out[:, i, 0:8], values[:, i])
                    dve.drain()
                    for i in range(rows):
                        v.max_index(index[:, i, 0:8], out[:, i, 0:8], values[:, i])
                    for i in range(rows):
                        v.match_replace(values[:, i], out[:, i, 0:8], values[:, i], NEG)
                    dve.drain()
                    for i in range(rows):
                        v.max(out[:, i, 8:16], values[:, i])
                    dve.drain()
                    for i in range(rows):
                        v.max_index(index[:, i, 8:16], out[:, i, 8:16], values[:, i])
                    dve.drain()

                def head(h):
                    cols = bass.ds(h * TOPK, TOPK)
                    dve.wait_ge(S["scores_out"], h + 1)
                    v.tensor_copy(sums[:, 0, 0:1], sc[0][:, 0, 0:1])
                    top16(sc[0], top, topi, TT * 2)
                    v.tensor_copy(keyb, topi)
                    pair = top.rearrange("p (t c) k -> p t c k", c=2)
                    shape = [P, TT, TOPK, TOPK]
                    v.tensor_tensor(cand.rearrange("p t (a b) -> p t a b", b=TOPK),
                                    pair[:, :, 0].unsqueeze(3).broadcast_to(shape),
                                    pair[:, :, 1].unsqueeze(2).broadcast_to(shape), ALU.add)
                    dve.drain()
                    top16(cand, best, besti, TT)
                    v.tensor_scalar(rank[:, 0], besti, 4, None, ALU.logical_shift_right)
                    v.tensor_scalar(rank[:, 1], besti, 15, None, ALU.bitwise_and)
                    v.tensor_tensor(picks[:, 2, :, cols], best,
                                    best[:, :, 0:1].broadcast_to([P, TT, TOPK]), ALU.subtract)
                    dve.drain()
                    v.tensor_copy(rankb, rank)
                    dve.drain()
                    keypair = keyb.rearrange("p (t c) k -> p t c k", c=2)
                    iota16 = K.iotab[:, 0:TOPK].unsqueeze(1).unsqueeze(1).broadcast_to(shape)
                    for c in range(2):
                        v.tensor_tensor(eq, rankb[:, c].unsqueeze(3).broadcast_to(shape), iota16, ALU.is_equal)
                        dve.drain()
                        v.tensor_tensor(eq, eq, keypair[:, :, c].unsqueeze(2).broadcast_to(shape), ALU.mult)
                        dve.drain()
                        last = v.tensor_reduce(picks[:, c, :, cols], eq, AX.X, ALU.add)
                        dve.drain()
                    dve.sem_inc(S["ranked"], 1)

                v.tensor_copy(K.iotab[:], K.iota[:])
                dve.drain()
                loop(dve, HEADS, head)
                dve.drain().then_inc(S["shifted"], 1)
                dve.wait_ge(S["exped"], 1)
                weights = picks[:, 2].rearrange("p t (h k) -> p t h k", k=TOPK)
                v.tensor_reduce(sums, weights, AX.X, ALU.add)
                dve.drain()
                v.reciprocal(sums, sums)
                dve.drain()
                v.tensor_tensor(weights, weights, sums.unsqueeze(3).broadcast_to([P, TT, HEADS, TOPK]),
                                ALU.mult).then_inc(S["picked"], 1)
                dve.wait_ge(S["pick_turn"], 3)
                v.tensor_copy(rest, ps_v[:, 2])
                dve.drain()
                for part in range(3):
                    v.tensor_copy(gate_t[:, part], rest)
                    dve.drain()
                    if part < 2:
                        v.tensor_tensor(rest, rest, gate_t[:, part], ALU.subtract)
                        dve.drain()
                dve.sem_inc(S["pick_turned"], 1)
                dve.wait_ge(S["pick_turned"], 3)

                def gate_quad(q, quad):
                    i_shape, j_shape = [P, BATCH, KEYS], [P, BATCH, JB]
                    for u in range(4):
                        at = bass.ds(quad * 4 * BATCH + u * BATCH, BATCH)
                        if not (isinstance(quad, int) and q == 0 and quad == 0 and u < 2):
                            dve.wait_ge(S["gate"], q * (T // BATCH) + quad * 4 + u - 1)
                        v.tensor_tensor(hot_i[:, u % 2], K.iotab[:].unsqueeze(1).broadcast_to(i_shape),
                                        key_t[:, 0, at].unsqueeze(2).broadcast_to(i_shape), ALU.is_equal)
                        v.tensor_tensor(is_j[:, u % 2], K.iotab[:, q * JB:(q + 1) * JB].unsqueeze(1).broadcast_to(j_shape),
                                        key_t[:, 1, at].unsqueeze(2).broadcast_to(j_shape), ALU.is_equal)
                        dve.drain()
                        v.tensor_tensor(hot_j[:, u % 2], is_j[:, u % 2].unsqueeze(1).broadcast_to([P, 3, BATCH, JB]),
                                        gate_t[:, :, at].unsqueeze(3).broadcast_to([P, 3, BATCH, JB]),
                                        ALU.mult).then_inc(S["onehot"], 1)
                        if u == 0 and not (isinstance(quad, int) and quad == 0):
                            apply(q, quad - 1, 1)
                        if u == 2:
                            apply(q, quad, 0)

                def apply(q, quad, bank):
                    dve.wait_ge(S["gate"], q * (T // BATCH) + quad * 4 + bank * 2 + 2)
                    w = wbuf[q % 2][:, :, bass.ds(quad * 2 * GB + bank * GB, GB)]
                    v.tensor_tensor(w, w, ps_g[:, bank].rearrange("p t j -> p j t"),
                                    ALU.mult).then_inc(S["gated"], 1)

                def gate_quads(q, a, b):
                    if a == 0:
                        dve.wait_ge(S["gelu"], JB * (q + 1))
                        gate_quad(q, 0)
                    with dve.Fori(max(a, 1), b) as quad:
                        gate_quad(q, quad)
                    if b == 2 * TURNS:
                        apply(q, b - 1, 1)

                def add(q, half):
                    dve.wait_ge(S["used"], up_at[q] + (half + 1) * JB)
                    for c in range(VB):
                        n = half * VB + c
                        v.tensor_tensor(K.h[:, n], K.h[:, n], ps_v[:, c], ALU.add).then_inc(S["added"], 1)

                gate_quads(0, 0, 2 * TURNS)
                for q in range(BLOCKS):
                    for half in range(2):
                        if q + 1 < BLOCKS:
                            gate_quads(q + 1, half * TURNS, (half + 1) * TURNS)
                        add(q, half)


class Views:
    pass


def encoder(nc, x_t, const, vec, w_in, rope_a, rope_b, w_qup, w_kvup, s5_lam, s5_bc, s5_d, w_glu, w_out,
            w_query, sub_keys, down_t, up, p_t, w_ple, scratch, out):
    with ExitStack() as ctx:
        def sb(name, shape, dt=F32):
            return ctx.enter_context(nc.sbuf_tensor(name, shape, dt))

        K = Views()
        K.h = sb("h", [P, DT, T])
        K.const = sb("const", [P, 5, P])
        K.ident, K.pairs, K.turn_a, K.iota = (K.const[:, n] for n in range(4))
        K.turn_b = K.const[:, 4, 0:ROPE]
        K.iotab = sb("iotab", [P, P], BF16)
        K.ones = sb("ones", [P, P])
        K.eps = sb("eps", [P, 1])
        K.vec = sb("vec", [P, NVEC])
        constants(nc, K, x_t, const)

        with nc.Fori(0, LAYERS) as l:
            with Phase(nc, "vec_load") as ph:
                s_load, = ph.sems
                with nc.Block() as block:

                    @block.sync
                    def _(sp):
                        sp.dma_start(K.vec[:], vec[l]).then_inc(s_load, 16)
                        sp.wait_ge(s_load, 16)

            def tiles(t, a, b):
                return [t[:, n] for n in range(a, b)]

            def halves(stack, name):
                K.xh, K.xl = (stack.enter_context(nc.sbuf_tensor(f"{name}_{n}", [P, DT, T], F32R)) for n in ("xh", "xl"))
                return [(K.xh[:, n], K.xl[:, n]) for n in range(DT)]

            with ExitStack() as layer:
                def lb(name, shape):
                    return layer.enter_context(nc.sbuf_tensor(name, shape, F32))

                A = Views()
                A.qka = lb("qka", [P, 3, T])
                A.va = lb("va", [P, TT, P])
                A.ql = lb("ql", [P, 2, T])
                A.kvl = lb("kvl", [P, T])
                A.kpe = lb("kpe", [P, T])
                A.up = lb("up_cols", [P, MT, T])
                with ExitStack() as norm:
                    pairs = halves(norm, "in")
                    rmsnorm(nc, K, "mixn", [(tiles(K.h, 0, DT), D, K.ones, MIX, pairs)])
                    in_projection(nc, K, A, l, w_in)
                with ExitStack() as ssm:
                    def mb(name, shape):
                        return ssm.enter_context(nc.sbuf_tensor(name, shape, F32))

                    S = Views()
                    S.ug = mb("ug", [P, G, NK])
                    S.qmap = mb("qmap", [P, 2, G, Q + 2, CH])
                    S.m0 = mb("m0", [P, G, Q * CH])
                    S.xq = mb("s5_xq", [P, 2, G, NK])
                    s5_states(nc, K, A, S, l, s5_lam, s5_bc, s5_d, scratch)
                    z = mb("s5_z", [P, G, NK])
                    s5_output(nc, S, z)
                    regroup(nc, "zout", scratch, A.up, z)
                A.mixed = lb("mixed", [P, DT, T])
                s5_glu(nc, K, A, l, w_glu)
                rmsnorm(nc, K, "latn", [
                    (tiles(A.qka, 0, 1), HD, K.pairs, GQ, tiles(A.qka, 0, 1)),
                    (tiles(A.qka, 1, 2), HD, K.pairs, GQ, tiles(A.qka, 1, 2)),
                    (tiles(A.qka, 2, 3), HD, K.pairs, GK, tiles(A.qka, 2, 3)),
                    (tiles(A.ql, 0, 2), 2 * P, K.ones, MQ, tiles(A.ql, 0, 2)),
                    ([A.kvl[:]], P, K.ones, MKV, [A.kvl[:]])])
                gqa_rope(nc, K, A, rope_a)
                with nc.sbuf_tensor("qb", [P, 4, T], F32) as qb, nc.sbuf_tensor("kb", [P, 4, T], F32) as kb, \
                        nc.sbuf_tensor("vb", [P, TT, 4 * HD], F32) as vb:
                    A.qb, A.kb, A.vb = qb, kb, vb
                    mla_heads(nc, K, A, l, w_qup, w_kvup, rope_b)
                    attention(nc, K, A)
                with ExitStack() as norm:
                    pairs = halves(norm, "mix")
                    rmsnorm(nc, K, "groupn", [(tiles(A.mixed, a, b), (b - a) * P, K.ones, GROUP + a, pairs[a:b])
                                              for a, b in ((0, 2), (2, 4), (4, 8))])
                    mix_out(nc, K, l, w_out)
            with ExitStack() as norm:
                pairs = halves(norm, "ffn")
                rmsnorm(nc, K, "ffnn", [(tiles(K.h, 0, DT), D, K.ones, FFN, pairs)])
                peer(nc, K, l, w_query, sub_keys, down_t, up)
                rmsnorm(nc, K, "plen", [(tiles(K.h, 0, DT), D, K.ones, PLE, pairs)])
                ple(nc, K, l, p_t, w_ple)

        final = sb("final", [P, DT, T])
        rmsnorm(nc, K, "finn", [([K.h[:, n] for n in range(DT)], D, K.ones, FIN, [final[:, n] for n in range(DT)])])
        with Phase(nc, "out_store") as ph:
            s_store, = ph.sems
            with nc.Block() as block:

                @block.sync
                def _(sp):
                    sp.dma_start(out, final[:]).then_inc(s_store, 16)
                    sp.wait_ge(s_store, 16)


def rope_table(n, dim):
    half = dim // 2
    t = np.arange(n)
    freqs = (np.float32(10000.0) ** (-np.arange(0, half, 2, dtype=np.float32) / np.float32(half))).astype(np.float32)
    r, c = (t // 64).astype(np.float32), (t % 64).astype(np.float32)
    ang = np.concatenate([r[:, None] * freqs, c[:, None] * freqs], axis=-1).astype(np.float32)
    return np.cos(ang).T, np.sin(ang).T


def shape_constants():
    const = np.zeros((P, 5, P), np.float32)
    const[:, 0] = np.eye(P)
    const[:, 1] = np.kron(np.eye(2), np.ones((HD, HD)))
    const[:, 3] = np.arange(P)

    def turn(dim):
        m = np.zeros((dim, dim), np.float32)
        h = dim // 2
        m[np.arange(h) + h, np.arange(h)] = -1.0
        m[np.arange(h), np.arange(h) + h] = 1.0
        return m

    const[:, 2] = np.kron(np.eye(2), turn(HD))
    const[HD:MD, 4, 0:ROPE] = turn(ROPE)
    ca, sa = rope_table(T, HD)
    cb, sb = rope_table(T, ROPE)
    rope_a = np.stack([np.tile(ca, (4, 1)), np.tile(sa, (4, 1))], 1).astype(np.float32)
    rope_b = np.stack([np.tile(cb, (2, 1)), np.tile(sb, (2, 1))], 1).astype(np.float32)
    return const, np.ascontiguousarray(rope_a), np.ascontiguousarray(rope_b)


def lay_out(i):
    L = LAYERS
    c = np.ascontiguousarray
    const, rope_a, rope_b = shape_constants()

    def cols(a, n):
        return np.asarray(a).reshape(L, n, P).transpose(0, 2, 1)

    def tiled(a, rows, width=P):
        return a.reshape(L, rows, P, -1, width).transpose(0, 3, 2, 1, 4)

    vec = np.concatenate([
        cols(i["mix_norm"], DT), cols(np.tile(i["gqa_q_norm"], (1, 2)), 1), cols(np.tile(i["gqa_k_norm"], (1, 2)), 1),
        cols(i["mla_q_norm"], 2), cols(i["mla_kv_norm"], 1), cols(i["group_out_norm"], DT), cols(i["ffn_norm"], DT),
        cols(i["ple_norm"], DT), cols(np.tile(i["final_norm"], (L, 1)), DT), cols(i["b_glu"], MT)], axis=2)
    w = i["w_in"]
    qa, ka, va, ql, kvl, kr, u = np.split(w, np.cumsum([256, 128, 128, 256, 128, 32]), axis=2)
    qa = qa.reshape(L, D, 2, 2, HD).transpose(0, 1, 3, 2, 4).reshape(L, D, 256)
    w_in = tiled(np.concatenate([qa, ka, ql, kvl, u, va, kr, kr, kr, kr], axis=2), DT)
    w_qup = i["w_mla_q_up"].reshape(L, 2, P, 4 * MD).transpose(0, 2, 1, 3)
    w_kvup = i["w_mla_kv_up"].reshape(L, P, 4, 2, HD)

    def states(a):
        return a.transpose(0, 1, 3, 2).reshape(L, P, G)

    ldt = np.broadcast_to(i["s5_log_dt"][:, :, :, None], (L, 2, G, ST))
    s5_lam = np.stack([states(i["s5_a_re"]), states(i["s5_a_im"]), states(ldt)], axis=2)
    b = [i[n].transpose(0, 1, 3, 2, 4).reshape(L, P, G, CH) for n in ("s5_b_re", "s5_b_im")]
    cc = [i[n].transpose(0, 1, 4, 2, 3).reshape(L, P, G, CH) for n in ("s5_c_re", "s5_c_im")]
    s5_bc = np.stack(b + cc, axis=2)
    s5_d = i["s5_d"].reshape(L, G, CH).transpose(0, 2, 1)
    w_query = i["w_peer_query"].reshape(L, 4, 2, P, HEADS, 256).transpose(0, 4, 1, 3, 2, 5).reshape(
        L, HEADS, 4, P, 512)
    sub_keys = i["peer_sub_keys"].transpose(0, 3, 1, 2)
    down_t = i["peer_down"].reshape(L, KEYS, KEYS, DT, P).transpose(0, 2, 4, 3, 1)
    up = i["peer_up"].reshape(L, KEYS, KEYS, 2, D // 2).transpose(0, 2, 3, 1, 4)
    w_ple = np.concatenate([tiled(i["w_ple_gate"], DT), tiled(i["w_ple_proj"], 2)], axis=3)
    return [c(a) for a in (
        i["x"][0].reshape(T, DT, P).transpose(2, 1, 0), const, vec, w_in, rope_a, rope_b, w_qup, w_kvup,
        s5_lam, s5_bc, s5_d, tiled(i["w_glu"], MT), tiled(i["w_out"], DT), w_query, sub_keys, down_t, up,
        i["p"][:, 0].reshape(L, T, 2, P).transpose(0, 3, 2, 1), w_ple)]


_NAMES = ["x_t", "const", "vec", "w_in", "rope_a", "rope_b", "w_qup", "w_kvup", "s5_lam", "s5_bc", "s5_d",
          "w_glu", "w_out", "w_query", "sub_keys", "down_t", "up", "p_t", "w_ple"]


def kernel(**inputs):
    import concourse.bacc as _bacc
    from concourse import mybir as _mybir
    from concourse.bass_utils import run_bass_kernel_spmd as _run

    nc = _bacc.Bacc("TRN2", target_bir_lowering=False, num_devices=1, dynamic_dma_scratch_size=1024)
    arrays, args = {}, []
    for name, a in zip(_NAMES, lay_out({k: np.asarray(v) for k, v in inputs.items()})):
        arrays[f"in_{name}"] = a
        args.append(nc.dram_tensor(f"in_{name}", a.shape, _mybir.dt.from_np(a.dtype), kind="ExternalInput").ap())
    scratch = nc.dram_tensor("s5_scratch", (G * CH, Q, NK), F32, kind="Internal").ap()
    out = nc.dram_tensor("out_0_dram", (P, DT, T), F32, kind="ExternalOutput").ap()
    encoder(nc, *args, scratch, out)
    r = _run(nc, [arrays], core_ids=[0])
    got = r.results[0]["out_0_dram"]
    return np.ascontiguousarray(got.transpose(2, 1, 0).reshape(1, T, D))
```

```python
from contextlib import ExitStack

import numpy as np

import concourse.bass as bass
from concourse import mybir

F32 = mybir.dt.float32
F32R = mybir.dt.float32r
BF16 = mybir.dt.bfloat16
U32 = mybir.dt.uint32
ALU = mybir.AluOpType
ACT = mybir.ActivationFunctionType
AX = mybir.AxisListType

P = 128
LAYERS = 2
T = 512
TT = T // P
D = 1024
DT = D // P
EPS = 1e-6
HD = 64
ROPE = 32
MD = HD + ROPE
G, CH, ST = 32, 16, 64
Q = 8
NK = T // Q
MT = G * CH // P
GM = G // MT
SPAN = 8
SPANS = NK // SPAN
KEYS = 128
HEADS, TOPK = 8, 16
BLOCKS = 4
JB = KEYS // BLOCKS
BATCH = 16
KEPT = 3 * P + ROPE

MIX, GQ, GK, MQ, MKV, GROUP, FFN, PLE, FIN, BGLU, NVEC = 0, 8, 9, 10, 12, 13, 21, 29, 37, 45, 49
T_QA, T_KA, T_QL, T_KVL, T_U, T_VA, T_KR = 0, 2, 3, 5, 6, 10, 11
N_IN = 12

MAGIC = 12582912.0
TWO_PI = (6.28125, 0.0019350051879882812, 3.019916050561733e-07)
PI_SAFE = 3.1415925


class Phase:

    def __init__(self, nc, *names):
        self.nc, self.names = nc, names

    def __enter__(self):
        self.stack = ExitStack()
        self.sems = [self.stack.enter_context(self.nc.semaphore(n)) for n in self.names]
        return self

    def sb(self, name, shape, dt=F32):
        return self.stack.enter_context(self.nc.sbuf_tensor(name, shape, dt))

    def psum(self, name, shape):
        return self.stack.enter_context(self.nc.psum_tensor(name, shape, F32))

    def __exit__(self, *exc):
        if exc[0] is None:
            nc = self.nc
            nc.all_engine_barrier()
            for s in self.sems:
                nc.gpsimd.sem_clear(s)
            nc.all_engine_barrier()
        return self.stack.__exit__(*exc)


def split_products(out, weights, acts, first, last, **kw):
    def go(nc):
        nc.tensor.matmul(out, weights[0], acts[0], start=first, stop=False, **kw)
        nc.tensor.matmul(out, weights[0], acts[1], start=False, stop=False, **kw)
        return nc.tensor.matmul(out, weights[1], acts[0], start=False, stop=last, **kw)
    return go


def split_linear(nc, K, name, tiles, k, weight, products, act_step=None, dve_step=None, banks=1, groups=None,
                 prepare=None):
    ring = 3
    early = 2
    extra = prepare.names if prepare else []
    with Phase(nc, *[f"{name}_weight{r}" for r in range(ring)], f"{name}_high", f"{name}_low",
               f"{name}_product", f"{name}_act", f"{name}_dve", *[f"{name}_norm_{n}" for n in Norm.NAMES],
               *extra) as ph:
        s_weight, sems = ph.sems[:ring], ph.sems[ring:]
        s_high, s_low, s_product, s_act, s_dve = sems[:5]
        w = ph.sb(f"{name}_w", [P, ring, k, P])
        high = ph.sb(f"{name}_wh", [P, 2, k, P], F32R)
        low = ph.sb(f"{name}_wl", [P, 2, k, P], F32R)
        ps = ph.psum(f"{name}_ps", [P, 2, banks, T])
        norm = Norm(nc, K, groups, sems[5:5 + len(Norm.NAMES)], *norm_room(ph, name, groups))
        if prepare:
            prepare.sems = sems[5 + len(Norm.NAMES):]
        s_free = s_dve if dve_step else s_act

        def flat(t):
            return t.rearrange("p k c -> p (k c)")

        with nc.Block() as block:

            @block.sync
            def _(sp):
                for i in range(tiles):
                    if i == 1 and prepare:
                        prepare.sync(sp)
                    if i >= ring:
                        sp.wait_ge(s_low, i - ring + 1)
                    sp.dma_start(w[:, i % ring], weight(i)).then_inc(s_weight[i % ring], 16)

            @block.gpsimd
            def _(pool):
                for i in range(tiles):
                    if i == early:
                        norm.gpsimd(pool)
                    pool.wait_ge(s_high, i + 1)
                    nc.gpsimd.tensor_tensor(flat(low[:, i % 2]), flat(w[:, i % ring]),
                                            flat(high[:, i % 2].bitcast(F32)), ALU.subtract).then_inc(s_low, 1)

            @block.tensor
            def _(pe):
                norm.tensor(pe)
                if prepare:
                    prepare.tensor(pe)
                for i in range(tiles):
                    pe.wait_ge(s_low, i + 1)
                    if i >= 2:
                        pe.wait_ge(s_free, i - 1)
                    products(pe, norm, i, ps[:, i % 2], (high[:, i % 2], low[:, i % 2])).then_inc(s_product, 1)

            @block.scalar
            def _(act):
                def high_part(i):
                    act.wait_ge(s_weight[i % ring], 16 * (i // ring + 1))
                    if i >= 2:
                        act.wait_ge(s_product, i - 1)
                    nc.scalar.copy(flat(high[:, i % 2]), flat(w[:, i % ring])).then_inc(s_high, 1)

                norm.squares(act)
                for i in range(early):
                    high_part(i)
                if prepare:
                    prepare.scalar(act)
                norm.scalar(act)
                for i in range(tiles + 1):
                    if early <= i < tiles:
                        high_part(i)
                    if i >= 1 and act_step:
                        act.wait_ge(s_product, i)
                        if dve_step and i >= 3:
                            act.wait_ge(s_dve, i - 2)
                        act_step(act, i - 1, ps[:, (i - 1) % 2]).then_inc(s_act, 1)

            @block.vector
            def _(dve):
                norm.vector(dve)
                if prepare:
                    prepare.vector(dve)
                for i in range(tiles if dve_step else 0):
                    if act_step:
                        dve.wait_ge(s_act, i + 1)
                    else:
                        dve.wait_ge(s_product, i + 1)
                    dve_step(dve, i, ps[:, i % 2]).then_inc(s_dve, 1)


class Norm:
    NAMES = ["square", "sum", "root", "tile", "high", "low_even", "low_odd"]

    def __init__(self, nc, K, groups, sems, sq, root, ps):
        self.nc, self.K, self.groups = nc, K, groups
        self.s_square, self.s_sum, self.s_root, self.s_tile, self.s_high, *self.s_low = sems
        self.sq, self.root, self.ps = sq, root, ps
        self.split = isinstance(groups[0][4][0], tuple)
        self.tiles = [(i, src, gain + j, dst) for i, (srcs, _, _, gain, dsts) in enumerate(groups)
                      for j, (src, dst) in enumerate(zip(srcs, dsts))]

    def squares(self, act):
        for n, (_, src, _, _) in enumerate(self.tiles):
            self.nc.scalar.activation(self.sq[:, n], src, ACT.Square).then_inc(self.s_square, 1)

    def tensor(self, pe):
        n = 0
        for i, (src, _, ones, _, _) in enumerate(self.groups):
            for j in range(len(src)):
                pe.wait_ge(self.s_square, n + 1)
                last = self.nc.tensor.matmul(self.ps[:, i], ones[:], self.sq[:, n], start=(j == 0),
                                             stop=(j == len(src) - 1))
                n += 1
            last.then_inc(self.s_sum, 1)

    def scalar(self, act):
        nc = self.nc
        for i, (_, mean, _, _, _) in enumerate(self.groups):
            act.wait_ge(self.s_sum, i + 1)
            nc.scalar.activation(self.root[:, i], self.ps[:, i], ACT.Sqrt, bias=self.K.eps[:, 0:1],
                                 scale=1.0 / mean).then_inc(self.s_root, 1)
        for n, (_, _, _, dst) in enumerate(self.tiles if self.split else ()):
            act.wait_ge(self.s_tile, n + 1)
            nc.scalar.copy(dst[0], self.sq[:, n]).then_inc(self.s_high, 1)

    def low_part(self, eng, engine, n):
        engine.wait_ge(self.s_high, n + 1)
        dst = self.tiles[n][3]
        eng.tensor_tensor(dst[1], self.sq[:, n], dst[0].bitcast(F32), ALU.subtract).then_inc(self.s_low[n % 2], 1)

    def gpsimd(self, pool):
        for n in range(0, len(self.tiles) if self.split else 0, 2):
            self.low_part(self.nc.gpsimd, pool, n)

    def vector(self, dve):
        v = self.nc.vector
        group = -1
        for n, (i, src, gain, dst) in enumerate(self.tiles):
            if i != group:
                group = i
                dve.wait_ge(self.s_root, i + 1)
                v.reciprocal(self.root[:, i], self.root[:, i])
                dve.drain()
            v.scalar_tensor_tensor(out=self.sq[:, n] if self.split else dst, in0=src,
                                   scalar=self.K.vec[:, gain:gain + 1], in1=self.root[:, i],
                                   op0=ALU.mult, op1=ALU.mult).then_inc(self.s_tile, 1)
        for n in range(1, len(self.tiles) if self.split else 0, 2):
            self.low_part(v, dve, n)

    def ready(self, pe, n):
        pe.wait_ge(self.s_low[n % 2], n // 2 + 1)


def norm_room(ph, name, groups):
    n = sum(len(g[0]) for g in groups)
    return (ph.sb(f"{name}_sq", [P, n, T]), ph.sb(f"{name}_rt", [P, len(groups), T]),
            ph.psum(f"{name}_sum", [P, len(groups), T]))


def rmsnorm(nc, K, name, groups):
    with Phase(nc, *[f"{name}_{n}" for n in Norm.NAMES]) as ph:
        norm = Norm(nc, K, groups, ph.sems, *norm_room(ph, name, groups))
        with nc.Block() as block:

            @block.scalar
            def _(act):
                norm.squares(act)
                norm.scalar(act)

            @block.tensor
            def _(pe):
                norm.tensor(pe)

            @block.vector
            def _(dve):
                norm.vector(dve)


def constants(nc, K, x_t, const):
    with Phase(nc, "start_load", "start_iota", "start_fill") as ph:
        s_load, s_iota, s_fill = ph.sems
        iota = ph.sb("iota", [P, P])
        with nc.Block() as block:

            @block.sync
            def _(sp):
                sp.dma_start(K.h[:], x_t).then_inc(s_load, 16)
                sp.dma_start(K.const[:], const[:, 0:KEPT]).then_inc(s_load, 16)
                sp.dma_start(iota[:], const[:, KEPT:]).then_inc(s_iota, 16)
                sp.wait_ge(s_load, 32)

            @block.vector
            def _(dve):
                dve.wait_ge(s_iota, 16)
                nc.vector.tensor_copy(K.iotab[:], iota[:])

            @block.gpsimd
            def _(pool):
                nc.gpsimd.memset(K.ones[:], 1.0).then_inc(s_fill, 1)
                nc.gpsimd.memset(K.eps[:], EPS).then_inc(s_fill, 1)


def in_projection(nc, K, A, l, w_in, groups):
    def products(pe, norm, i, ps, w):
        for tt in range(TT if i == T_VA else 1):
            for k in range(DT):
                if i == 0:
                    norm.ready(pe, k)
                tile = tuple(x[:, k] for x in w)
                if i != T_VA:
                    last = split_products(ps[:, 0], tile, (K.xh[:, k], K.xl[:, k]), k == 0, k == DT - 1)(nc)
                else:
                    cols = slice(tt * P, (tt + 1) * P)
                    last = split_products(ps[:, 0, cols], (K.xh[:, k, cols], K.xl[:, k, cols]), tile, k == 0,
                                          k == DT - 1)(nc)
        return last

    def out(act, i, ps):
        if T_U <= i < T_VA:
            return nc.scalar.copy(A.up[:, i - T_U].rearrange("p (q k) -> p q k", q=Q),
                                  ps[:, 0].rearrange("p (k q) -> p q k", q=Q))
        if i == T_KR:
            return nc.scalar.copy(A.kpe[HD:MD, :], ps[HD:MD, 0])
        dst = (A.va[:].rearrange("p a b -> p (a b)") if i == T_VA else A.kvl[:] if i == T_KVL
               else A.ql[:, i - T_QL] if i >= T_QL else A.qka[:, i])
        return nc.scalar.copy(dst, ps[:, 0])

    split_linear(nc, K, "inproj", N_IN, DT, lambda i: w_in[l, i], products, act_step=out, groups=groups)


def cmul(eng, out_r, out_i, a, b, tmp_r, tmp_i):
    eng.tensor_tensor(out_r, a[0], b[0], ALU.mult)
    eng.tensor_tensor(tmp_r, a[1], b[1], ALU.mult)
    eng.tensor_tensor(out_i, a[0], b[1], ALU.mult)
    eng.tensor_tensor(tmp_i, a[1], b[0], ALU.mult)
    eng.drain()
    eng.tensor_tensor(out_r, out_r, tmp_r, ALU.subtract)
    return eng.tensor_tensor(out_i, out_i, tmp_i, ALU.add)


def s5_states(nc, K, A, S, l, s5_lam, s5_bc, s5_d, scratch):
    H = ST
    by_chan = scratch.rearrange("(m p) q k -> p m (q k)", p=P)
    by_place = scratch.rearrange("(g c) q k -> q c g k", c=CH)
    with Phase(nc, "s5_stored", "s5_u_loaded", "s5_lam_loaded", "s5_bc_loaded", "s5_d_loaded", "s5_act", "s5_dve",
               "s5_tables", "s5_p1", "s5_turn", "s5_turned", "s5_s", "s5_s_out", "s5_q", "s5_k", "s5_k_out",
               "s5_full", "s5_m0") as ph:
        (s_stored, s_u, s_lam, s_bc, s_d, s_act, s_dve, s_tables, s_p1, s_turn, s_turned, s_s, s_s_out, s_q, s_k,
         s_k_out, s_full, s_m0) = ph.sems
        lam = ph.sb("lam", [P, 3, G])
        t = ph.sb("lam_t", [P, 8, G])
        power = ph.sb("lam_power", [P, 2, Q + 1, G])
        factor = ph.sb("factor", [P, 2, G])
        outpow = ph.sb("outpow", [P, 3, Q + 2, G])
        inpow = ph.sb("inpow", [P, 2, Q, G])
        leap = ph.sb("leap", [P, 2, SPAN + 1, 2, G])
        bc = ph.sb("bc", [P, 4, G, CH])
        dd = ph.sb("dd", [CH, G])
        bbar = ph.sb("bbar", [P, 2, G, CH])
        p1 = ph.sb("p1", [P, 2, GM, Q, CH])
        qtmp = ph.sb("qtmp", [P, GM, Q + 2, CH])
        work = ph.sb("s5_work", [P, 2 * GM * Q * CH])
        full = ph.sb("full", [CH, GM, 2 * Q - 1, CH])
        near = ph.sb("near", [CH, GM, CH])
        diag = ph.sb("diag", [CH, GM, CH])
        s = ph.sb("s5_s", [P, NK, 2, G])
        x = ph.sb("s5_x", [P, NK, 2, G])
        ps_t = ph.psum("ps_t", [P, 2, 4, P])
        ps_k = ph.psum("ps_k", [P, 2, GM, P])
        ps_s = ph.psum("ps_s", [P, 2, GM, NK])
        p1t = A.up[:].rearrange("p m t -> p (m t)").rearrange("p (n s) -> p n s", s=P)
        big = work[:, 0:8 * G].rearrange("p (r n g) -> p r n g", r=2, g=G)
        btmp = work[:, 0:2 * GM * CH].rearrange("p (r g c) -> p r g c", r=2, c=CH)
        ptmp = work[:].rearrange("p (r g q c) -> p r g q c", r=2, g=GM, c=CH)
        scan = work[:].rearrange("p (n b r g) -> p n b r g", n=4, b=SPANS, r=2)
        turns = 2 * GM // 4
        tile_of = [slice(m * GM, (m + 1) * GM) for m in range(MT)]
        with nc.Block() as block:

            @block.sync
            def _(sp):
                sp.dma_start(lam[:], s5_lam[l]).then_inc(s_lam, 16)
                sp.dma_start(by_chan, A.up[:]).then_inc(s_stored, 16)
                sp.dma_start(bc[:], s5_bc[l]).then_inc(s_bc, 16)
                sp.dma_start(dd[:], s5_d[l]).then_inc(s_d, 16)
                sp.wait_ge(s_stored, 16)
                for q in range(Q):
                    sp.dma_start(S.ug[q * CH:(q + 1) * CH], by_place[q]).then_inc(s_u, 16)
                for m in range(MT):
                    sp.wait_ge(s_full, m + 1)
                    for q in range(Q):
                        sp.dma_start(S.m0[q * CH:(q + 1) * CH, tile_of[m], :],
                                     full[:, :, Q - 1 - q:2 * Q - 1 - q].rearrange("c g t d -> c g (t d)")
                                     ).then_inc(s_m0, 16)
                    sp.wait_ge(s_m0, 16 * Q * (m + 1))

            @block.vector
            def _(dve):
                v = nc.vector
                dve.wait_ge(s_act, 1)
                v.tensor_tensor(t[:, 1], lam[:, 0], t[:, 0], ALU.mult).then_inc(s_dve, 1)
                v.tensor_tensor(t[:, 2], lam[:, 1], t[:, 0], ALU.mult)
                dve.drain()
                v.tensor_scalar(t[:, 4], t[:, 2], 1.0 / (2.0 * float(np.pi)), MAGIC, ALU.mult, ALU.add)
                dve.drain()
                v.tensor_scalar(t[:, 4], t[:, 4], MAGIC, None, ALU.subtract)
                dve.drain()
                for part in TWO_PI:
                    v.scalar_tensor_tensor(out=t[:, 2], in0=t[:, 4], scalar=-part, in1=t[:, 2],
                                           op0=ALU.mult, op1=ALU.add)
                    dve.drain()
                v.tensor_scalar(t[:, 4], t[:, 2], PI_SAFE, -PI_SAFE, ALU.min, ALU.max)
                dve.drain()
                v.tensor_scalar(t[:, 5], t[:, 4], -1.0, None, ALU.mult)
                dve.drain()
                v.tensor_tensor(t[:, 5], t[:, 5], t[:, 4], ALU.max)
                dve.drain()
                v.tensor_scalar(t[:, 5], t[:, 5], -1.0, float(np.pi) / 2, ALU.mult, ALU.add).then_inc(s_dve, 1)
                dve.wait_ge(s_act, 4)
                v.memset(power[:, 0, 0], 1.0)
                v.memset(power[:, 1, 0], 0.0)
                v.tensor_tensor(power[:, 0, 1], t[:, 3], t[:, 7], ALU.mult)
                v.tensor_tensor(power[:, 1, 1], t[:, 3], t[:, 6], ALU.mult)
                dve.drain()
                for lo, n in ((1, 1), (2, 2), (4, 4)):
                    a = [power[:, r, 1:1 + n] for r in range(2)]
                    b = [power[:, r, lo:lo + 1].broadcast_to([P, n, G]) for r in range(2)]
                    cmul(v, power[:, 0, lo + 1:lo + 1 + n], power[:, 1, lo + 1:lo + 1 + n], a, b,
                         big[:, 0, 0:n], big[:, 1, 0:n])
                    dve.drain()
                v.tensor_scalar(t[:, 0], power[:, 0, 1], -1.0, None, ALU.add)
                v.tensor_tensor(t[:, 1], lam[:, 0], lam[:, 0], ALU.mult)
                v.tensor_tensor(t[:, 2], lam[:, 1], lam[:, 1], ALU.mult)
                v.tensor_scalar(t[:, 3], lam[:, 1], -1.0, None, ALU.mult)
                dve.drain()
                v.tensor_tensor(t[:, 1], t[:, 1], t[:, 2], ALU.add)
                cmul(v, t[:, 4], t[:, 5], (t[:, 0], power[:, 1, 1]), (lam[:, 0], t[:, 3]), t[:, 6], t[:, 7])
                dve.drain()
                v.reciprocal(t[:, 2], t[:, 1])
                dve.drain()
                v.tensor_tensor(factor[:, 0], t[:, 4], t[:, 2], ALU.mult)
                v.tensor_tensor(factor[:, 1], t[:, 5], t[:, 2], ALU.mult)
                v.memset(outpow[:], 0.0)
                dve.drain()
                for r in range(2):
                    v.tensor_copy(outpow[0:H, r, 0:Q + 1], power[0:H, r])
                    v.tensor_copy(outpow[H:P, r, 1:Q + 2], power[H:P, r, ::-1])
                    v.tensor_copy(inpow[0:H, r], power[0:H, r, 0:Q][:, ::-1])
                    v.tensor_copy(inpow[H:P, r], power[H:P, r, 0:Q])
                dve.drain()
                v.tensor_scalar(outpow[:, 2], outpow[:, 1], -1.0, None, ALU.mult)
                dve.drain().then_inc(s_tables, 1)
                dve.wait_ge(s_bc, 16)
                f = [factor[:, r].unsqueeze(2).broadcast_to([P, G, CH]) for r in range(2)]
                cmul(v, bbar[:, 0], bbar[:, 1], f, (bc[:, 0], bc[:, 1]), p1[:, 0, 0:4].rearrange(
                    "p g q c -> p (g q) c"), p1[:, 1, 0:4].rearrange("p g q c -> p (g q) c"))
                dve.drain()
                shape = [P, GM, Q, CH]
                for m in range(MT):
                    pw = [inpow[:, r, :, tile_of[m]].rearrange("p q g -> p g q").unsqueeze(3).broadcast_to(shape)
                          for r in range(2)]
                    bb = [bbar[:, r, tile_of[m]].unsqueeze(2).broadcast_to(shape) for r in range(2)]
                    if m:
                        dve.wait_ge(s_turn, turns * m)
                    cmul(v, p1[:, 0], p1[:, 1], pw, bb, ptmp[:, 0], ptmp[:, 1]).then_inc(s_p1, 1)
                    dve.drain()
                for r in range(2):
                    v.tensor_copy(leap[:, 0, 1, r], power[:, 0, Q])
                    v.tensor_copy(leap[:, 1, 1, r], power[:, 1, Q])
                    v.memset(leap[:, 0, 0, r], 1.0)
                    v.memset(leap[:, 1, 0, r], 0.0)
                dve.drain()
                for lo, n in ((1, 1), (2, 2), (4, 4)):
                    a = [leap[:, r, 1:1 + n, 0] for r in range(2)]
                    b = [leap[:, r, lo:lo + 1, 0].broadcast_to([P, n, G]) for r in range(2)]
                    cmul(v, leap[:, 0, lo + 1:lo + 1 + n, 0], leap[:, 1, lo + 1:lo + 1 + n, 0], a, b,
                         big[:, 0, 0:n], big[:, 1, 0:n])
                    dve.drain()
                for r in range(2):
                    v.tensor_copy(leap[:, r, 2:, 1], leap[:, r, 2:, 0])
                dve.drain()
                v.tensor_scalar(leap[:, 1, :, 0], leap[:, 1, :, 0], -1.0, None, ALU.mult)
                dve.drain()

                def step(out, state, power_n, add):
                    shape = [P, state.shape[1], 2, G]
                    tmp = scan[:, 0:2, 0:shape[1]]
                    v.tensor_tensor(tmp[:, 0], leap[:, 0, power_n].unsqueeze(1).broadcast_to(shape), state, ALU.mult)
                    v.tensor_tensor(tmp[:, 1], leap[:, 1, power_n].unsqueeze(1).broadcast_to(shape),
                                    state[:, :, ::-1], ALU.mult)
                    dve.drain()
                    v.tensor_tensor(tmp[:, 0], tmp[:, 0], add, ALU.add)
                    dve.drain()
                    v.tensor_tensor(out, tmp[:, 0], tmp[:, 1], ALU.add)
                    dve.drain()

                dve.wait_ge(s_s_out, 4 * MT)
                xs = x[:].rearrange("p (b i) r g -> p b i r g", i=SPAN)
                ss = s[:].rearrange("p (b i) r g -> p b i r g", i=SPAN)
                end, enter = scan[:, 2], scan[:, 3]
                v.memset(xs[:, :, 0], 0.0)
                v.tensor_copy(xs[:, :, 1], ss[:, :, 0])
                v.memset(enter[:, 0:1], 0.0)
                dve.drain()
                for i in range(1, SPAN):
                    step(xs[:, :, i + 1] if i < SPAN - 1 else end, xs[:, :, i], 1, ss[:, :, i])
                v.tensor_copy(enter[:, 1:2], end[:, 0:1])
                dve.drain()
                for b in range(1, SPANS - 1):
                    step(enter[:, b + 1:b + 2], enter[:, b:b + 1], SPAN, end[:, b:b + 1])
                swapped = scan[:, 0]
                v.tensor_copy(swapped, enter[:, :, ::-1])
                dve.drain()
                sf = s[:].rearrange("p k r g -> p k (r g)")
                mf = S.xq[:].rearrange("p r g k -> p (r g k)").rearrange("p (k n) -> p k n", k=NK)
                for out, plane, state in ((sf, 0, enter), (mf, 1, swapped)):
                    v.tensor_tensor(
                        out.rearrange("p (b i) n -> p b i n", i=SPAN),
                        leap[:, plane, 0:SPAN].rearrange("p i r g -> p i (r g)").unsqueeze(1)
                        .broadcast_to([P, SPANS, SPAN, 2 * G]),
                        state.rearrange("p b r g -> p b (r g)").unsqueeze(2)
                        .broadcast_to([P, SPANS, SPAN, 2 * G]), ALU.mult)
                dve.drain()
                v.tensor_tensor(sf, sf, mf, ALU.add)
                dve.drain()
                for lo, order in ((0, 1), (H, -1)):
                    v.tensor_tensor(S.xq[lo:lo + H].rearrange("p r g k -> p k (r g)")[:, ::order],
                                    s[lo:lo + H].rearrange("p k r g -> p k (r g)"),
                                    x[lo:lo + H].rearrange("p k r g -> p k (r g)"), ALU.add)

            @block.gpsimd
            def _(pool):
                g = nc.gpsimd
                pool.wait_ge(s_bc, 16)
                pool.wait_ge(s_tables, 1)
                shape = [P, GM, Q + 2, CH]
                for m in range(MT):
                    c = [bc[:, 2 + r, tile_of[m]].unsqueeze(2).broadcast_to(shape) for r in range(2)]
                    pw = [outpow[:, r, :, tile_of[m]].rearrange("p q g -> p g q").unsqueeze(3).broadcast_to(shape)
                          for r in range(3)]
                    q_re, q_im = (S.qmap[:, r, tile_of[m]] for r in range(2))
                    g.tensor_tensor(q_re, c[0], pw[0], ALU.mult)
                    g.tensor_tensor(qtmp[:], c[1], pw[2], ALU.mult)
                    g.tensor_tensor(q_im, c[0], pw[2], ALU.mult)
                    pool.drain()
                    g.tensor_tensor(q_re, q_re, qtmp[:], ALU.add)
                    pool.drain()
                    g.tensor_tensor(qtmp[:], c[1], pw[0], ALU.mult)
                    pool.drain()
                    g.tensor_tensor(q_im, q_im, qtmp[:], ALU.subtract).then_inc(s_q, 1)
                    pool.drain()
                pool.wait_ge(s_d, 16)
                for m in range(MT):
                    g.tensor_tensor(diag[:], K.ident[0:CH, 0:CH].unsqueeze(1).broadcast_to([CH, GM, CH]),
                                    dd[:, tile_of[m]].unsqueeze(2).broadcast_to([CH, GM, CH]), ALU.mult)
                    pool.wait_ge(s_k_out, 2 * (m + 1))
                    mid = full[:, :, Q - 1]
                    g.tensor_tensor(mid, mid, near[:], ALU.add)
                    pool.drain()
                    g.tensor_tensor(mid, mid, diag[:], ALU.add).then_inc(s_full, 1)
                    pool.drain()

            @block.tensor
            def _(pe):
                for m in range(MT):
                    pe.wait_ge(s_p1, m + 1)
                    for n in range(turns):
                        if m or n >= 2:
                            pe.wait_ge(s_turned, turns * m + n - 1)
                        for u in range(4):
                            r, g = divmod(4 * n + u, GM)
                            last = nc.tensor.transpose(ps_t[:, n % 2, u], p1[:, r, g].rearrange("p q c -> p (q c)"),
                                                       K.ident[:])
                        last.then_inc(s_turn, 1)
                    if m == 0:
                        pe.wait_ge(s_u, 16 * Q)
                    pe.wait_ge(s_turned, turns * (m + 1))
                    if m:
                        pe.wait_ge(s_s_out, 4 * m)
                    for r in range(2):
                        for g in range(GM):
                            last = nc.tensor.matmul(ps_s[:, r, g], p1t[:, r * GM + g], S.ug[:, m * GM + g],
                                                    start=True, stop=True)
                    last.then_inc(s_s, 1)
                for m in range(MT):
                    pe.wait_ge(s_q, m + 1)
                    for back in range(2):
                        if m:
                            pe.wait_ge(s_k_out, 2 * m - 1 + back)
                        lo = back * ST
                        for g in range(GM):
                            for r in range(2):
                                rhs = S.qmap[lo:lo + ST, r, m * GM + g, 2 * back:2 * back + Q]
                                last = nc.tensor.matmul(ps_k[0:CH, back, g], bbar[lo:lo + ST, r, m * GM + g],
                                                        rhs.rearrange("p s c -> p (s c)"),
                                                        start=(r == 0), stop=(r == 1))
                        last.then_inc(s_k, 1)

            @block.scalar
            def _(act):
                act.wait_ge(s_lam, 16)
                nc.scalar.activation(t[:, 0], lam[:, 2], ACT.Exp).then_inc(s_act, 1)
                act.wait_ge(s_dve, 1)
                nc.scalar.activation(t[:, 3], t[:, 1], ACT.Exp).then_inc(s_act, 1)
                act.wait_ge(s_dve, 2)
                nc.scalar.activation(t[:, 6], t[:, 4], ACT.Sin).then_inc(s_act, 1)
                nc.scalar.activation(t[:, 7], t[:, 5], ACT.Sin).then_inc(s_act, 1)
                act.wait_ge(s_stored, 16)
                for m in range(MT):
                    for n in range(turns):
                        act.wait_ge(s_turn, turns * m + n + 1)
                        if m and n == 0:
                            act.wait_ge(s_s, m)
                        nc.scalar.copy(p1t[:, 4 * n:4 * n + 4], ps_t[:, n % 2]).then_inc(s_turned, 1)
                    act.wait_ge(s_s, m + 1)
                    for r in range(2):
                        for lo, order in ((0, 1), (H, -1)):
                            nc.scalar.copy(s[lo:lo + H, :, r, tile_of[m]].rearrange("p k g -> p g k"),
                                           ps_s[lo:lo + H, r][:, :, ::order]).then_inc(s_s_out, 1)
                kf, kb = (ps_k[0:CH, back].rearrange("c g (t d) -> c g t d", d=CH) for back in range(2))
                for m in range(MT):
                    if m:
                        act.wait_ge(s_m0, 16 * Q * m)
                    act.wait_ge(s_k, 2 * m + 1)
                    nc.scalar.copy(near[:], kf[:, :, 0])
                    nc.scalar.copy(full[:, :, Q:2 * Q - 1], kf[:, :, 1:Q]).then_inc(s_k_out, 1)
                    act.wait_ge(s_k, 2 * m + 2)
                    nc.scalar.copy(full[:, :, 0:Q], kb).then_inc(s_k_out, 1)


def s5_output(nc, K, A, S, l, w_glu, scratch):
    by_chan = scratch.rearrange("(m p) q k -> m p (q k)", p=P)
    by_place = scratch.rearrange("(m g c) q k -> m q c g k", g=GM, c=CH)
    with Phase(nc, "y_product", "y_gelu", *[f"y_stored{m}" for m in range(MT)], *[f"y_loaded{m}" for m in range(MT)],
               "glu_weight", "glu_product", "glu_gate", "glu_out") as ph:
        s_y, s_gelu, *s_tiles, s_w, s_glu, s_gate, s_out = ph.sems
        s_stored, s_loaded = s_tiles[:MT], s_tiles[MT:]
        z = ph.sb("s5_z", [P, G, NK])
        w = ph.sb("glu_w", [P, MT, MT, P])
        sig = ph.sb("sig", [P, 2, T])
        ps = ph.psum("ps_y", [P, 2, GM, NK])
        ps_g = ph.psum("ps_glu", [P, 2, T])
        with nc.Block() as block:

            @block.sync
            def _(sp):
                for i in range(MT):
                    sp.dma_start(w[:, i], w_glu[l, i]).then_inc(s_w, 16)
                for m in range(MT):
                    sp.wait_ge(s_gelu, m + 1)
                    for q in range(Q):
                        sp.dma_start(by_place[m, q], z[q * CH:(q + 1) * CH, m * GM:(m + 1) * GM]
                                     ).then_inc(s_stored[m], 16)
                    sp.wait_ge(s_stored[m], 16 * Q)
                    sp.dma_start(A.up[:, m], by_chan[m]).then_inc(s_loaded[m], 16)

            @block.tensor
            def _(pe):
                for m in range(MT):
                    if m >= 2:
                        pe.wait_ge(s_gelu, m - 1)
                    for gg in range(GM):
                        g = m * GM + gg
                        nc.tensor.matmul(ps[:, m % 2, gg], S.m0[:, g], S.ug[:, g], start=True, stop=False)
                        for r in range(2):
                            last = nc.tensor.matmul(ps[:, m % 2, gg],
                                                    S.qmap[:, r, g, 1:Q + 1].rearrange("p s c -> p (s c)"),
                                                    S.xq[:, r, g], start=False, stop=(r == 1))
                    last.then_inc(s_y, 1)
                pe.wait_ge(s_w, 16 * MT)
                for i in range(MT):
                    if i >= 2:
                        pe.wait_ge(s_gate, i - 1)
                    for k in range(MT):
                        if i == 0:
                            pe.wait_ge(s_loaded[k], 16)
                        last = nc.tensor.matmul(ps_g[:, i % 2], w[:, i, k], A.up[:, k], start=(k == 0),
                                                stop=(k == MT - 1))
                    last.then_inc(s_glu, 1)

            @block.scalar
            def _(act):
                for m in range(MT):
                    act.wait_ge(s_y, m + 1)
                    nc.scalar.activation(z[:, m * GM:(m + 1) * GM], ps[:, m % 2],
                                         ACT.Gelu_apprx_tanh).then_inc(s_gelu, 1)
                for i in range(MT):
                    act.wait_ge(s_glu, i + 1)
                    if i >= 2:
                        act.wait_ge(s_out, i - 1)
                    nc.scalar.activation(sig[:, i % 2], ps_g[:, i % 2], ACT.Sigmoid,
                                         bias=K.vec[:, BGLU + i:BGLU + i + 1]).then_inc(s_gate, 1)

            @block.vector
            def _(dve):
                for i in range(MT):
                    dve.wait_ge(s_loaded[i], 16)
                    dve.wait_ge(s_gate, i + 1)
                    nc.vector.tensor_tensor(
                        A.gated[:, i].rearrange("p (k q) -> p q k", q=Q),
                        A.up[:, i].rearrange("p (q k) -> p q k", q=Q),
                        sig[:, i % 2].rearrange("p (q k) -> p q k", q=Q), ALU.mult).then_inc(s_out, 1)


def gqa_rope(nc, K, A, rope_a):
    with Phase(nc, "ropea_load", "ropea_turn", "ropea_out") as ph:
        s_load, s_turn, s_out = ph.sems
        table = ph.sb("rope_a", [P, 2, T])
        t = ph.sb("rope_at", [P, 2, T])
        ps = ph.psum("ps_ra", [P, 3, T])
        with nc.Block() as block:

            @block.sync
            def _(sp):
                sp.dma_start(table[:], rope_a).then_inc(s_load, 16)

            @block.tensor
            def _(pe):
                for i in range(3):
                    nc.tensor.matmul(ps[:, i], K.turn_a[:], A.qka[:, i], start=True, stop=True).then_inc(s_turn, 1)

            @block.vector
            def _(dve):
                v = nc.vector
                dve.wait_ge(s_load, 16)
                for i in range(3):
                    dve.wait_ge(s_turn, i + 1)
                    v.tensor_tensor(t[:, 0], ps[:, i], table[:, 1], ALU.mult)
                    v.tensor_tensor(t[:, 1], A.qka[:, i], table[:, 0], ALU.mult)
                    dve.drain()
                    v.tensor_tensor(A.qka[:, i], t[:, 0], t[:, 1], ALU.add).then_inc(s_out, 1)
                    dve.drain()


def mla_heads(nc, K, A, l, w_qup, w_kvup, rope_b):
    with Phase(nc, "up_load", "up_q", "up_k", "up_v", "up_qout", "up_kout", "up_vout", "up_turn", "up_out") as ph:
        s_load, s_q, s_k, s_v, s_qout, s_kout, s_vout, s_turn, s_out = ph.sems
        wq = ph.sb("w_qup", [P, 2, 4 * MD])
        wkv = ph.sb("w_kvup", [P, 4, 2, HD])
        table = ph.sb("rope_b", [P, 2, T])
        t = ph.sb("rope_bt", [P, 2, T])
        ps_a = ph.psum("ps_up", [P, 2, T])
        ps_v = ph.psum("ps_v", [P, 2, T])
        ps_r = ph.psum("ps_rb", [P, 2, T])
        rot = slice(HD, MD)
        with nc.Block() as block:

            @block.sync
            def _(sp):
                sp.dma_start(wq[:], w_qup[l]).then_inc(s_load, 16)
                sp.dma_start(wkv[:], w_kvup[l]).then_inc(s_load, 16)
                sp.dma_start(table[rot], rope_b).then_inc(s_load, 16)

            @block.tensor
            def _(pe):
                pe.wait_ge(s_load, 48)
                for h in range(4):
                    if h >= 2:
                        pe.wait_ge(s_qout, h - 1)
                    for k in range(2):
                        last = nc.tensor.matmul(ps_a[0:MD, h % 2], wq[:, k, h * MD:(h + 1) * MD], A.ql[:, k],
                                                start=(k == 0), stop=(k == 1))
                    last.then_inc(s_q, 1)
                for h in range(4):
                    pe.wait_ge(s_qout if h < 2 else s_kout, h + 3 if h < 2 else h - 1)
                    nc.tensor.matmul(ps_a[0:HD, h % 2], wkv[:, h, 0], A.kvl[:], start=True,
                                     stop=True).then_inc(s_k, 1)
                for tt in range(TT):
                    last = nc.tensor.matmul(ps_v[:, tt // 2, (tt % 2) * 256:(tt % 2 + 1) * 256],
                                            A.kvl[:, tt * P:(tt + 1) * P], wkv[:, :, 1], start=True, stop=True)
                last.then_inc(s_v, 1)
                for n in range(5):
                    if n >= 2:
                        pe.wait_ge(s_out, n - 1)
                    rhs = A.qb[rot, n] if n < 4 else A.kpe[rot, :]
                    nc.tensor.matmul(ps_r[rot, n % 2], K.turn_b[rot], rhs, start=True, stop=True).then_inc(s_turn, 1)

            @block.scalar
            def _(act):
                for h in range(4):
                    act.wait_ge(s_q, h + 1)
                    nc.scalar.copy(A.qb[0:MD, h], ps_a[0:MD, h % 2]).then_inc(s_qout, 1)
                for h in range(4):
                    act.wait_ge(s_k, h + 1)
                    nc.scalar.copy(A.kb[0:HD, h], ps_a[0:HD, h % 2]).then_inc(s_kout, 1)
                act.wait_ge(s_v, 1)
                nc.scalar.copy(A.vb[:].rearrange("p a b -> p (a b)"),
                               ps_v[:].rearrange("p a b -> p (a b)")).then_inc(s_vout, 1)

            @block.vector
            def _(dve):
                v = nc.vector
                for n in range(5):
                    dve.wait_ge(s_turn, n + 1)
                    x = A.qb[rot, n] if n < 4 else A.kpe[rot, :]
                    v.tensor_tensor(t[rot, 0], ps_r[rot, n % 2], table[rot, 1], ALU.mult)
                    v.tensor_tensor(t[rot, 1], x, table[rot, 0], ALU.mult)
                    dve.drain()
                    if n < 4:
                        v.tensor_tensor(x, t[rot, 0], t[rot, 1], ALU.add).then_inc(s_out, 1)
                        dve.drain()
                    else:
                        for h in range(4):
                            v.tensor_tensor(A.kb[rot, h], t[rot, 0], t[rot, 1], ALU.add)


def attention(nc, K, A):
    heads = []
    for h in range(4):
        g, r = h // 2, h % 2
        lo = g * HD
        heads.append((A.qka[lo:lo + HD, r], A.qka[lo:lo + HD, 2], [A.va[:, kt, lo:lo + HD] for kt in range(TT)],
                      float(HD) ** -0.5))
    for h in range(4):
        heads.append((A.qb[0:MD, h], A.kb[0:MD, h], [A.vb[:, kt, h * HD:(h + 1) * HD] for kt in range(TT)],
                      float(MD) ** -0.5))
    N = len(heads) * TT
    with Phase(nc, "att_score", "att_max", "att_exp", "att_norm", "att_turn", "att_turned", "att_value",
               "att_out") as ph:
        s_score, s_max, s_exp, s_norm, s_turn, s_turned, s_value, s_out = ph.sems
        w = ph.sb("att_w", [P, 2, T])
        wt = ph.sb("att_wt", [P, 2, TT, T])
        st = ph.sb("att_st", [P, 4, N])
        ps_s = ph.psum("ps_as", [P, 3, T])
        ps_t = ph.psum("ps_at", [P, 2, TT, P])
        ps_o = ph.psum("ps_ao", [P, 2, T])
        with nc.Block() as block:

            @block.tensor
            def _(pe):
                def turn(n):
                    pe.wait_ge(s_norm, n + 1)
                    if n >= 2:
                        pe.wait_ge(s_turned, n - 1)
                    for kt in range(TT):
                        last = nc.tensor.transpose(ps_t[:, n % 2, kt], w[:, n % 2, kt * P:(kt + 1) * P], K.ident[:])
                    last.then_inc(s_turn, 1)

                def values(h):
                    lo = (h % 2) * HD
                    pe.wait_ge(s_turned, TT * (h + 1))
                    if h >= 2:
                        pe.wait_ge(s_out, h - 1)
                    for kt in range(TT):
                        last = nc.tensor.matmul(ps_o[lo:lo + HD, h % 2], heads[h][2][kt], wt[:, h % 2, kt],
                                                start=(kt == 0), stop=(kt == TT - 1))
                    last.then_inc(s_value, 1)

                for n in range(N + 2):
                    if n < N:
                        h, qt = divmod(n, TT)
                        if n >= 3:
                            pe.wait_ge(s_exp, n - 2)
                        nc.tensor.matmul(ps_s[:, n % 3], heads[h][0][:, qt * P:(qt + 1) * P], heads[h][1],
                                         start=True, stop=True).then_inc(s_score, 1)
                    if n >= 2:
                        turn(n - 2)
                    if n >= 6 and (n - 6) % TT == 0:
                        values((n - 6) // TT)
                values(len(heads) - 1)

            @block.vector
            def _(dve):
                v = nc.vector
                for n in range(N + 1):
                    if n < N:
                        scale = heads[n // TT][3]
                        dve.wait_ge(s_score, n + 1)
                        v.tensor_reduce(st[:, 0, n:n + 1], ps_s[:, n % 3], AX.X, ALU.max)
                        dve.drain()
                        v.tensor_scalar(st[:, 1, n:n + 1], st[:, 0, n:n + 1], -scale, None,
                                        ALU.mult).then_inc(s_max, 1)
                    if n >= 1:
                        m = n - 1
                        dve.wait_ge(s_exp, n)
                        v.reciprocal(st[:, 3, m:n], st[:, 2, m:n])
                        dve.drain()
                        v.tensor_scalar(w[:, m % 2], w[:, m % 2], st[:, 3, m:n], None, ALU.mult).then_inc(s_norm, 1)

            @block.scalar
            def _(act):
                def turned(n):
                    h, qt = divmod(n, TT)
                    act.wait_ge(s_turn, n + 1)
                    if h >= 2:
                        act.wait_ge(s_value, h - 1)
                    nc.scalar.copy(wt[:, h % 2, :, qt * P:(qt + 1) * P], ps_t[:, n % 2]).then_inc(s_turned, 1)

                def out(h):
                    lo = (h % 2) * HD
                    act.wait_ge(s_value, h + 1)
                    nc.scalar.copy(A.mixed[lo:lo + HD, h // 2], ps_o[lo:lo + HD, h % 2]).then_inc(s_out, 1)

                for n in range(N + 2):
                    if n < N:
                        act.wait_ge(s_max, n + 1)
                        if n >= 2:
                            act.wait_ge(s_turn, n - 1)
                        nc.scalar.activation(w[:, n % 2], ps_s[:, n % 3], ACT.Exp, bias=st[:, 1, n:n + 1],
                                             scale=heads[n // TT][3], accum_out=st[:, 2, n:n + 1]
                                             ).then_inc(s_exp, 1)
                    if n >= 2:
                        turned(n - 2)
                    if n >= 7 and (n - 7) % TT == 0:
                        out((n - 7) // TT)
                for h in range((N + 1 - 7) // TT + 1, len(heads)):
                    out(h)


def mix_out(nc, K, l, w_out, groups):
    def products(pe, norm, i, ps, w):
        for k in range(DT):
            if i == 0:
                norm.ready(pe, k)
            last = split_products(ps[:, 0], tuple(x[:, k] for x in w), (K.xh[:, k], K.xl[:, k]), k == 0,
                                  k == DT - 1)(nc)
        return last

    split_linear(nc, K, "mixout", DT, DT, lambda i: w_out[l, i], products, groups=groups,
                 dve_step=lambda dve, i, ps: nc.vector.tensor_tensor(K.h[:, i], K.h[:, i], ps[:, 0], ALU.add))


class Embeddings:
    names = ["emb_load", "emb_high", "emb_low"]

    def __init__(self, nc, src, emb, high, low):
        self.nc, self.src, self.emb, self.high, self.low = nc, src, emb, high, low

    def sync(self, sp):
        sp.dma_start(self.emb[:], self.src).then_inc(self.sems[0], 16)

    def scalar(self, act):
        act.wait_ge(self.sems[0], 16)
        self.nc.scalar.copy(self.high[:], self.emb[:]).then_inc(self.sems[1], 1)

    def vector(self, dve):
        dve.wait_ge(self.sems[1], 1)
        self.nc.vector.tensor_tensor(self.low[:], self.emb[:], self.high[:].bitcast(F32),
                                     ALU.subtract).then_inc(self.sems[2], 1)

    def tensor(self, pe):
        pe.wait_ge(self.sems[2], 1)


def ple(nc, K, l, p_t, w_ple, groups):
    with ExitStack() as stack:
        def sb(name, dt=F32):
            return stack.enter_context(nc.sbuf_tensor(name, [P, 2, T], dt))

        emb, emb_h, emb_l, gate, t = sb("emb"), sb("emb_h", F32R), sb("emb_l", F32R), sb("emb_gate"), sb("emb_t")

        def products(pe, norm, i, ps, w):
            for k in range(DT):
                if i == 0:
                    norm.ready(pe, k)
                split_products(ps[:, 0], tuple(x[:, k] for x in w), (K.xh[:, k], K.xl[:, k]), k == 0,
                               k == DT - 1)(nc)
            for k in range(2):
                last = split_products(ps[:, 1], tuple(x[:, DT + k] for x in w), (emb_h[:, k], emb_l[:, k]), k == 0,
                                      k == 1)(nc)
            return last

        def out(dve, i, ps):
            nc.vector.tensor_tensor(t[:, i % 2], gate[:, i % 2], ps[:, 1], ALU.mult)
            dve.drain()
            return nc.vector.tensor_tensor(K.h[:, i], K.h[:, i], t[:, i % 2], ALU.add)

        split_linear(nc, K, "ple", DT, DT + 2, lambda i: w_ple[l, i], products,
                     act_step=lambda act, i, ps: nc.scalar.activation(gate[:, i % 2], ps[:, 0], ACT.Sigmoid),
                     dve_step=out, banks=2, groups=groups, prepare=Embeddings(nc, p_t[l], emb, emb_h, emb_l))


def peer(nc, K, l, w_query, sub_keys, down_t, up, groups):
    NB = T // BATCH
    STEPS = 4
    TURNS = JB // STEPS
    RAW = 4
    UNIT = 4 * P
    VB = DT // 2
    EARLY = 2
    HU = 12
    down_at, up_at, at = {0: 0}, {}, HEADS * HU
    for q in range(BLOCKS):
        if q + 1 < BLOCKS:
            down_at[q + 1] = at
            at += 2 * JB
        up_at[q] = at
        at += 2 * JB
    names = ([f"raw{r}" for r in range(RAW)]
             + ["sub_keys", "high", "low", "act_high", "act_low", "used", "gelu", "query_out",
                "scores", "scores_out", "ranked", "shifted", "exped", "picked", "pick_turn", "pick_turned", "onehot",
                "gate", "gated", "added"])
    norm_names = ["norm_" + n for n in Norm.NAMES]
    with Phase(nc, *["peer_" + n for n in names + norm_names]) as ph:
        S = dict(zip(names, ph.sems))
        s_raw = [S[f"raw{r}"] for r in range(RAW)]
        act_w = ph.sb("act_w", [P, JB, T])
        raw = ph.sb("raw", [P, RAW, UNIT])
        high = ph.sb("high", [P, 2, UNIT], F32R)
        low = ph.sb("low", [P, 2, UNIT], F32R)
        act_h = ph.sb("act_h", [P, 2, T], F32R)
        act_l = ph.sb("act_l", [P, 2, T], F32R)
        hot_i = ph.sb("hot_i", [P, 2, BATCH, KEYS], BF16)
        hot_j = ph.sb("hot_j", [P, 2, 3, BATCH, JB], BF16)
        is_j = ph.sb("is_j", [P, BATCH, JB], BF16)
        key_t = ph.sb("key_t", [P, 2, T], BF16)
        gate_t = ph.sb("gate_t", [P, 3, T], BF16)
        ps_v = ph.psum("ps_val", [P, VB, T])
        ps_a = ph.psum("ps_hid", [P, 2, T])
        ps_g = ph.psum("ps_gate", [P, 2, BATCH, JB])
        other = ph.sb("act_o", [P, JB, T])
        room = [other[:].rearrange("p j t -> p (j t)"), 0]

        def carve(shape, dt=F32):
            n = int(np.prod(shape)) // (2 if dt == BF16 else 1)
            v = room[0][:, room[1]:room[1] + n]
            room[1] += n
            v = v if dt == F32 else v.bitcast(dt)
            names = "abcd"[:len(shape)]
            sizes = {c: s for c, s in zip(names[1:], shape[1:])}
            return v.rearrange(f"p ({' '.join(names)}) -> p {' '.join(names)}", **sizes) if len(shape) > 1 else v

        keys = carve([2, KEYS])
        qh = carve([2, 2, T])
        sc = [carve([TT * 2, KEYS]) for _ in range(2)]
        top = carve([TT * 2, TOPK])
        topi = carve([TT * 2, TOPK], U32)
        cand = carve([TT, TOPK * TOPK])
        best = carve([TT, TOPK])
        besti = carve([TT, TOPK], U32)
        rank = carve([2, TT, TOPK], U32)
        rankb = carve([2, TT, TOPK], BF16)
        keyb = carve([TT * 2, TOPK], BF16)
        eq = carve([TT, TOPK, TOPK], BF16)
        picks = carve([3, TT, P])
        sums = carve([TT, HEADS])
        rest = carve([T])
        norm = Norm(nc, K, groups, ph.sems[len(names):], carve([DT, T]), carve([1, T]), ps_g[:, 0:1].rearrange(
            "p o t j -> p o (t j)"))
        assert room[1] <= JB * T
        wbuf = [act_w, other]

        with nc.Block() as block:

            def loop(eng, turns, turn):
                turn(0)
                with eng.Fori(1, turns) as it:
                    turn(it)

            def first(it):
                return isinstance(it, int) and it == 0

            @block.sync
            def _(sp):
                def load(n, pos, src, early=False):
                    if not early:
                        sp.wait_ge(S["low"], n - RAW + 1)
                    sp.dma_start(raw[:, pos], src).then_inc(s_raw[pos], 16)

                def down_unit(q, j, half):
                    return down_t[l, bass.ds(q * JB + j, 1), :, half * 4:half * 4 + 4].rearrange(
                        "o p k i -> p (o k i)")

                def head_turn(it):
                    for g in range(4):
                        load(it * HU + g, g, w_query[l, bass.ds(it, 1), g].rearrange("o p c -> p (o c)"), first(it))
                    for u in range(8):
                        load(it * HU + 4 + u, u % RAW, down_unit(0, it * 4 + u // 2, u % 2))

                def down_turn(q, it):
                    for u in range(2 * STEPS):
                        load(down_at[q] + it * 2 * STEPS + u, u % RAW, down_unit(q, it * STEPS + u // 2, u % 2))

                def up_turn(q, half, it):
                    for u in range(STEPS):
                        load(up_at[q] + half * JB + it * STEPS + u, u,
                             up[l, bass.ds(q * JB + it * STEPS + u, 1), half].rearrange("o p d -> p (o d)"))

                loop(sp, HEADS, head_turn)
                for q in range(BLOCKS):
                    if q + 1 < BLOCKS:
                        loop(sp, TURNS, lambda it: down_turn(q + 1, it))
                    for half in range(2):
                        loop(sp, TURNS, lambda it: up_turn(q, half, it))

            @block.gpsimd
            def _(pool):
                def low_part(n, pos):
                    pool.wait_ge(S["high"], n + 1)
                    nc.gpsimd.tensor_tensor(low[:, pos % 2], raw[:, pos], high[:, pos % 2].bitcast(F32),
                                            ALU.subtract).then_inc(S["low"], 1)

                def head_turn(it):
                    for u in range(EARLY if first(it) else 0, HU):
                        low_part(it * HU + u, u % RAW)

                def down_turn(q, it):
                    for u in range(2 * STEPS):
                        low_part(down_at[q] + it * 2 * STEPS + u, u % RAW)

                def up_turn(q, half, it):
                    for u in range(STEPS):
                        n = half * JB + it * STEPS + u
                        pool.wait_ge(S["act_high"], q * 2 * JB + n + 1)
                        w = wbuf[q % 2][:, bass.ds(it * STEPS + u, 1)].rearrange("p o t -> p (o t)")
                        nc.gpsimd.tensor_tensor(act_l[:, u % 2], w, act_h[:, u % 2].bitcast(F32),
                                                ALU.subtract).then_inc(S["act_low"], 1)
                        low_part(up_at[q] + n, u)

                for u in range(EARLY):
                    low_part(u, u)
                norm.gpsimd(pool)
                loop(pool, HEADS, head_turn)
                for q in range(BLOCKS):
                    if q + 1 < BLOCKS:
                        loop(pool, TURNS, lambda it: down_turn(q + 1, it))
                    for half in range(2):
                        loop(pool, TURNS, lambda it: up_turn(q, half, it))

            @block.tensor
            def _(pe):
                def unit(n, pos, outs, acts, starts, stops):
                    pe.wait_ge(S["high"], n + 1)
                    w = [t[:, pos % 2].rearrange("p (c i) -> p c i", c=4) for t in (high, low)]
                    for c in range(4):
                        for part in range(2):
                            nc.tensor.matmul(outs[c], w[0][:, c], acts[c][part], start=starts[c] and part == 0,
                                             stop=False)
                    pe.wait_ge(S["low"], n + 1)
                    for c in range(4):
                        last = nc.tensor.matmul(outs[c], w[1][:, c], acts[c][0], start=False, stop=stops[c])
                    last.then_inc(S["used"], 1)

                def x(k):
                    return K.xh[:, k], K.xl[:, k]

                def hidden(q, it, per, u, base):
                    n = it * per + u
                    if not (isinstance(it, int) and q * JB + n < 2):
                        pe.wait_ge(S["gelu"], q * JB + n - 1)
                    for half in range(2):
                        unit(base + 2 * u + half, 2 * u + half, [ps_a[:, u % 2]] * 4, [x(4 * half + c) for c in range(4)],
                             [half == 0 and c == 0 for c in range(4)], [half == 1 and c == 3 for c in range(4)])

                def head(h):
                    if not first(h):
                        pe.wait_ge(S["query_out"], 2 * h)
                    for g in range(4):
                        for k in range(2 * g, 2 * g + 2):
                            if first(h):
                                norm.ready(pe, k)
                        unit(h * HU + g, g, [ps_v[:, c % 2] for c in range(4)], [x(2 * g + c // 2) for c in range(4)],
                             [g == 0 and c < 2 for c in range(4)], [g == 3 and c >= 2 for c in range(4)])

                def scores(h):
                    pe.wait_ge(S["query_out"], 2 * h + 2)
                    if not first(h):
                        pe.wait_ge(S["scores_out"], h)
                    for tt in range(TT):
                        for c in range(2):
                            lo = (tt % 2) * 256 + c * P
                            last = nc.tensor.matmul(ps_v[:, 2 + tt // 2, lo:lo + P], qh[:, 0, c, tt * P:(tt + 1) * P],
                                                    keys[:, c], start=True, stop=True)
                    last.then_inc(S["scores"], 1)

                def value(q, half, it, u):
                    n = half * JB + it * STEPS + u
                    start = first(it) and u == 0
                    if start and 2 * q + half:
                        pe.wait_ge(S["added"], VB * (2 * q + half))
                    w = [t[:, u % 2].rearrange("p (c i) -> p c i", c=4) for t in (high, low)]
                    a_high, a_low = act_h[:, u % 2], act_l[:, u % 2]
                    pe.wait_ge(S["high"], up_at[q] + n + 1)
                    for c in range(4):
                        nc.tensor.matmul(ps_v[:, c], w[0][:, c], a_high, start=start, stop=False,
                                         skip_group_check=True)
                    pe.wait_ge(S["act_low"], q * 2 * JB + n + 1)
                    for c in range(4):
                        nc.tensor.matmul(ps_v[:, c], w[0][:, c], a_low, start=False, stop=False,
                                         skip_group_check=True)
                    pe.wait_ge(S["low"], up_at[q] + n + 1)
                    for c in range(4):
                        last = nc.tensor.matmul(ps_v[:, c], w[1][:, c], a_high, start=False, stop=False,
                                                skip_group_check=True)
                    last.then_inc(S["used"], 1)

                def gates(q, pair, u):
                    if not (isinstance(pair, int) and q == 0 and pair == 0):
                        pe.wait_ge(S["gated"], q * NB + pair * 2 + u - 1)
                    pe.wait_ge(S["onehot"], q * NB + pair * 2 + u + 1)
                    for i in range(BATCH):
                        for part in range(3):
                            last = nc.tensor.matmul(ps_g[:, u, i], hot_i[:, u, i], hot_j[:, u, part, i],
                                                    start=(part == 0), stop=(part == 2))
                    last.then_inc(S["gate"], 1)

                def head_turn(h):
                    head(h)
                    for u in range(4):
                        hidden(0, h, 4, u, h * HU + 4)
                        if u == 0:
                            scores(h)

                norm.tensor(pe)
                pe.wait_ge(S["sub_keys"], 16)
                loop(pe, HEADS, head_turn)
                pe.wait_ge(S["picked"], 1)
                for n in range(3):
                    for tt in range(TT):
                        last = nc.tensor.transpose(ps_v[:, n, tt * P:(tt + 1) * P], picks[:, n, tt], K.ident[:])
                    last.then_inc(S["pick_turn"], 1)

                def second_block(it):
                    for u in range(STEPS):
                        hidden(1, it, STEPS, u, down_at[1] + it * 2 * STEPS)
                        gates(0, it * 2 + u // 2, u % 2)

                def value_turn(q, half, it):
                    for u in range(STEPS):
                        value(q, half, it, u)
                        if q + 1 < BLOCKS and u % 2 == 0:
                            gates(q + 1, half * TURNS + it, u // 2)

                def hidden_turn(q, it):
                    for u in range(STEPS):
                        hidden(q, it, STEPS, u, down_at[q] + it * 2 * STEPS)

                loop(pe, TURNS, second_block)
                pe.wait_ge(S["pick_turned"], 3)
                for q in range(BLOCKS):
                    for half in range(2):
                        loop(pe, TURNS, lambda it: value_turn(q, half, it))
                    if q + 2 < BLOCKS:
                        loop(pe, TURNS, lambda it: hidden_turn(q + 2, it))

            @block.scalar
            def _(act):
                def gelu(q, it, per, u, done):
                    act.wait_ge(S["used"], done)
                    dst = wbuf[q % 2][:, bass.ds(it * per + u, 1)].rearrange("p o t -> p (o t)")
                    nc.scalar.activation(dst, ps_a[:, u % 2], ACT.Gelu_apprx_tanh).then_inc(S["gelu"], 1)

                def high_part(n, pos, count):
                    act.wait_ge(s_raw[pos], 16 * count)
                    if not (isinstance(n, int) and n < 2):
                        act.wait_ge(S["used"], n - 1)
                    nc.scalar.copy(high[:, pos % 2], raw[:, pos]).then_inc(S["high"], 1)

                def head_turn(h):
                    def high_parts(lo, hi):
                        for u in range(lo, hi):
                            high_part(h * HU + u, u % RAW, h * (HU // RAW) + u // RAW + 1)

                    high_parts(EARLY if first(h) else 0, 6)
                    for c in range(2):
                        act.wait_ge(S["used"], h * HU + 4)
                        if not first(h):
                            act.wait_ge(S["scores"], h)
                        nc.scalar.copy(qh[:, 0, c], ps_v[:, c]).then_inc(S["query_out"], 1)
                    high_parts(6, 8)
                    gelu(0, h, 4, 0, h * HU + 6)
                    act.wait_ge(S["scores"], h + 1)
                    if not first(h):
                        act.wait_ge(S["ranked"], h)
                    nc.scalar.copy(sc[0].rearrange("p a b -> p (a b)"),
                                   ps_v[:, 2:4].rearrange("p a b -> p (a b)")).then_inc(S["scores_out"], 1)
                    high_parts(8, 10)
                    gelu(0, h, 4, 1, h * HU + 8)
                    high_parts(10, 12)
                    gelu(0, h, 4, 2, h * HU + 10)
                    gelu(0, h, 4, 3, h * HU + 12)

                def block_turn(q, it):
                    for u in range(STEPS):
                        for half in range(2):
                            n = 2 * u + half
                            high_part(down_at[q] + it * 2 * STEPS + n, n % RAW,
                                      down_at[q] // RAW + it * 2 + n // RAW + 1)
                        if u:
                            gelu(q, it, STEPS, u - 1, down_at[q] + it * 2 * STEPS + 2 * u)
                        elif not first(it):
                            gelu(q, it - 1, STEPS, STEPS - 1, down_at[q] + it * 2 * STEPS)

                def block(q):
                    loop(act, TURNS, lambda it: block_turn(q, it))
                    gelu(q, TURNS - 1, STEPS, STEPS - 1, down_at[q] + 2 * JB)

                def value_turn(q, half, it):
                    for u in range(STEPS):
                        n = half * JB + it * STEPS + u
                        w = wbuf[q % 2][:, bass.ds(it * STEPS + u, 1)].rearrange("p o t -> p (o t)")
                        act.wait_ge(S["used"], up_at[q] + n - 1)
                        nc.scalar.copy(act_h[:, u % 2], w).then_inc(S["act_high"], 1)
                        high_part(up_at[q] + n, u, (up_at[q] + half * JB) // RAW + it + 1)

                act.dma_start(keys, sub_keys[l]).then_inc(S["sub_keys"], 16)
                norm.squares(act)
                for u in range(EARLY):
                    high_part(u, u, 1)
                norm.scalar(act)
                loop(act, HEADS, head_turn)
                act.wait_ge(S["shifted"], 1)
                nc.scalar.activation(picks[:, 2], picks[:, 2], ACT.Exp).then_inc(S["exped"], 1)
                for n in range(2):
                    act.wait_ge(S["pick_turn"], n + 1)
                    nc.scalar.copy(key_t[:, n], ps_v[:, n]).then_inc(S["pick_turned"], 1)
                block(1)
                for q in range(BLOCKS):
                    act.wait_ge(S["gated"], (q + 1) * NB)
                    for half in range(2):
                        loop(act, TURNS, lambda it: value_turn(q, half, it))
                    if q + 2 < BLOCKS:
                        block(q + 2)

            @block.vector
            def _(dve):
                v = nc.vector
                NEG = -3.0e38

                def top16(values, out, index, rows):
                    for i in range(rows):
                        v.max(out[:, i, 0:8], values[:, i])
                    dve.drain()
                    for i in range(rows):
                        v.max_index(index[:, i, 0:8], out[:, i, 0:8], values[:, i])
                    for i in range(rows):
                        v.match_replace(values[:, i], out[:, i, 0:8], values[:, i], NEG)
                    dve.drain()
                    for i in range(rows):
                        v.max(out[:, i, 8:16], values[:, i])
                    dve.drain()
                    for i in range(rows):
                        v.max_index(index[:, i, 8:16], out[:, i, 8:16], values[:, i])
                    dve.drain()

                def head(h):
                    cols = bass.ds(h * TOPK, TOPK)
                    dve.wait_ge(S["scores_out"], h + 1)
                    v.tensor_copy(sums[:, 0, 0:1], sc[0][:, 0, 0:1])
                    top16(sc[0], top, topi, TT * 2)
                    v.tensor_copy(keyb, topi)
                    pair = top.rearrange("p (t c) k -> p t c k", c=2)
                    shape = [P, TT, TOPK, TOPK]
                    v.tensor_tensor(cand.rearrange("p t (a b) -> p t a b", b=TOPK),
                                    pair[:, :, 0].unsqueeze(3).broadcast_to(shape),
                                    pair[:, :, 1].unsqueeze(2).broadcast_to(shape), ALU.add)
                    dve.drain()
                    top16(cand, best, besti, TT)
                    v.tensor_scalar(rank[:, 0], besti, 4, None, ALU.logical_shift_right)
                    v.tensor_scalar(rank[:, 1], besti, 15, None, ALU.bitwise_and)
                    v.tensor_tensor(picks[:, 2, :, cols], best,
                                    best[:, :, 0:1].broadcast_to([P, TT, TOPK]), ALU.subtract)
                    dve.drain()
                    v.tensor_copy(rankb, rank)
                    dve.drain()
                    keypair = keyb.rearrange("p (t c) k -> p t c k", c=2)
                    iota16 = K.iotab[:, 0:TOPK].unsqueeze(1).unsqueeze(1).broadcast_to(shape)
                    for c in range(2):
                        v.tensor_tensor(eq, rankb[:, c].unsqueeze(3).broadcast_to(shape), iota16, ALU.is_equal)
                        dve.drain()
                        v.tensor_tensor(eq, eq, keypair[:, :, c].unsqueeze(2).broadcast_to(shape), ALU.mult)
                        dve.drain()
                        last = v.tensor_reduce(picks[:, c, :, cols], eq, AX.X, ALU.add)
                        dve.drain()
                    dve.sem_inc(S["ranked"], 1)

                norm.vector(dve)
                dve.drain()
                loop(dve, HEADS, head)
                dve.drain().then_inc(S["shifted"], 1)
                dve.wait_ge(S["exped"], 1)
                weights = picks[:, 2].rearrange("p t (h k) -> p t h k", k=TOPK)
                v.tensor_reduce(sums, weights, AX.X, ALU.add)
                dve.drain()
                v.reciprocal(sums, sums)
                dve.drain()
                v.tensor_tensor(weights, weights, sums.unsqueeze(3).broadcast_to([P, TT, HEADS, TOPK]),
                                ALU.mult).then_inc(S["picked"], 1)
                dve.wait_ge(S["pick_turn"], 3)
                v.tensor_copy(rest, ps_v[:, 2])
                dve.drain()
                for part in range(3):
                    v.tensor_copy(gate_t[:, part], rest)
                    dve.drain()
                    if part < 2:
                        v.tensor_tensor(rest, rest, gate_t[:, part], ALU.subtract)
                        dve.drain()
                dve.sem_inc(S["pick_turned"], 1)
                dve.wait_ge(S["pick_turned"], 3)

                def gate_pair(q, pair):
                    i_shape, j_shape = [P, BATCH, KEYS], [P, BATCH, JB]
                    for u in range(2):
                        at = bass.ds(pair * 2 * BATCH + u * BATCH, BATCH)
                        start = isinstance(pair, int) and q == 0 and pair == 0
                        if not start:
                            dve.wait_ge(S["gate"], q * NB + pair * 2 + u - 1)
                        v.tensor_tensor(hot_i[:, u], K.iotab[:].unsqueeze(1).broadcast_to(i_shape),
                                        key_t[:, 0, at].unsqueeze(2).broadcast_to(i_shape), ALU.is_equal)
                        if not (start and u == 0):
                            dve.wait_ge(S["onehot"], q * NB + pair * 2 + u)
                        v.tensor_tensor(is_j[:], K.iotab[:, q * JB:(q + 1) * JB].unsqueeze(1).broadcast_to(j_shape),
                                        key_t[:, 1, at].unsqueeze(2).broadcast_to(j_shape), ALU.is_equal)
                        dve.drain()
                        v.tensor_tensor(hot_j[:, u], is_j[:].unsqueeze(1).broadcast_to([P, 3, BATCH, JB]),
                                        gate_t[:, :, at].unsqueeze(3).broadcast_to([P, 3, BATCH, JB]),
                                        ALU.mult).then_inc(S["onehot"], 1)
                        if u == 1:
                            apply(q, pair, 0)
                        elif not (isinstance(pair, int) and pair == 0):
                            apply(q, pair - 1, 1)

                def apply(q, pair, bank):
                    dve.wait_ge(S["gate"], q * NB + pair * 2 + bank + 1)
                    w = wbuf[q % 2][:, :, bass.ds(pair * 2 * BATCH + bank * BATCH, BATCH)]
                    v.tensor_tensor(w, w, ps_g[:, bank].rearrange("p t j -> p j t"),
                                    ALU.mult).then_inc(S["gated"], 1)

                def gate_pairs(q, a, b):
                    if a == 0:
                        dve.wait_ge(S["gelu"], JB * (q + 1))
                        gate_pair(q, 0)
                    with dve.Fori(max(a, 1), b) as pair:
                        gate_pair(q, pair)
                    if b == 2 * TURNS:
                        apply(q, b - 1, 1)

                def add(q, half):
                    dve.wait_ge(S["used"], up_at[q] + (half + 1) * JB)
                    for c in range(VB):
                        n = half * VB + c
                        v.tensor_tensor(K.h[:, n], K.h[:, n], ps_v[:, c], ALU.add).then_inc(S["added"], 1)

                gate_pairs(0, 0, 2 * TURNS)
                for q in range(BLOCKS):
                    for half in range(2):
                        if q + 1 < BLOCKS:
                            gate_pairs(q + 1, half * TURNS, (half + 1) * TURNS)
                        add(q, half)


class Views:
    pass


def encoder(nc, x_t, const, vec, w_in, rope_a, rope_b, w_qup, w_kvup, s5_lam, s5_bc, s5_d, w_glu, w_out,
            w_query, sub_keys, down_t, up, p_t, w_ple, scratch, out):
    with ExitStack() as ctx:
        def sb(name, shape, dt=F32):
            return ctx.enter_context(nc.sbuf_tensor(name, shape, dt))

        K = Views()
        K.h = sb("h", [P, DT, T])
        K.const = sb("const", [P, KEPT])
        K.ident, K.pairs, K.turn_a = (K.const[:, n * P:(n + 1) * P] for n in range(3))
        K.turn_b = K.const[:, 3 * P:KEPT]
        K.iotab = sb("iotab", [P, P], BF16)
        K.ones = sb("ones", [P, P])
        K.eps = sb("eps", [P, 1])
        K.vec = sb("vec", [P, NVEC])
        constants(nc, K, x_t, const)

        with nc.Fori(0, LAYERS) as l:
            with Phase(nc, "vec_load") as ph:
                s_load, = ph.sems
                with nc.Block() as block:

                    @block.sync
                    def _(sp):
                        sp.dma_start(K.vec[:], vec[l]).then_inc(s_load, 16)
                        sp.wait_ge(s_load, 16)

            def tiles(t, a, b):
                return [t[:, n] for n in range(a, b)]

            def halves(stack, name):
                K.xh, K.xl = (stack.enter_context(nc.sbuf_tensor(f"{name}_{n}", [P, DT, T], F32R)) for n in ("xh", "xl"))
                return [(K.xh[:, n], K.xl[:, n]) for n in range(DT)]

            with ExitStack() as layer:
                def lb(name, shape):
                    return layer.enter_context(nc.sbuf_tensor(name, shape, F32))

                A = Views()
                A.qka = lb("qka", [P, 3, T])
                A.va = lb("va", [P, TT, P])
                A.ql = lb("ql", [P, 2, T])
                A.kvl = lb("kvl", [P, T])
                A.kpe = lb("kpe", [P, T])
                A.up = lb("up_cols", [P, MT, T])
                A.gated = lb("gated", [P, MT, T])
                with ExitStack() as norm:
                    pairs = halves(norm, "in")
                    in_projection(nc, K, A, l, w_in, [(tiles(K.h, 0, DT), D, K.ones, MIX, pairs)])
                with ExitStack() as ssm:
                    def mb(name, shape):
                        return ssm.enter_context(nc.sbuf_tensor(name, shape, F32))

                    S = Views()
                    S.ug = mb("ug", [P, G, NK])
                    S.qmap = mb("qmap", [P, 2, G, Q + 2, CH])
                    S.m0 = mb("m0", [P, G, Q * CH])
                    S.xq = mb("s5_xq", [P, 2, G, NK])
                    s5_states(nc, K, A, S, l, s5_lam, s5_bc, s5_d, scratch)
                    s5_output(nc, K, A, S, l, w_glu, scratch)
                A.mixed = lb("mixed", [P, DT - MT, T])
                rmsnorm(nc, K, "latn", [
                    (tiles(A.qka, 0, 1), HD, K.pairs, GQ, tiles(A.qka, 0, 1)),
                    (tiles(A.qka, 1, 2), HD, K.pairs, GQ, tiles(A.qka, 1, 2)),
                    (tiles(A.qka, 2, 3), HD, K.pairs, GK, tiles(A.qka, 2, 3)),
                    (tiles(A.ql, 0, 2), 2 * P, K.ones, MQ, tiles(A.ql, 0, 2)),
                    ([A.kvl[:]], P, K.ones, MKV, [A.kvl[:]])])
                gqa_rope(nc, K, A, rope_a)
                with nc.sbuf_tensor("qb", [P, 4, T], F32) as qb, nc.sbuf_tensor("kb", [P, 4, T], F32) as kb, \
                        nc.sbuf_tensor("vb", [P, TT, 4 * HD], F32) as vb:
                    A.qb, A.kb, A.vb = qb, kb, vb
                    mla_heads(nc, K, A, l, w_qup, w_kvup, rope_b)
                    attention(nc, K, A)
                with ExitStack() as norm:
                    pairs = halves(norm, "mix")
                    mix_out(nc, K, l, w_out, [
                        (tiles(A.mixed, 0, 2), 2 * P, K.ones, GROUP, pairs[0:2]),
                        (tiles(A.mixed, 2, 4), 2 * P, K.ones, GROUP + 2, pairs[2:4]),
                        (tiles(A.gated, 0, MT), MT * P, K.ones, GROUP + 4, pairs[4:8])])
            with ExitStack() as norm:
                pairs = halves(norm, "ffn")
                peer(nc, K, l, w_query, sub_keys, down_t, up, [(tiles(K.h, 0, DT), D, K.ones, FFN, pairs)])
                ple(nc, K, l, p_t, w_ple, [(tiles(K.h, 0, DT), D, K.ones, PLE, pairs)])

        final = sb("final", [P, DT, T])
        rmsnorm(nc, K, "finn", [([K.h[:, n] for n in range(DT)], D, K.ones, FIN, [final[:, n] for n in range(DT)])])
        with Phase(nc, "out_store") as ph:
            s_store, = ph.sems
            with nc.Block() as block:

                @block.sync
                def _(sp):
                    sp.dma_start(out, final[:]).then_inc(s_store, 16)
                    sp.wait_ge(s_store, 16)


def rope_table(n, dim):
    half = dim // 2
    t = np.arange(n)
    freqs = (np.float32(10000.0) ** (-np.arange(0, half, 2, dtype=np.float32) / np.float32(half))).astype(np.float32)
    r, c = (t // 64).astype(np.float32), (t % 64).astype(np.float32)
    ang = np.concatenate([r[:, None] * freqs, c[:, None] * freqs], axis=-1).astype(np.float32)
    return np.cos(ang).T, np.sin(ang).T


def shape_constants():
    const = np.zeros((P, KEPT + P), np.float32)
    const[:, 0:P] = np.eye(P)
    const[:, P:2 * P] = np.kron(np.eye(2), np.ones((HD, HD)))
    const[:, KEPT:] = np.arange(P)

    def turn(dim):
        m = np.zeros((dim, dim), np.float32)
        h = dim // 2
        m[np.arange(h) + h, np.arange(h)] = -1.0
        m[np.arange(h), np.arange(h) + h] = 1.0
        return m

    const[:, 2 * P:3 * P] = np.kron(np.eye(2), turn(HD))
    const[HD:MD, 3 * P:KEPT] = turn(ROPE)
    ca, sa = rope_table(T, HD)
    cb, sb = rope_table(T, ROPE)
    rope_a = np.stack([np.tile(ca, (4, 1)), np.tile(sa, (4, 1))], 1).astype(np.float32)
    rope_b = np.stack([np.tile(cb, (2, 1)), np.tile(sb, (2, 1))], 1).astype(np.float32)
    return const, np.ascontiguousarray(rope_a), np.ascontiguousarray(rope_b)


def lay_out(i):
    L = LAYERS
    c = np.ascontiguousarray
    const, rope_a, rope_b = shape_constants()

    def cols(a, n):
        return np.asarray(a).reshape(L, n, P).transpose(0, 2, 1)

    def tiled(a, rows, width=P):
        return a.reshape(L, rows, P, -1, width).transpose(0, 3, 2, 1, 4)

    vec = np.concatenate([
        cols(i["mix_norm"], DT), cols(np.tile(i["gqa_q_norm"], (1, 2)), 1), cols(np.tile(i["gqa_k_norm"], (1, 2)), 1),
        cols(i["mla_q_norm"], 2), cols(i["mla_kv_norm"], 1), cols(i["group_out_norm"], DT), cols(i["ffn_norm"], DT),
        cols(i["ple_norm"], DT), cols(np.tile(i["final_norm"], (L, 1)), DT), cols(i["b_glu"], MT)], axis=2)
    w = i["w_in"]
    qa, ka, va, ql, kvl, kr, u = np.split(w, np.cumsum([256, 128, 128, 256, 128, 32]), axis=2)
    qa = qa.reshape(L, D, 2, 2, HD).transpose(0, 1, 3, 2, 4).reshape(L, D, 256)
    w_in = tiled(np.concatenate([qa, ka, ql, kvl, u, va, kr, kr, kr, kr], axis=2), DT)
    w_qup = i["w_mla_q_up"].reshape(L, 2, P, 4 * MD).transpose(0, 2, 1, 3)
    w_kvup = i["w_mla_kv_up"].reshape(L, P, 4, 2, HD)

    def states(a):
        return a.transpose(0, 1, 3, 2).reshape(L, P, G)

    ldt = np.broadcast_to(i["s5_log_dt"][:, :, :, None], (L, 2, G, ST))
    s5_lam = np.stack([states(i["s5_a_re"]), states(i["s5_a_im"]), states(ldt)], axis=2)
    b = [i[n].transpose(0, 1, 3, 2, 4).reshape(L, P, G, CH) for n in ("s5_b_re", "s5_b_im")]
    cc = [i[n].transpose(0, 1, 4, 2, 3).reshape(L, P, G, CH) for n in ("s5_c_re", "s5_c_im")]
    s5_bc = np.stack(b + cc, axis=2)
    s5_d = i["s5_d"].reshape(L, G, CH).transpose(0, 2, 1)
    w_query = i["w_peer_query"].reshape(L, 4, 2, P, HEADS, 256).transpose(0, 4, 1, 3, 2, 5).reshape(
        L, HEADS, 4, P, 512)
    sub_keys = i["peer_sub_keys"].transpose(0, 3, 1, 2)
    down_t = i["peer_down"].reshape(L, KEYS, KEYS, DT, P).transpose(0, 2, 4, 3, 1)
    up = i["peer_up"].reshape(L, KEYS, KEYS, 2, D // 2).transpose(0, 2, 3, 1, 4)
    w_ple = np.concatenate([tiled(i["w_ple_gate"], DT), tiled(i["w_ple_proj"], 2)], axis=3)
    return [c(a) for a in (
        i["x"][0].reshape(T, DT, P).transpose(2, 1, 0), const, vec, w_in, rope_a, rope_b, w_qup, w_kvup,
        s5_lam, s5_bc, s5_d, tiled(i["w_glu"], MT), tiled(i["w_out"], DT), w_query, sub_keys, down_t, up,
        i["p"][:, 0].reshape(L, T, 2, P).transpose(0, 3, 2, 1), w_ple)]


_NAMES = ["x_t", "const", "vec", "w_in", "rope_a", "rope_b", "w_qup", "w_kvup", "s5_lam", "s5_bc", "s5_d",
          "w_glu", "w_out", "w_query", "sub_keys", "down_t", "up", "p_t", "w_ple"]


def kernel(**inputs):
    import concourse.bacc as _bacc
    from concourse import mybir as _mybir
    from concourse.bass_utils import run_bass_kernel_spmd as _run

    nc = _bacc.Bacc("TRN2", target_bir_lowering=False, num_devices=1, dynamic_dma_scratch_size=1024)
    arrays, args = {}, []
    for name, a in zip(_NAMES, lay_out({k: np.asarray(v) for k, v in inputs.items()})):
        arrays[f"in_{name}"] = a
        args.append(nc.dram_tensor(f"in_{name}", a.shape, _mybir.dt.from_np(a.dtype), kind="ExternalInput").ap())
    scratch = nc.dram_tensor("s5_scratch", (G * CH, Q, NK), F32, kind="Internal").ap()
    out = nc.dram_tensor("out_0_dram", (P, DT, T), F32, kind="ExternalOutput").ap()
    encoder(nc, *args, scratch, out)
    r = _run(nc, [arrays], core_ids=[0])
    got = r.results[0]["out_0_dram"]
    return np.ascontiguousarray(got.transpose(2, 1, 0).reshape(1, T, D))
```
